# Optimizing a Trainium2 kernel written in Bass

```python
import math
import jax, jax.numpy as jnp
from jax import lax
import numpy as np
import jax
import jax.numpy as jnp

D_MODEL = 1024
BATCH = 1
SEQ = 256
DEPTH = 1

HEAD_DIM = 64
QBLOCK = 128
EPS = 1e-5
SWA_HEADS = 8
SWA_KV_HEADS = 2
SWA_WINDOW = 128
DIFF_HEADS = 4
NSA_HEADS = 8
NSA_KV_HEADS = 2
CMP_BLOCK = 32
CMP_STRIDE = 16
CMP_HIDDEN = 256
SEL_BLOCK = 64
SEL_TOPN = 16
SEL_QCHUNK = 32
NSA_WINDOW = 512
BRANCH_WIDTH = 512
N_BRANCHES = 3
N_EXPERTS = 32
TOP_K = 4
D_EXPERT = D_MODEL
SWIGLU_LIMIT = 7.0
SWIGLU_ALPHA = 1.702
MOE_BLOCK = 128
A_Q = SWA_HEADS * HEAD_DIM
A_KV = SWA_KV_HEADS * HEAD_DIM
B_QK = DIFF_HEADS * 2 * HEAD_DIM
B_V = DIFF_HEADS * 2 * HEAD_DIM
C_Q = NSA_HEADS * HEAD_DIM
C_KV = NSA_KV_HEADS * HEAD_DIM
NSA_GATES = NSA_HEADS * 3
MERGE_GATES = N_BRANCHES * D_MODEL
IN_SPLITS = (A_Q, A_KV, A_KV, B_QK, B_QK, B_V, C_Q, C_KV, C_KV, C_KV, C_KV, C_KV, C_KV, NSA_GATES, MERGE_GATES)
IN_WIDTH = sum(IN_SPLITS)


def rms_norm(x, g):
    xf = x.astype(jnp.float32)
    y = xf * lax.rsqrt(jnp.mean(xf * xf, axis=-1, keepdims=True) + EPS)
    return (y * g.astype(jnp.float32)).astype(x.dtype)

def alibi_slopes(n):
    return 2.0 ** (-8.0 * jnp.arange(1, n + 1, dtype=jnp.float32) / n)

def banded_attention(q, k, v, window, slopes, sinks=None):
    B, S, Hkv, G, d = q.shape
    nb = S // QBLOCK
    n_prev = -(-(window - 1) // QBLOCK)
    ctx = (n_prev + 1) * QBLOCK
    pad = ((0, 0), (n_prev * QBLOCK, 0), (0, 0), (0, 0))
    kp = jnp.pad(k, pad)
    vp = jnp.pad(v, pad)
    qb = q.reshape(B, nb, QBLOCK, Hkv, G, d).swapaxes(0, 1)
    scale = d ** -0.5

    def block(args):
        qi, i = args
        start = i * QBLOCK
        kc = lax.dynamic_slice_in_dim(kp, start, ctx, axis=1)
        vc = lax.dynamic_slice_in_dim(vp, start, ctx, axis=1)
        s = jnp.einsum('bqhgd,bkhd->bhgqk', qi, kc).astype(jnp.float32) * scale
        t = start + jnp.arange(QBLOCK)
        pos = start - n_prev * QBLOCK + jnp.arange(ctx)
        dist = t[:, None] - pos[None, :]
        valid = (dist >= 0) & (dist < window) & (pos[None, :] >= 0)
        s = s - slopes[:, :, None, None] * dist.astype(jnp.float32)
        s = jnp.where(valid, s, -jnp.inf)
        if sinks is None:
            p = jax.nn.softmax(s, axis=-1)
        else:
            lse = jnp.logaddexp(jax.nn.logsumexp(s, axis=-1, keepdims=True), sinks[:, :, None, None])
            p = jnp.exp(s - lse)
        return jnp.einsum('bhgqk,bkhd->bqhgd', p.astype(vc.dtype), vc)

    o = lax.map(block, (qb, jnp.arange(nb)))
    return o.swapaxes(0, 1).reshape(B, S, Hkv, G, d)

def diff_attention(q, k, v, lam_params, subln_g, slopes, lam_init):
    B, S, H, _, d = q.shape
    nb = S // QBLOCK
    lp = lam_params.astype(jnp.float32)
    lam = jnp.exp(jnp.sum(lp[0] * lp[1])) - jnp.exp(jnp.sum(lp[2] * lp[3])) + lam_init
    qb = q.reshape(B, nb, QBLOCK, H, 2, d).swapaxes(0, 1)
    kpos = jnp.arange(S)
    scale = d ** -0.5

    def block(args):
        qi, i = args
        s = jnp.einsum('bqhcd,bkhcd->bhcqk', qi, k).astype(jnp.float32) * scale
        t = i * QBLOCK + jnp.arange(QBLOCK)
        dist = t[:, None] - kpos[None, :]
        s = s - slopes[:, None, None, None] * dist.astype(jnp.float32)
        s = jnp.where(dist >= 0, s, -jnp.inf)
        p = jax.nn.softmax(s, axis=-1)
        w = p[:, :, 0] - lam * p[:, :, 1]
        return jnp.einsum('bhqk,bkhe->bqhe', w.astype(v.dtype), v)

    o = lax.map(block, (qb, jnp.arange(nb)))
    o = o.swapaxes(0, 1).reshape(B, S, H, 2 * d)
    return rms_norm(o, subln_g) * (1.0 - lam_init)

def compress_blocks(x, pos, w1, b1, w2, b2):
    B, S, Hkv, d = x.shape
    nc = (S - CMP_BLOCK) // CMP_STRIDE + 1
    idx = jnp.arange(nc)[:, None] * CMP_STRIDE + jnp.arange(CMP_BLOCK)[None, :]
    blk = x[:, idx] + pos[:, None, :]
    blk = blk.transpose(0, 1, 3, 2, 4).reshape(B, nc, Hkv, CMP_BLOCK * d)
    hid = jax.nn.gelu(blk @ w1 + b1)
    return hid @ w2 + b2

def nsa_attention(q, k_cmp, v_cmp, k_slc, v_slc, k_win, v_win, gates, cmp_pos, cmp_w1, cmp_b1, cmp_w2, cmp_b2, slopes):
    B, S, Hkv, G, d = q.shape
    scale = d ** -0.5
    t = jnp.arange(S)
    kc = compress_blocks(k_cmp, cmp_pos[0], cmp_w1[0], cmp_b1[0], cmp_w2[0], cmp_b2[0])
    vc = compress_blocks(v_cmp, cmp_pos[1], cmp_w1[1], cmp_b1[1], cmp_w2[1], cmp_b2[1])
    nc = kc.shape[1]
    cstart = jnp.arange(nc) * CMP_STRIDE
    cvalid = (cstart[None, :] + CMP_BLOCK - 1) <= t[:, None]
    s = jnp.einsum('bqhgd,bchd->bhgqc', q, kc).astype(jnp.float32) * scale
    p_cmp = jax.nn.softmax(jnp.where(cvalid, s, -1e30), axis=-1) * cvalid
    o_cmp = jnp.einsum('bhgqc,bchd->bqhgd', p_cmp.astype(vc.dtype), vc)
    nsb = S // SEL_BLOCK
    sstart = jnp.arange(nsb) * SEL_BLOCK
    overlap = jnp.clip(jnp.minimum(cstart[:, None] + CMP_BLOCK, sstart[None, :] + SEL_BLOCK)
                       - jnp.maximum(cstart[:, None], sstart[None, :]), 0).astype(jnp.float32) / CMP_BLOCK
    imp = jnp.einsum('bhgqc,cn->bhqn', p_cmp, overlap)
    cur = t // SEL_BLOCK
    blk = jnp.arange(nsb)
    causal_blk = blk[None, :] <= cur[:, None]
    forced = (blk[None, :] == 0) | (blk[None, :] == cur[:, None]) | (blk[None, :] == cur[:, None] - 1)
    score = jnp.where(forced, jnp.inf, jnp.where(causal_blk, imp, -jnp.inf))
    n_sel = min(SEL_TOPN, nsb)
    top_s, top_i = lax.top_k(score, n_sel)
    sel_ok = top_s > -jnp.inf
    kb = k_slc.reshape(B, nsb, SEL_BLOCK, Hkv, d).transpose(0, 3, 1, 2, 4)
    vb = v_slc.reshape(B, nsb, SEL_BLOCK, Hkv, d).transpose(0, 3, 1, 2, 4)
    nq = S // SEL_QCHUNK
    qch = q.reshape(B, nq, SEL_QCHUNK, Hkv, G, d).swapaxes(0, 1)
    ich = top_i.reshape(B, Hkv, nq, SEL_QCHUNK, n_sel).transpose(2, 0, 1, 3, 4)
    och = sel_ok.reshape(B, Hkv, nq, SEL_QCHUNK, n_sel).transpose(2, 0, 1, 3, 4)
    bidx = jnp.arange(B)[:, None, None, None]
    hidx = jnp.arange(Hkv)[None, :, None, None]

    def chunk(args):
        qi, ii, oki, cidx = args
        kg = kb[bidx, hidx, ii]
        vg = vb[bidx, hidx, ii]
        sc = jnp.einsum('bqhgd,bhqnld->bhgqnl', qi, kg).astype(jnp.float32) * scale
        tq = cidx * SEL_QCHUNK + jnp.arange(SEL_QCHUNK)
        kpos = ii[..., None] * SEL_BLOCK + jnp.arange(SEL_BLOCK)
        dist = tq[None, None, :, None, None] - kpos
        ok = (dist >= 0) & oki[..., None]
        sc = sc - slopes[None, :, :, None, None, None] * dist[:, :, None].astype(jnp.float32)
        sc = jnp.where(ok[:, :, None], sc, -jnp.inf)
        shp = sc.shape
        pr = jax.nn.softmax(sc.reshape(shp[:4] + (shp[4] * shp[5],)), axis=-1).reshape(shp)
        return jnp.einsum('bhgqnl,bhqnld->bqhgd', pr.astype(vg.dtype), vg)

    o_slc = lax.map(chunk, (qch, ich, och, jnp.arange(nq)))
    o_slc = o_slc.swapaxes(0, 1).reshape(B, S, Hkv, G, d)
    o_win = banded_attention(q, k_win, v_win, NSA_WINDOW, slopes)
    g = jax.nn.sigmoid(gates)
    return g[..., 0:1] * o_cmp + g[..., 1:2] * o_slc + g[..., 2:3] * o_win

def hybrid_mixer(h, w_in, b_in, sinks, diff_lambda, diff_subln_g, cmp_pos, cmp_w1, cmp_b1, cmp_w2, cmp_b2, w_branch, w_out, lam_init):
    B, S, _ = h.shape
    z = h @ w_in + b_in
    offs = np.cumsum(IN_SPLITS)[:-1].tolist()
    (qa, ka, va, qb, kb, vb, qc, kcm, vcm, ksl, vsl, kwn, vwn, g_nsa, g_merge) = jnp.split(z, offs, axis=-1)
    ga = SWA_HEADS // SWA_KV_HEADS
    o_a = banded_attention(qa.reshape(B, S, SWA_KV_HEADS, ga, HEAD_DIM),
                           ka.reshape(B, S, SWA_KV_HEADS, HEAD_DIM), va.reshape(B, S, SWA_KV_HEADS, HEAD_DIM),
                           SWA_WINDOW, alibi_slopes(SWA_HEADS).reshape(SWA_KV_HEADS, ga),
                           sinks.astype(jnp.float32).reshape(SWA_KV_HEADS, ga)).reshape(B, S, BRANCH_WIDTH)
    o_b = diff_attention(qb.reshape(B, S, DIFF_HEADS, 2, HEAD_DIM), kb.reshape(B, S, DIFF_HEADS, 2, HEAD_DIM),
                         vb.reshape(B, S, DIFF_HEADS, 2 * HEAD_DIM), diff_lambda, diff_subln_g,
                         alibi_slopes(DIFF_HEADS), lam_init).reshape(B, S, BRANCH_WIDTH)
    gc = NSA_HEADS // NSA_KV_HEADS
    kv = lambda a: a.reshape(B, S, NSA_KV_HEADS, HEAD_DIM)
    o_c = nsa_attention(qc.reshape(B, S, NSA_KV_HEADS, gc, HEAD_DIM), kv(kcm), kv(vcm), kv(ksl), kv(vsl), kv(kwn), kv(vwn),
                        g_nsa.reshape(B, S, NSA_KV_HEADS, gc, 3), cmp_pos, cmp_w1, cmp_b1, cmp_w2, cmp_b2,
                        alibi_slopes(NSA_HEADS).reshape(NSA_KV_HEADS, gc)).reshape(B, S, BRANCH_WIDTH)
    gm = jax.nn.sigmoid(g_merge.reshape(B, S, N_BRANCHES, D_MODEL))
    merged = gm[:, :, 0] * (o_a @ w_branch[0]) + gm[:, :, 1] * (o_b @ w_branch[1]) + gm[:, :, 2] * (o_c @ w_branch[2])
    return merged @ w_out

def moe_ffn(h, router_w, router_b, w1, b1, w2, b2):
    B, S, D = h.shape
    N = B * S
    xt = h.reshape(N, D)
    logits = (xt @ router_w + router_b).astype(jnp.float32)
    top_v, top_e = lax.top_k(logits, TOP_K)
    gate = jax.nn.softmax(top_v, axis=-1)
    A = N * TOP_K
    e_flat = top_e.reshape(A)
    order = jnp.argsort(e_flat)
    e_sorted = e_flat[order]
    tok_sorted = order // TOP_K
    g_sorted = gate.reshape(A)[order]
    counts = jnp.bincount(e_flat, length=N_EXPERTS)
    group_start = jnp.cumsum(counts) - counts
    padded = (counts + MOE_BLOCK - 1) // MOE_BLOCK * MOE_BLOCK
    pad_end = jnp.cumsum(padded)
    pad_start = pad_end - padded
    dest = pad_start[e_sorted] + (jnp.arange(A) - group_start[e_sorted])
    n_blocks = -(-A // MOE_BLOCK) + N_EXPERTS
    P = n_blocks * MOE_BLOCK
    row_tok = jnp.zeros((P,), jnp.int32).at[dest].set(tok_sorted.astype(jnp.int32))
    row_w = jnp.zeros((P,), jnp.float32).at[dest].set(g_sorted)
    block_expert = jnp.clip(jnp.searchsorted(pad_end, jnp.arange(n_blocks) * MOE_BLOCK, side='right'), 0, N_EXPERTS - 1)

    def expert_block(args):
        rows, e = args
        xb = xt[rows]
        hb = xb @ w1[e] + b1[e]
        g, u = hb[:, :D_EXPERT], hb[:, D_EXPERT:]
        g = jnp.minimum(g, SWIGLU_LIMIT)
        u = jnp.clip(u, -SWIGLU_LIMIT, SWIGLU_LIMIT)
        glu = g * jax.nn.sigmoid(g * SWIGLU_ALPHA)
        return ((u + 1.0) * glu) @ w2[e] + b2[e]

    y = lax.map(expert_block, (row_tok.reshape(n_blocks, MOE_BLOCK), block_expert)).reshape(P, D)
    out = jnp.zeros((N, D), y.dtype).at[row_tok].add(y * row_w[:, None].astype(y.dtype))
    return out.reshape(B, S, D)

def first_inputs(seed: int = 0) -> dict:
    key = jax.random.key(seed)
    ks = jax.random.split(key, 32)
    L, D, E, F = DEPTH, D_MODEL, N_EXPERTS, D_EXPERT
    nrm = lambda k, shape, s: jax.random.normal(k, shape, jnp.float32) * s
    return {
        'x': nrm(ks[0], (BATCH, SEQ, D), 1.0),
        'c': nrm(ks[1], (BATCH, D), 1.0),
        'mod_w': nrm(ks[2], (L, D, 6 * D), 0.5 * D ** -0.5),
        'mod_b': nrm(ks[3], (L, 6 * D), 0.02),
        'norm1_g': 1.0 + nrm(ks[4], (L, D), 0.1),
        'norm2_g': 1.0 + nrm(ks[5], (L, D), 0.1),
        'w_in': nrm(ks[6], (L, D, IN_WIDTH), D ** -0.5),
        'b_in': nrm(ks[7], (L, IN_WIDTH), 0.02),
        'sinks': nrm(ks[8], (L, SWA_HEADS), 0.5),
        'diff_lambda': nrm(ks[9], (L, 4, HEAD_DIM), 0.1),
        'diff_subln_g': 1.0 + nrm(ks[10], (L, 2 * HEAD_DIM), 0.1),
        'cmp_pos': nrm(ks[11], (L, 2, CMP_BLOCK, HEAD_DIM), 0.1),
        'cmp_w1': nrm(ks[12], (L, 2, CMP_BLOCK * HEAD_DIM, CMP_HIDDEN), (CMP_BLOCK * HEAD_DIM) ** -0.5),
        'cmp_b1': nrm(ks[13], (L, 2, CMP_HIDDEN), 0.02),
        'cmp_w2': nrm(ks[14], (L, 2, CMP_HIDDEN, HEAD_DIM), CMP_HIDDEN ** -0.5),
        'cmp_b2': nrm(ks[15], (L, 2, HEAD_DIM), 0.02),
        'w_branch': nrm(ks[16], (L, N_BRANCHES, BRANCH_WIDTH, D), BRANCH_WIDTH ** -0.5),
        'w_out': nrm(ks[17], (L, D, D), D ** -0.5),
        'router_w': nrm(ks[18], (L, D, E), D ** -0.5),
        'router_b': nrm(ks[19], (L, E), 0.01),
        'exp_w1': nrm(ks[20], (L, E, D, 2 * F), D ** -0.5),
        'exp_b1': nrm(ks[21], (L, E, 2 * F), 0.02),
        'exp_w2': nrm(ks[22], (L, E, F, D), F ** -0.5),
        'exp_b2': nrm(ks[23], (L, E, D), 0.02),
        'final_g': 1.0 + nrm(ks[24], (D,), 0.1),
    }

def first_block(x, c, mod_w, mod_b, norm1_g, norm2_g, w_in, b_in, sinks, diff_lambda, diff_subln_g, cmp_pos, cmp_w1, cmp_b1, cmp_w2, cmp_b2, w_branch, w_out, router_w, router_b, exp_w1, exp_b1, exp_w2, exp_b2, final_g):
    cs = jax.nn.silu(c)
    for l in range(DEPTH):
        mod = cs @ mod_w[l] + mod_b[l]
        sh1, sc1, g1, sh2, sc2, g2 = [m[:, None, :] for m in jnp.split(mod, 6, axis=-1)]
        lam_init = 0.8 - 0.6 * math.exp(-0.3 * l)
        h = rms_norm(x, norm1_g[l]) * (1.0 + sc1) + sh1
        x = x + g1 * hybrid_mixer(h, w_in[l], b_in[l], sinks[l], diff_lambda[l], diff_subln_g[l], cmp_pos[l], cmp_w1[l],
                                  cmp_b1[l], cmp_w2[l], cmp_b2[l], w_branch[l], w_out[l], lam_init)
        h = rms_norm(x, norm2_g[l]) * (1.0 + sc2) + sh2
        x = x + g2 * moe_ffn(h, router_w[l], router_b[l], exp_w1[l], exp_b1[l], exp_w2[l], exp_b2[l])
    return rms_norm(x, final_g)


DEPTH_2 = 2

GRID_W = 64
CTX_LEN = 256
N_MOD = 9
D_FF = 2816
NA_HEADS = 8
NA_HEAD_DIM = 64
NA_WIDTH = NA_HEADS * NA_HEAD_DIM
NA_KH = 8
NA_KW = 16
POOL_WINDOWS = (2, 4, 8, 16)
POOL_GROUPS = len(POOL_WINDOWS)
POOL_WIDTH = D_MODEL - NA_WIDTH
POOL_GROUP_DIM = POOL_WIDTH // POOL_GROUPS
EVEN_IN_WIDTH = 3 * NA_WIDTH + POOL_WIDTH
EVEN_MIX_WIDTH = NA_WIDTH + POOL_WIDTH
CONV_WIDTH = D_MODEL
CONV_K = 3
N_EVEN = (DEPTH_2 + 1) // 2
N_ODD = DEPTH_2 // 2
RMS_EPS = 1e-6
NEG_INF = -1e30


def rms_norm_2(x, g):
    x32 = x.astype(jnp.float32)
    y = x32 * lax.rsqrt(jnp.mean(x32 * x32, axis=-1, keepdims=True) + RMS_EPS)
    return (y * g.astype(jnp.float32)).astype(x.dtype)

def modulate(h, shift, scale):
    return h * (1 + scale) + shift

def adaln(cond, w, b):
    m = jax.nn.silu(cond) @ w + b
    return m.reshape(m.shape[:-1] + (N_MOD, D_MODEL))

def swiglu(h, w13, w2):
    a, b = jnp.split(h @ w13, 2, axis=-1)
    return (jax.nn.silu(a) * b) @ w2

def ffn_sublayer(h, m, g, w13, w2, base):
    hn = modulate(rms_norm_2(h, g), m[:, :, base], m[:, :, base + 1])
    return h + 0.5 * m[:, :, base + 2] * swiglu(hn, w13, w2)

def split_heads(t):
    return t.reshape(t.shape[:2] + (NA_HEADS, NA_HEAD_DIM))

def neighbourhood_attention(q, k, v, k_ctx, v_ctx, rpb):
    B, L, H, dh = q.shape
    R = L // GRID_W
    kh = min(NA_KH, R)
    kw = NA_KW
    scale = dh ** -0.5
    qg = q.reshape(B, R, GRID_W, H, dh)
    kg = k.reshape(B, R, GRID_W, H, dh)
    vg = v.reshape(B, R, GRID_W, H, dh)
    r = jnp.arange(R)
    row_start = jnp.clip(r - kh // 2, 0, R - kh)
    ridx = row_start[:, None] + jnp.arange(kh)[None, :]
    k_blk = kg[:, ridx]
    v_blk = vg[:, ridx]
    col = jnp.arange(GRID_W)
    col_start = jnp.clip(col - kw // 2, 0, GRID_W - kw)
    col_ok = (col[None, :] >= col_start[:, None]) & (col[None, :] < col_start[:, None] + kw)
    ri = ridx - r[:, None] + (NA_KH - 1)
    ci = jnp.clip(col[None, :] - col[:, None] + (NA_KW - 1), 0, 2 * NA_KW - 2)
    bias = rpb[:, ri[:, None, :, None], ci[None, :, None, :]].astype(jnp.float32)
    s_win = jnp.einsum('brqhd,brkwhd->bhrqkw', qg, k_blk).astype(jnp.float32) * scale + bias
    s_win = jnp.where(col_ok[:, None, :], s_win, NEG_INF)
    n_win = kh * GRID_W
    s_win = s_win.reshape(B, H, R, GRID_W, n_win)
    s_ctx = jnp.einsum('brqhd,bchd->bhrqc', qg, k_ctx).astype(jnp.float32) * scale
    p = jax.nn.softmax(jnp.concatenate([s_win, s_ctx], axis=-1), axis=-1).astype(v.dtype)
    p_win = p[..., :n_win].reshape(B, H, R, GRID_W, kh, GRID_W)
    o = (jnp.einsum('bhrqkw,brkwhd->brqhd', p_win, v_blk)
         + jnp.einsum('bhrqc,bchd->brqhd', p[..., n_win:], v_ctx))
    return o.reshape(B, L, H * dh)

def context_attention(q, k, v):
    B, C, H, dh = q.shape
    s = jnp.einsum('bqhd,bkhd->bhqk', q, k).astype(jnp.float32) * dh ** -0.5
    p = jax.nn.softmax(s, axis=-1).astype(v.dtype)
    return jnp.einsum('bhqk,bkhd->bqhd', p, v).reshape(B, C, H * dh)

def multiscale_pool(u, pool_w, pool_scale):
    B, L, _ = u.shape
    t = jnp.arange(L)
    ug = u.reshape(B, L, POOL_GROUPS, POOL_GROUP_DIM)
    outs = []
    for g, w in enumerate(POOL_WINDOWS):
        xg = ug[:, :, g].astype(jnp.float32)
        cs = jnp.pad(jnp.cumsum(xg, axis=1), ((0, 0), (1, 0), (0, 0)))
        lo = jnp.clip(t - w // 2, 0, L)
        hi = jnp.clip(t - w // 2 + w, 0, L)
        cnt = (hi - lo).astype(jnp.float32)[None, :, None]
        mean = (jnp.take(cs, hi, axis=1) - jnp.take(cs, lo, axis=1)) / cnt
        outs.append((mean - xg).astype(u.dtype) @ pool_w[g])
    return jnp.concatenate(outs, axis=-1) * pool_scale

def even_mixer(hl, hc, w_in, w_out, rpb, pool_w, pool_scale, ctx_out):
    q, k, v, u = jnp.split(hl @ w_in, [NA_WIDTH, 2 * NA_WIDTH, 3 * NA_WIDTH], axis=-1)
    k_c, v_c = jnp.split(hc @ w_in[:, NA_WIDTH:3 * NA_WIDTH], 2, axis=-1)
    k_c, v_c = split_heads(k_c), split_heads(v_c)
    att = neighbourhood_attention(split_heads(q), split_heads(k), split_heads(v), k_c, v_c, rpb)
    pool = multiscale_pool(u, pool_w, pool_scale)
    y_lat = jnp.concatenate([att, pool], axis=-1) @ w_out
    y_ctx = None
    if ctx_out:
        q_c = split_heads(hc @ w_in[:, :NA_WIDTH])
        u_c = hc @ w_in[:, 3 * NA_WIDTH:]
        att_c = context_attention(q_c, k_c, v_c)
        pool_c = multiscale_pool(u_c, pool_w, pool_scale)
        y_ctx = jnp.concatenate([att_c, pool_c], axis=-1) @ w_out
    return y_lat, y_ctx

def short_conv_mixer(h, w_in, conv_w, w_out):
    bg, cg, xin = jnp.split(h @ w_in, 3, axis=-1)
    z = cg * xin
    L = h.shape[1]
    zp = jnp.pad(z, ((0, 0), (1, 1), (0, 0)))
    y = zp[:, 0:L] * conv_w[0] + zp[:, 1:L + 1] * conv_w[1] + zp[:, 2:L + 2] * conv_w[2]
    return (bg * y) @ w_out

def second_inputs(seed: int = 0) -> dict:
    key = jax.random.key(seed)
    ks = jax.random.split(key, 18)
    D = D_MODEL

    def nrm(k, shape, s):
        return jax.random.normal(k, shape, jnp.float32) * s

    return {
        "x": nrm(ks[0], (BATCH, SEQ, D), 1.0),
        "c": nrm(ks[1], (BATCH, D), 1.0),
        "ctx": nrm(ks[2], (BATCH, CTX_LEN, D), 1.0),
        "c_ctx": nrm(ks[3], (D,), 1.0),
        "mod_w": nrm(ks[4], (DEPTH_2, D, N_MOD * D), 0.5 * D ** -0.5),
        "mod_b": nrm(ks[5], (DEPTH_2, N_MOD * D), 0.01),
        "norm_g": 1.0 + nrm(ks[6], (DEPTH_2, 3, D), 0.02),
        "ffn_w13": nrm(ks[7], (DEPTH_2, 2, D, 2 * D_FF), D ** -0.5),
        "ffn_w2": nrm(ks[8], (DEPTH_2, 2, D_FF, D), D_FF ** -0.5),
        "even_w_in": nrm(ks[9], (N_EVEN, D, EVEN_IN_WIDTH), D ** -0.5),
        "even_w_out": nrm(ks[10], (N_EVEN, EVEN_MIX_WIDTH, D), EVEN_MIX_WIDTH ** -0.5),
        "na_rpb": nrm(ks[11], (N_EVEN, NA_HEADS, 2 * NA_KH - 1, 2 * NA_KW - 1), 0.1),
        "pool_w": nrm(ks[12], (N_EVEN, POOL_GROUPS, POOL_GROUP_DIM, POOL_GROUP_DIM), POOL_GROUP_DIM ** -0.5),
        "pool_scale": 1.0 + nrm(ks[13], (N_EVEN, POOL_WIDTH), 0.1),
        "conv_w_in": nrm(ks[14], (N_ODD, D, 3 * CONV_WIDTH), D ** -0.5),
        "conv_w": nrm(ks[15], (N_ODD, CONV_K, CONV_WIDTH), CONV_K ** -0.5),
        "conv_w_out": nrm(ks[16], (N_ODD, CONV_WIDTH, D), CONV_WIDTH ** -0.5),
        "final_g": 1.0 + nrm(ks[17], (D,), 0.02),
    }

def second_block(x, c, ctx, c_ctx, mod_w, mod_b, norm_g, ffn_w13, ffn_w2, even_w_in, even_w_out,
              na_rpb, pool_w, pool_scale, conv_w_in, conv_w, conv_w_out, final_g):
    for i in range(DEPTH_2):
        even = (i % 2 == 0)
        ctx_out = any(j % 2 == 0 for j in range(i + 1, DEPTH_2))
        ctx_here = even or ctx_out
        m_l = adaln(c[:, None, :], mod_w[i], mod_b[i])
        m_c = adaln(c_ctx[None, None, :], mod_w[i], mod_b[i])

        x = ffn_sublayer(x, m_l, norm_g[i, 0], ffn_w13[i, 0], ffn_w2[i, 0], 0)
        if ctx_here:
            ctx = ffn_sublayer(ctx, m_c, norm_g[i, 0], ffn_w13[i, 0], ffn_w2[i, 0], 0)

        xn = modulate(rms_norm_2(x, norm_g[i, 1]), m_l[:, :, 3], m_l[:, :, 4])
        y_c = None
        if even:
            e = i // 2
            cn = modulate(rms_norm_2(ctx, norm_g[i, 1]), m_c[:, :, 3], m_c[:, :, 4])
            y_l, y_c = even_mixer(xn, cn, even_w_in[e], even_w_out[e], na_rpb[e],
                                  pool_w[e], pool_scale[e], ctx_out)
        else:
            o = i // 2
            y_l = short_conv_mixer(xn, conv_w_in[o], conv_w[o], conv_w_out[o])
            if ctx_out:
                cn = modulate(rms_norm_2(ctx, norm_g[i, 1]), m_c[:, :, 3], m_c[:, :, 4])
                y_c = short_conv_mixer(cn, conv_w_in[o], conv_w[o], conv_w_out[o])
        x = x + m_l[:, :, 5] * y_l

        x = ffn_sublayer(x, m_l, norm_g[i, 2], ffn_w13[i, 1], ffn_w2[i, 1], 6)
        if ctx_out:
            ctx = ctx + m_c[:, :, 5] * y_c
            ctx = ffn_sublayer(ctx, m_c, norm_g[i, 2], ffn_w13[i, 1], ffn_w2[i, 1], 6)

    return rms_norm_2(x, final_g)


def setup_inputs(seed=0):
    out = dict(first_inputs(seed))
    for name, value in second_inputs(seed + 1).items():
        if name != "x":
            out[name + "_2"] = value
    return out


def reference(
    x, c, mod_w, mod_b, norm1_g, norm2_g, w_in, b_in, sinks, diff_lambda, diff_subln_g, cmp_pos,
    cmp_w1, cmp_b1, cmp_w2, cmp_b2, w_branch, w_out, router_w, router_b, exp_w1, exp_b1, exp_w2,
    exp_b2, final_g, c_2, ctx_2, c_ctx_2, mod_w_2, mod_b_2, norm_g_2, ffn_w13_2, ffn_w2_2,
    even_w_in_2, even_w_out_2, na_rpb_2, pool_w_2, pool_scale_2, conv_w_in_2, conv_w_2,
    conv_w_out_2, final_g_2,
):
    x = first_block(
        x, c, mod_w, mod_b, norm1_g, norm2_g, w_in, b_in, sinks, diff_lambda, diff_subln_g,
        cmp_pos, cmp_w1, cmp_b1, cmp_w2, cmp_b2, w_branch, w_out, router_w, router_b, exp_w1,
        exp_b1, exp_w2, exp_b2, final_g,
    )
    return second_block(
        x, c_2, ctx_2, c_ctx_2, mod_w_2, mod_b_2, norm_g_2, ffn_w13_2, ffn_w2_2, even_w_in_2,
        even_w_out_2, na_rpb_2, pool_w_2, pool_scale_2, conv_w_in_2, conv_w_2, conv_w_out_2,
        final_g_2,
    )


_drawn_inputs = setup_inputs


def setup_inputs(seed=0):
    import zlib

    import numpy as np

    out = dict(_drawn_inputs(seed))
    spreads = {}
    factors = {'b_in': 3.574,
     'sinks': 7.095,
     'diff_lambda': 5.343,
     'cmp_pos': 5.94,
     'cmp_b1': 8.0,
     'cmp_b2': 8.0,
     'router_b': 3.652,
     'exp_b1': 8.0,
     'exp_b2': 8.0,
     'mod_b_2': 3.183,
     'norm_g_2': 3.962,
     'na_rpb_2': 8.0,
     'final_g_2': 2.865}
    for name, (base, spread) in spreads.items():
        noise = np.random.default_rng([zlib.crc32(name.encode()), seed]).standard_normal(out[name].shape)
        drawn = base * np.exp(spread * noise) if base else spread * noise
        out[name] = jnp.asarray(drawn.astype(out[name].dtype))
    for name, factor in factors.items():
        out[name] = (out[name] * factor).astype(out[name].dtype)
    return out
```

```python
from contextlib import ExitStack

import numpy as np

import concourse.bass as bass
from concourse import mybir

ALU = mybir.AluOpType
ACT = mybir.ActivationFunctionType
F32 = mybir.dt.float32
BF16 = mybir.dt.bfloat16
I32 = mybir.dt.int32
AX_X = mybir.AxisListType.X

P = 128
D = 1024
T = 256
DC = D // P
TB = T // P
EPS1, EPS2 = 1e-5, 1e-6
HD = 64
N_EXPERTS, TOP_K = 32, 4
LIMIT, ALPHA = 7.0, 1.702
NCMP = (T - 32) // 16 + 1
LAM_INIT = 0.8 - 0.6 * 1.0
NEG = -1e30
FF = 2816
FC = FF // P
N_MOD = 9
GRID_W, ROWS = 64, T // 64
KW = 16

Z_QA, Z_QC, Z_QB, Z_KB, Z_KA, Z_VA, Z_VB, Z_KCM, Z_VCM, Z_KSL, Z_VSL, Z_KWN, Z_VWN, Z_GATE, Z_MERGE = (
    0, 4, 8, 12, 16, 17, 18, 22, 23, 24, 25, 26, 27, 28, 29)
Z_ALL = Z_MERGE + 3 * DC
Z_V = [Z_VA, Z_VB, Z_VB + 1, Z_VB + 2, Z_VB + 3, Z_VSL, Z_VWN]
Z_PASSES = [(0, 8), (8, 8), (16, 8), (24, 5)]

RING = 12
SLOT = 2 * D

CAP = 96
ROUNDS = -(-T // CAP)
PAIRS = N_EXPERTS // 2

VECS = [
    ("c", DC), ("mod_b", 6 * DC), ("norm1", DC), ("norm2", DC), ("b_in", Z_ALL), ("final1", DC),
    ("exp_b1", N_EXPERTS * 2 * DC), ("exp_b2", N_EXPERTS * DC), ("cmp_pos", 2 * 16), ("cmp_b1", 4),
    ("cmp_b2k", 1), ("cmp_b2v", HD), ("cmp_w2", 4 * P), ("sinks", 8), ("lambda", 4 * HD), ("subln", P),
    ("router_w", DC * N_EXPERTS), ("router_b", N_EXPERTS), ("cond2", 2 * DC), ("mod_b2", 2 * N_MOD * DC),
    ("norm_g2", 2 * 3 * DC), ("pool_w", 4 * P), ("pool_scale", 4), ("conv_w", 3 * DC), ("final2", DC),
]
VEC_AT = {}
_at = 0
for _name, _width in VECS:
    VEC_AT[_name] = (_at, _width)
    _at += _width
VEC_COLS = _at

CONSTS = [("ident", P), ("ones", P), ("before", P), ("iota", P), ("col_mask", GRID_W),
          ("cmp_bias", 2 * 16), ("cmp_valid", 2 * 16)]
CONST_AT = {}
_at = 0
for _name, _width in CONSTS:
    CONST_AT[_name] = (_at, _width)
    _at += _width
CONST_COLS = _at

ATT = [(kind, blk, g) for kind in ("swa", "slc", "win", "diff") for blk in range(TB) for g in range(2)]
NA_STEPS = [(blk, pair) for blk in range(TB) for pair in range(4)]


MODS = [(1, 0, g, 1) for g in range(6)] + [(2, layer, g, 2 if (layer, g) < (0, 5) else 1)
                                           for layer in range(2) for g in range(N_MOD)]
MOD_SUMS = 3
ATT_MOD_SLOTS = [4 * N_MOD * s // len(ATT) for s in range(len(ATT) + 1)]


def mod_unit(n):
    return f"mod{n}"


def mods_ending(lo, hi):
    return [6 + s // 4 for s in range(lo, hi) if s % 4 == 3]


class Plan:

    def __init__(self):
        self.units, self.n_units = {}, 0
        self.slots, self.stream = {}, []
        self.released = {}
        self.n_slot_signals = 0
        self.mod_at, self.n_mod_slots = [], 0

    def unit(self, name, n=1):
        self.units[name] = self.n_units
        self.n_units += n

    def load(self, name, sources):
        self.slots[name] = len(self.stream)
        self.stream += sources

    def gemm(self, name, tensor, index, k_chunks, col0, cols, n_units, mods_between=0):
        self.unit(name, n_units)
        self.slots[name] = []
        for k in range(0, k_chunks, 2):
            self.slots[name].append(len(self.stream))
            if k + 2 < k_chunks:
                self.n_slot_signals += 1
                self.released[len(self.stream)] = ("slots", self.n_slot_signals)
            else:
                self.released[len(self.stream)] = ("units", self.n_units)
            self.stream.append((tensor, index, k, 2, col0, cols))
            self.mod_slots(mods_between)

    def mod_slots(self, n):
        for _ in range(n):
            block_, layer, g, _ = MODS[self.n_mod_slots // 4]
            self.mod_at.append(len(self.stream))
            self.n_mod_slots += 1
            self.released[len(self.stream)] = ("mods", self.n_mod_slots)
            k = 2 * ((self.n_mod_slots - 1) % 4)
            self.stream.append(("mod_w" if block_ == 1 else "mod_w_2", layer, k, 2, g * D, D))


def make_plan():
    p = Plan()
    p.mod_slots(8)
    p.unit(mod_unit(0))
    p.unit(mod_unit(1))
    p.unit("norm0")
    for n, (c0, nc_) in enumerate(Z_PASSES):
        p.gemm(f"z{n}", "w_in", 0, DC, c0 * P, nc_ * P, 2, mods_between=1)
        p.unit(mod_unit(2 + n))
    p.unit("vnat", 2)
    p.load("cmp_w1", [("cmp_w1", kv, 8 * half, 8, 0, 256) for kv in range(2) for half in range(2)])
    p.unit("cmp_hidden")
    for s in range(4):
        p.released[p.slots["cmp_w1"] + s] = ("units", p.n_units)
    p.unit("cmp_kv")
    p.unit("cmp_scores")
    p.unit("cmp_turn", 2)
    p.unit("cmp_out")
    p.unit("scores0")
    for s in range(len(ATT)):
        if s + 1 < len(ATT):
            p.unit(f"scores{s + 1}")
        p.mod_slots(ATT_MOD_SLOTS[s + 1] - ATT_MOD_SLOTS[s])
        p.unit(f"turn{s}")
        p.unit(f"out{s}")
        for n in mods_ending(*ATT_MOD_SLOTS[s:s + 2]):
            p.unit(mod_unit(n))
    p.unit("branch_turn", 3)
    for b in range(3):
        p.gemm(f"merge{b}", "w_in", 0, DC, (Z_MERGE + b * DC) * P, D, 2)
        p.gemm(f"branch{b}", "w_branch", b, 4, 0, D, 2)
    p.gemm("w_out", "w_out", 0, DC, 0, D, 2)
    p.unit("norm1")
    p.unit("h_turn", 2)
    p.unit("logits")
    p.unit("positions")
    while p.n_units % 4:
        p.unit("pad")
        p.n_pad = p.n_units
    p.moe_unit, p.moe_slot, p.moe_signals = p.n_units, len(p.stream), p.n_slot_signals
    p.n_units += 16 * PAIRS
    p.stream += [None] * (24 * PAIRS)
    p.n_slot_signals += 18 * PAIRS
    for s in range(len(p.stream) - RING, len(p.stream)):
        p.released[s] = ("experts", 0)
    p.unit("norm2")
    for f in range(4):
        sets = 2 if f == 0 else 1
        if f == 0:
            p.unit("norm3")
            p.unit("norm4")
        else:
            p.unit(f"norm{(7, 8, 10)[f - 1]}")
        for ab in range(2):
            for n, (c0, nc_) in enumerate(((0, 8), (8, 8), (16, 6))):
                layer1 = f == 0 and ab == 0
                p.gemm(f"ffn{f}_{'ab'[ab]}{n}", "ffn_w13", f, DC, ab * FF + c0 * P, nc_ * P, 2 * sets,
                       mods_between=3 if layer1 else 0)
                if layer1:
                    for m in range(3):
                        p.unit(mod_unit(6 + N_MOD + 3 * n + m))
        p.gemm(f"ffn{f}_out", "ffn_w2", f, FC, 0, D, 2 * sets)
        if f == 0:
            p.unit("norm5")
            p.unit("norm6")
            p.gemm("even_qk", "even_w_in", 0, DC, 0, D, 3)
            p.gemm("even_vu", "even_w_in", 0, DC, D, D, 3)
            p.unit("na_vturn", 2)
            p.unit("pool_map")
            p.unit("pool_out")
            p.unit("na_scores0")
            for s in range(len(NA_STEPS)):
                if s + 1 < len(NA_STEPS):
                    p.unit(f"na_scores{s + 1}")
                p.unit(f"na_turn{s}")
                p.unit(f"na_out{s}")
            p.unit("na_oturn")
            p.gemm("even_out", "even_w_out", 0, DC, 0, D, 2)
        if f == 2:
            p.unit("norm9")
            for n in range(3):
                p.gemm(f"conv{n}", "conv_w_in", 0, DC, n * D, D, 2)
            p.gemm("conv_out", "conv_w_out", 0, DC, 0, D, 2)
    p.unit("norm11")
    return p


def mod_buffers():
    at, holder, buffers, earlier = 0, [None] * MOD_SUMS, [], []
    for n, (_, _, _, conds) in enumerate(MODS):
        mine = [(at + c) % MOD_SUMS for c in range(conds)]
        buffers.append(mine)
        earlier.append([holder[b] for b in mine])
        for b in mine:
            holder[b] = n
        at += conds
    return buffers, earlier


MOD_BUFFERS, MOD_BUFFER_BEFORE = mod_buffers()
PLAN = make_plan()
U = PLAN.units
N_NORMS = 12


class Steps:

    def __init__(self, eng, sem):
        self.eng, self.sem, self.n, self.per_turn, self.turn, self.first = eng, sem, 0, 0, None, 0

    def done(self, ins):
        ins.then_inc(self.sem, 1)
        self.n += 1

    def settle(self):
        self.eng.wait_ge(self.sem, self.n if self.turn is None else self.turn * self.per_turn + self.n)

    def link(self, ins):
        self.done(ins)
        self.settle()

    def enter(self, turn, per_turn):
        self.turn, self.per_turn, self.first = turn, per_turn, self.n

    def leave(self, turns):
        assert self.n - self.first == self.per_turn, (self.n - self.first, self.per_turn)
        self.n, self.turn = self.first + turns * self.per_turn, None


def build(nc, ins, out):
    with ExitStack() as ctx:
        def sb(name, shape, dt=F32):
            return ctx.enter_context(nc.sbuf_tensor(name, shape, dt))

        sems = {}

        def sem(name):
            if name not in sems:
                sems[name] = ctx.enter_context(nc.semaphore(name))
            return sems[name]

        ring = sb("ring", [P, RING, SLOT])
        vecs = sb("vecs", [P, VEC_COLS])
        consts = sb("consts", [P, CONST_COLS])
        xT = sb("xT", [P, DC, T])
        hT = sb("hT", [P, DC, T])
        rstd = sb("rstd", [P, 2, T])
        cs = sb("cs", [P, DC])
        cs2 = sb("cs2", [P, DC, 2])
        mod1 = sb("mod1", [P, 6, DC])
        mod2 = sb("mod2", [P, 2, N_MOD, DC, 2])
        mod_sums = sb("mod_sums", [P, MOD_SUMS, D])
        stats = sb("stats", [P, 4, len(ATT), 4])
        small = sb("small", [P, 512])
        count_max = sb("count_max", [P, 1], I32)
        ARENA = 19456
        arena = sb("arena", [P, ARENA])
        psum = ctx.enter_context(nc.psum_tensor("psum", [P, 4, 1024], F32))

        def vec(name, *dims):
            at, width = VEC_AT[name]
            v = vecs[:, at:at + width]
            return v

        def const(name):
            at, width = CONST_AT[name]
            return consts[:, at:at + width]

        ident, ones, before = const("ident"), const("ones"), const("before")

        def area(at, *dims):
            n = int(np.prod(dims))
            assert at + n <= ARENA, (at, n)
            v = arena[:, at:at + n]
            if len(dims) == 2:
                v = v.rearrange("p (a b) -> p a b", a=dims[0])
            if len(dims) == 3:
                v = v.rearrange("p (a b c) -> p a b c", a=dims[0], b=dims[1])
            return v

        zT = area(0, 29, T)
        vnat = area(7424, TB, 7 * P)
        alibi_full = area(9216, 1024).bitcast(BF16).rearrange("p (h k) -> p h k", h=8)
        alibi_near = area(10240, 1024).bitcast(BF16).rearrange("p (h k) -> p h k", h=8)
        o_nat = area(13312, TB, 3, 512)
        probs = area(16384, 2, 1024)
        probsT = area(18432, 1024)
        blocks = area(13312, 2, 16 * 32)
        cmpP = area(14336, TB * 8, 16)
        cmpPT = area(16384, 2048)
        gm = area(0, 3 * DC, T)
        oT = area(9216, 12, T)
        merged = area(13312, DC, T)
        merge_tmp = area(15360, 4, T)
        cT = area(0, DC, T)
        acc = area(2048, DC, T)
        h_nat = area(4096, TB, D)
        moe = {}
        at = 6144
        for name, n in (("xg", DC * CAP), ("hid", DC * CAP), ("yN", D), ("selT", T),
                        ("sel", TB * CAP), ("selG", TB * CAP)):
            for e in range(2):
                moe[name, e] = (at, n)
                at += n
        for name in ("g", "u", "sig"):
            moe[name] = (at, DC * CAP)
            at += DC * CAP
        assert at <= ARENA

        def moe_buf(key, a=None):
            at_, n = moe[key]
            return area(at_, n) if a is None else area(at_, a, n // a)

        hC = area(2048, DC, T)
        hm = area(4096, 2, FC, T)
        rpb = area(15360, TB * 8, T)
        z2q, z2k, z2v, z2u = area(4096, 4, T), area(5120, 4, 2 * T), area(7168, 4, 2 * T), area(9216, 4, T)
        vnat2 = area(10240, 4, 512)
        pool_band = area(12288, TB, 4, T)
        cat = area(7168, DC, T)
        na_probs = area(0, 2, 512)
        na_probsT = area(1024, 1024)
        pool_mapped = area(2048, TB, 512)
        na_o = area(3072, TB, 512)
        conv_b, conv_c, conv_y = area(4096, DC, T), area(6144, DC, T), area(8192, DC, T)
        conv_z = area(10240, DC, T + 2)

        landed = [sem(f"slot_landed{i}") for i in range(RING)]
        slots_used = sem("slots_used")
        psum_full = sem("psum_full")
        psum_free = [sem(f"psum_free{i}") for i in range(4)]
        dve_steps = sem("dve_steps")

        def unit(u):
            return psum[:, u % 4, :]

        def open_unit(pe, u, turn=None, per_turn=0, free=None):
            n = u // 4
            if turn is not None:
                pe.wait_ge((free or psum_free)[u % 4], turn * (per_turn // 4) + n)
            elif n:
                pe.wait_ge((free or psum_free)[u % 4], n)

        def await_unit(eng, u, turn=None, per_turn=0, full=None):
            eng.wait_ge(full or psum_full, u + 1 if turn is None else turn * per_turn + (u + 1))

        def await_freed(eng, u, turn=None, per_turn=0, free=None):
            n = u // 4 + 1
            eng.wait_ge((free or psum_free)[u % 4], n if turn is None else turn * (per_turn // 4) + n)

        def await_slot(pe, s):
            pe.wait_ge(landed[s % RING], 16 * (s // RING + 1))

        def slot_ap(s, rows=2, cols=D):
            return ring[:, s % RING, 0:rows * cols].rearrange("p (k n) -> p k n", k=rows)

        def source(entry):
            name, index, k0, rows, c0, cols = entry
            t = ins[name][index]
            return t.rearrange("(k p) n -> p k n", p=P)[:, k0:k0 + rows, c0:c0 + cols]

        moe_end = PLAN.moe_slot + 24 * PAIRS
        block = ctx.enter_context(nc.Block())

        MOE_SLOTS = [("exp_w1", e, k, half) for e in range(2) for half in range(2) for k in range(0, DC, 2)] + \
                    [("exp_w2", e, k, 0) for e in range(2) for k in range(0, DC, 2)]
        GEMM_UNITS = [(4, 1), (5, 1), (6, 1), (7, 1), (8, 1), (9, 1)]
        MOE_RELEASE = []
        for j in range(24):
            gemm, k = divmod(j, 4)
            MOE_RELEASE.append(("units", GEMM_UNITS[gemm][0] + 1) if k == 3 else ("slots", gemm * 3 + k + 1))

        def load_pairs(sp, turn, base_slot, signals, units, full, used, land, land_base, first_waits):
            for j, (name, e, k, half) in enumerate(MOE_SLOTS):
                if j >= RING:
                    kind, n = MOE_RELEASE[j - RING]
                    if kind == "units":
                        sp.wait_ge(full, turn * 16 + (units + n))
                    else:
                        sp.wait_ge(used, turn * 18 + (signals + n))
                else:
                    first_waits(j)
                w = ins[name][turn * 2 + e] if name == "exp_w1" else ins[name][turn * 2 + e]
                src = w.rearrange("(k p) n -> p k n", p=P)[:, k:k + 2, half * D:(half + 1) * D]
                sp.dma_start(slot_ap(base_slot + j), src).then_inc(land[(base_slot + j) % RING], 16)

        def rounds_loop(eng, body):
            with eng.Fori(0, ROUNDS - 1) as r:
                with eng.Fori(0, PAIRS) as i:
                    body(eng, i, r * PAIRS + i)

        full_x, used_x = sem("psum_full_x"), sem("slots_used_x")
        free_x = [sem(f"psum_free_x{i}") for i in range(4)]
        landed_x = [sem(f"slot_landed_x{i}") for i in range(RING)]

        def many(eng):
            eng.wait_ge(sem("count_ready"), 1)
            return eng.value_load(count_max[0:1, 0:1], min_val=0, max_val=T)

        @block.sync
        def _(sp):
            def stream(s0, s1):
                for s in range(s0, s1):
                    if s >= RING:
                        kind, n = PLAN.released[s - RING]
                        if kind == "slots":
                            sp.wait_ge(slots_used, n)
                        elif kind == "units":
                            sp.wait_ge(psum_full, n)
                        elif kind == "mods":
                            sp.wait_ge(sem("mod_slots_used"), n)
                    entry = PLAN.stream[s]
                    sp.dma_start(slot_ap(s, entry[3], entry[5]), source(entry)).then_inc(landed[s % RING], 16)

            stream(0, PLAN.moe_slot)

            def ahead(j):
                s = PLAN.moe_slot + j - RING
                kind, n = PLAN.released[s]
                sp.wait_ge(slots_used if kind == "slots" else psum_full, n)

            load_pairs(sp, 0, PLAN.moe_slot, PLAN.moe_signals, PLAN.moe_unit, psum_full, slots_used, landed, 0, ahead)
            with sp.Fori(1, PAIRS) as i:
                def before_turn(j, i=i):
                    kind, n = MOE_RELEASE[j + RING]
                    if kind == "units":
                        sp.wait_ge(psum_full, i * 16 + (PLAN.moe_unit + n - 16))
                    else:
                        sp.wait_ge(slots_used, i * 18 + (PLAN.moe_signals + n - 18))
                load_pairs(sp, i, PLAN.moe_slot, PLAN.moe_signals, PLAN.moe_unit, psum_full, slots_used, landed, 0,
                           before_turn)
            with sp.If(many(sp) > CAP):
                sp.wait_ge(psum_full, PLAN.moe_unit + 16 * PAIRS)

                def pair(sp, i, turn):
                    def before_turn(j):
                        kind, n = MOE_RELEASE[j + RING]
                        if kind == "units":
                            sp.wait_ge(full_x, turn * 16 + n)
                        else:
                            sp.wait_ge(used_x, turn * 18 + n)
                    for j, (name, e, k, half) in enumerate(MOE_SLOTS):
                        if j >= RING:
                            kind, n = MOE_RELEASE[j - RING]
                            if kind == "units":
                                sp.wait_ge(full_x, turn * 16 + (16 + n))
                            else:
                                sp.wait_ge(used_x, turn * 18 + (18 + n))
                        else:
                            before_turn(j)
                        src = ins[name][i * 2 + e].rearrange("(k p) n -> p k n", p=P)[:, k:k + 2, half * D:(half + 1) * D]
                        sp.dma_start(slot_ap(PLAN.moe_slot + j), src).then_inc(
                            landed_x[(PLAN.moe_slot + j) % RING], 16)
                rounds_loop(sp, pair)
                sp.wait_ge(full_x, 16 + 16 * PAIRS * (ROUNDS - 1))
            for s in range(moe_end, moe_end + RING):
                kind, n = MOE_RELEASE[s - moe_end + RING]
                if kind == "units":
                    sp.wait_ge(psum_full, PLAN.moe_unit + 16 * (PAIRS - 1) + n)
                else:
                    sp.wait_ge(slots_used, PLAN.moe_signals + 18 * (PAIRS - 1) + n)
                entry = PLAN.stream[s]
                sp.dma_start(slot_ap(s, entry[3], entry[5]), source(entry)).then_inc(landed[s % RING], 16)
            stream(moe_end + RING, len(PLAN.stream))
            sp.wait_ge(sem("h_ready"), N_NORMS)
            sp.dma_start(out.rearrange("(k p) t -> p k t", p=P), hT[:, :, :]).then_inc(sem("stored"), 16)
            sp.wait_ge(sem("stored"), 16)

        @block.gpsimd
        def _(pool):
            pool.wait_ge(sem("rpb_landed"), 16 * ROWS)
            mask = const("col_mask")[:, None, :].broadcast_to([P, TB * 8 * ROWS, GRID_W])
            view = area(15360, TB * 8 * ROWS, GRID_W)
            pool.tensor_tensor(view, view, mask, ALU.add).then_inc(sem("rpb_masked"), 1)
            pool.wait_ge(sem("x_ready"), 6)
            pool.memset(conv_z[:, :, 0:1], 0.0).then_inc(sem("conv_edges"), 1)
            pool.memset(conv_z[:, :, T + 1:T + 2], 0.0).then_inc(sem("conv_edges"), 1)

        @block.scalar
        def _(act):
            act.dma_start(vecs[:, :], ins["vecs"]).then_inc(sem("vecs_landed"), 16)
            act.dma_start(consts[:, :], ins["consts"]).then_inc(sem("consts_landed"), 16)
            act.dma_start(xT[:, :, :], ins["xT"].rearrange("(k p) t -> p k t", p=P)).then_inc(sem("x_landed"), 16)
            act.dma_start(alibi_full, ins["alibi_full"]).then_inc(sem("alibi_landed"), 16)
            act.dma_start(alibi_near, ins["alibi_near"]).then_inc(sem("alibi_landed"), 16)

            act.wait_ge(sem("vecs_landed"), 16)
            act.activation(cs[:, :], vec("c"), ACT.Silu).then_inc(sem("cond_ready"), 1)
            act.activation(cs2[:, :, :], vec("cond2").rearrange("p (k s) -> p k s", s=2), ACT.Silu).then_inc(
                sem("cond_ready"), 1)

            act.wait_ge(sem("lambda_dots"), 1)
            act.activation(small[:, 412:414], small[:, 410:412], ACT.Exp).then_inc(sem("lambda_exp"), 1)

            def norm(n, src, squares):
                act.activation(squares, src, ACT.Square).then_inc(sem("squares_ready"), 1)
                await_freed(act, U[f"norm{n}"])
                act.activation(rstd[:, 1, :], rstd[:, 0, :], ACT.Sqrt).then_inc(sem("root_ready"), 1)

            act.wait_ge(sem("x_landed"), 16)
            norm(0, xT[:, :, :], hT[:, :, :])

            for b in range(TB):
                u = U["vnat"] + b
                await_unit(act, u)
                act.activation(vnat[:, b, :], unit(u)[:, 0:7 * P], ACT.Copy)
                act.activation(small[:, 24 * b:24 * b + 24], unit(u)[:, 7 * P:7 * P + 24],
                               ACT.Sigmoid).then_inc(psum_free[u % 4], 1)

            hidden = small[:, 64:192].rearrange("p (m f c) -> p m f c", m=2, f=2)
            cmp_bias = small[:, 192:196]
            act.wait_ge(sem("cmp_bias_ready"), 1)
            for m in range(2):
                for f in range(2):
                    last = act.activation(hidden[:, m, f, 0:2 * NCMP],
                                          unit(U["cmp_hidden"])[:, (2 * m + f) * 32:(2 * m + f) * 32 + 2 * NCMP],
                                          ACT.Gelu_apprx_tanh, bias=cmp_bias[:, 2 * m + f:2 * m + f + 1])
            last.then_inc(psum_free[U["cmp_hidden"] % 4], 1)
            act.wait_ge(sem("cmp_shifted"), 1)
            act.activation(cmpP[:, :, 0:NCMP], cmpP[:, :, 0:NCMP], ACT.Exp).then_inc(sem("cmp_exp"), 1)
            for n in range(2):
                u = U["cmp_turn"] + n
                await_unit(act, u)
                act.activation(cmpPT[0:NCMP, 1024 * n:1024 * n + 1024], unit(u)[0:NCMP, :], ACT.Copy).then_inc(
                    psum_free[u % 4], 1)
            await_unit(act, U["cmp_out"])

            def exps(s):
                kind, blk, g = ATT[s]
                kw = P * (blk + 1)
                u = U[f"scores{s}"]
                act.wait_ge(sem("row_max_ready"), s + 1)
                for j in range(4):
                    src = unit(u)[:, j * T:j * T + kw]
                    last = act.activation(probs[:, s % 2, j * T:j * T + kw], src, ACT.Exp,
                                          bias=stats[:, 1, s, j:j + 1], accum_out=stats[:, 2, s, j:j + 1])
                last.then_inc(psum_free[u % 4], 1)
                if kind == "swa":
                    act.activation(stats[:, 3, s, :], stats[:, 3, s, :], ACT.Exp).then_inc(sem("sink_exp"), 1)

            def turned(s):
                kind, blk, g = ATT[s]
                u = U[f"turn{s}"]
                n = 4 * (blk + 1) * P
                await_unit(act, u)
                act.activation(probsT[:, 0:n], unit(u)[:, 0:n], ACT.Copy).then_inc(psum_free[u % 4], 1)

            exps(0)
            for s in range(len(ATT)):
                if s + 1 < len(ATT):
                    exps(s + 1)
                turned(s)

            act.wait_ge(sem("subln_mean"), 1)
            act.activation(small[:, 400:408], small[:, 400:408], ACT.Sqrt).then_inc(sem("subln_root"), 1)

            for b in range(3):
                u = U["branch_turn"] + b
                await_unit(act, u)
                act.activation(oT[:, 4 * b:4 * b + 4, :], unit(u).rearrange("p (c t) -> p c t", c=4),
                               ACT.Copy).then_inc(psum_free[u % 4], 1)
            for b in range(3):
                for n in range(DC):
                    u = U[f"merge{b}"] + n // 4
                    z = Z_MERGE + b * DC + n
                    await_unit(act, u)
                    last = act.activation(gm[:, b * DC + n, :], unit(u)[:, (n % 4) * T:(n % 4 + 1) * T],
                                          ACT.Sigmoid, bias=vec("b_in")[:, z:z + 1])
                    if n % 4 == 3:
                        last.then_inc(psum_free[u % 4], 1)

            act.wait_ge(sem("x_ready"), 1)
            act.dma_start(cT, ins["ctxT"].rearrange("(k p) t -> p k t", p=P)).then_inc(sem("ctx_landed"), 16)
            for r in range(ROWS):
                half, blk = r % 2, r // 2
                act.dma_start(rpb[64 * half:64 * half + 64, 8 * blk:8 * blk + 8, :],
                              ins["rpb"][:, :, (7 - r) * GRID_W:(7 - r + ROWS) * GRID_W]).then_inc(
                    sem("rpb_landed"), 16)
            norm(1, xT[:, :, :], hT[:, :, :])

            for n in range(2):
                u = U["h_turn"] + n
                await_unit(act, u)
                act.activation(h_nat[:, n, :], unit(u)[:, :], ACT.Copy).then_inc(psum_free[u % 4], 1)
            route = small[:, 0:448]
            for b in range(TB):
                act.wait_ge(sem("top_ready"), b + 1)
                act.activation(route[:, 128 + 32 * b:160 + 32 * b], route[:, 36 * b:36 * b + 32], ACT.Exp,
                               bias=route[:, 88 + b:89 + b]).then_inc(sem("route_exp"), 1)

            def experts(turn, u0, full, free, x):
                def un(k):
                    return unit(u0 + k)

                def ready(k):
                    await_unit(act, u0 + k, turn, 16, full)
                for e in range(2):
                    ready(e)
                    act.activation(moe_buf(("xg", e), DC), un(e).rearrange("p (k c) -> p k c", k=DC)[:, :, 0:CAP],
                                   ACT.Copy).then_inc(free[(u0 + e) % 4], 1)
                for e in range(2):
                    ready(2 + e)
                    act.activation(moe_buf(("selT", e))[0:CAP, :], un(2 + e)[0:CAP, 0:T], ACT.Copy).then_inc(
                        free[(u0 + 2 + e) % 4], 1)
                for e in range(2):
                    act.wait_ge(sem("gate_clamped" + x), turn * 2 + (e + 1))
                    act.activation(moe_buf("sig"), moe_buf("g"), ACT.Sigmoid, scale=ALPHA).then_inc(
                        sem("gate_sigmoid" + x), 1)
                for e in range(2):
                    ready(10 + e)
                    act.activation(moe_buf(("yN", e))[0:CAP, :], un(10 + e)[0:CAP, :], ACT.Copy).then_inc(
                        free[(u0 + 10 + e) % 4], 1)

            with act.Fori(0, PAIRS) as i:
                experts(i, PLAN.moe_unit, psum_full, psum_free, "")
            with act.If(many(act) > CAP):
                rounds_loop(act, lambda eng, i, turn: experts(turn, 16, full_x, free_x, "_x"))

            act.wait_ge(sem("x_ready"), 2)
            norm(2, xT[:, :, :], hT[:, :, :])

            def ffn(f, sets):
                for n, (c0, nc_) in enumerate(((0, 8), (8, 8), (16, 6))):
                    for t in range(sets):
                        for half in range(2):
                            u = U[f"ffn{f}_a{n}"] + 2 * t + half
                            k = min(4, nc_ - 4 * half)
                            await_unit(act, u)
                            act.activation(hm[:, t, c0 + 4 * half:c0 + 4 * half + k, :],
                                           unit(u)[:, 0:k * T].rearrange("p (c t) -> p c t", c=k),
                                           ACT.Silu).then_inc(psum_free[u % 4], 1)

            act.wait_ge(sem("h_ready"), 3)
            norm(3, xT[:, :, :], hT[:, :, :])
            act.wait_ge(sem("ctx_landed"), 16)
            norm(4, cT, hC)
            ffn(0, 2)
            act.wait_ge(sem("x_ready"), 3)
            act.dma_start(pool_band, ins["pool_band"]).then_inc(sem("band_landed"), 16)
            norm(5, xT[:, :, :], hT[:, :, :])
            norm(6, cT, hC)
            for u, dst, scale in ((U["even_qk"], z2q, HD ** -0.5), (U["even_qk"] + 1, z2k[:, :, 0:T], 1.0),
                                  (U["even_qk"] + 2, z2k[:, :, T:2 * T], 1.0), (U["even_vu"], z2v[:, :, 0:T], 1.0),
                                  (U["even_vu"] + 1, z2u, 1.0), (U["even_vu"] + 2, z2v[:, :, T:2 * T], 1.0)):
                await_unit(act, u)
                act.activation(dst, unit(u).rearrange("p (c t) -> p c t", c=4), ACT.Copy, scale=scale).then_inc(
                    psum_free[u % 4], 1)
            for n in range(2):
                u = U["na_vturn"] + n
                await_unit(act, u)
                act.activation(vnat2[:, 2 * n:2 * n + 2, :], unit(u).rearrange("p (b c) -> p b c", b=2),
                               ACT.Copy).then_inc(psum_free[u % 4], 1)
            u = U["pool_map"]
            await_unit(act, u)
            act.activation(pool_mapped, unit(u).rearrange("p (b c) -> p b c", b=2), ACT.Copy).then_inc(
                psum_free[u % 4], 1)

            def na_exps(s):
                u = U[f"na_scores{s}"]
                act.wait_ge(sem("na_max_ready"), s + 1)
                if s >= 1:
                    await_unit(act, U[f"na_turn{s - 1}"])
                for j in range(2):
                    last = act.activation(na_probs[:, j, :], unit(u)[:, 512 * j:512 * j + 512], ACT.Exp,
                                          bias=stats[:, 1, s, j:j + 1], accum_out=stats[:, 2, s, j:j + 1])
                last.then_inc(psum_free[u % 4], 1)

            def na_turned(s):
                u = U[f"na_turn{s}"]
                await_unit(act, u)
                act.activation(na_probsT, unit(u), ACT.Copy).then_inc(psum_free[u % 4], 1)

            na_exps(0)
            for s in range(len(NA_STEPS)):
                na_turned(s)
                if s + 1 < len(NA_STEPS):
                    na_exps(s + 1)
            u = U["na_oturn"]
            await_unit(act, u)
            act.activation(cat[:, 0:4, :], unit(u).rearrange("p (c t) -> p c t", c=4), ACT.Copy).then_inc(
                psum_free[u % 4], 1)
            act.wait_ge(sem("x_ready"), 4)
            norm(7, xT[:, :, :], hT[:, :, :])
            ffn(1, 1)
            act.wait_ge(sem("x_ready"), 5)
            norm(8, xT[:, :, :], hT[:, :, :])
            ffn(2, 1)
            act.wait_ge(sem("x_ready"), 6)
            norm(9, xT[:, :, :], hT[:, :, :])
            for n, dst in enumerate((conv_b, conv_c)):
                for half in range(2):
                    u = U[f"conv{n}"] + half
                    await_unit(act, u)
                    act.activation(dst[:, 4 * half:4 * half + 4, :], unit(u).rearrange("p (c t) -> p c t", c=4),
                                   ACT.Copy).then_inc(psum_free[u % 4], 1)
            act.wait_ge(sem("x_ready"), 7)
            norm(10, xT[:, :, :], hT[:, :, :])
            ffn(3, 1)
            act.wait_ge(sem("x_ready"), 8)
            norm(11, xT[:, :, :], hT[:, :, :])

        @block.tensor
        def _(pe):
            def gemm(name, k_chunks, n_chunks, operands):
                slots, u0 = PLAN.slots[name], U[name]
                n_units = sum(-(-n // 4) for _, _, n in operands)
                for u in range(n_units):
                    open_unit(pe, u0 + u)
                for k in range(k_chunks):
                    s = slots[k // 2]
                    if k % 2 == 0:
                        await_slot(pe, s)
                    w = slot_ap(s, 2, n_chunks * P)
                    u = u0
                    for rhs, c0, n in operands:
                        for j in range(n):
                            mm = pe.matmul(unit(u + j // 4)[:, (j % 4) * T:(j % 4 + 1) * T],
                                           w[:, k % 2, (c0 + j) * P:(c0 + j + 1) * P], rhs(k),
                                           start=(k == 0 and j % 2 == 0), stop=(k == k_chunks - 1),
                                           skip_group_check=True)
                            if k == k_chunks - 1 and (j % 4 == 3 or j == n - 1):
                                mm.then_inc(psum_full, 1)
                        u += -(-n // 4)
                    if k % 2 == 1 and k != k_chunks - 1:
                        mm.then_inc(slots_used, 1)

            def mod_sum(n):
                conds = MODS[n][3]
                u = U[mod_unit(n)]
                pe.wait_ge(sem("mod_partials"), n + 1)
                open_unit(pe, u)
                for c in range(conds):
                    for j in range(DC):
                        at = j * conds + c
                        mm = pe.matmul(unit(u)[:, at:at + 1], mod_sums[:, MOD_BUFFERS[n][c], j * P:(j + 1) * P],
                                       ones[:, 0:1], start=True, stop=True)
                mm.then_inc(psum_full, 1)

            def norm(n, squares):
                pe.wait_ge(sem("squares_ready"), n + 1)
                u = U[f"norm{n}"]
                open_unit(pe, u)
                for k in range(DC):
                    mm = pe.matmul(unit(u)[:, 0:T], ones, squares[:, k, :], start=(k == 0), stop=(k == DC - 1))
                mm.then_inc(psum_full, 1)

            def h_rhs(k):
                return hT[:, k, :]

            def c_rhs(k):
                return hC[:, k, :]

            pe.wait_ge(sem("consts_landed"), 16)
            mod_sum(0)
            mod_sum(1)
            norm(0, hT)
            pe.wait_ge(sem("h_ready"), 1)
            for n, (c0, nc_) in enumerate(Z_PASSES):
                gemm(f"z{n}", DC, nc_, [(h_rhs, 0, nc_)])
                mod_sum(2 + n)
            pe.wait_ge(sem("z_ready"), len(Z_PASSES))
            for b in range(TB):
                u = U["vnat"] + b
                open_unit(pe, u)
                for n, z in enumerate(Z_V + [Z_GATE]):
                    mm = pe.transpose(unit(u)[:, n * P:(n + 1) * P], zT[:, z, b * P:(b + 1) * P], ident)
                mm.then_inc(psum_full, 1)
            pe.wait_ge(sem("blocks_ready"), 1)
            u = U["cmp_hidden"]
            open_unit(pe, u)
            for m in range(2):
                for half in range(2):
                    await_slot(pe, PLAN.slots["cmp_w1"] + 2 * m + half)
                for f in range(2):
                    for j in range(16):
                        w = slot_ap(PLAN.slots["cmp_w1"] + 2 * m + j // 8, 8, 256)
                        mm = pe.matmul(unit(u)[:, (2 * m + f) * 32:(2 * m + f) * 32 + 31],
                                       w[:, j % 8, f * P:(f + 1) * P],
                                       blocks[:, m, j * 32:j * 32 + 31], start=(j == 0), stop=(j == 15))
            mm.then_inc(psum_full, 1)
            hidden = small[:, 64:192].rearrange("p (m f c) -> p m f c", m=2, f=2)
            w2 = vec("cmp_w2").rearrange("p (m f c) -> p m f c", m=2, f=2)
            await_freed(pe, U["cmp_hidden"])
            u = U["cmp_kv"]
            open_unit(pe, u)
            for f in range(2):
                pe.matmul(unit(u)[:, 0:2 * NCMP], w2[:, 0, f, :], hidden[:, 0, f, 0:2 * NCMP],
                          start=(f == 0), stop=(f == 1))
            for g in range(2):
                for f in range(2):
                    mm = pe.matmul(unit(u)[0:NCMP, 512 + g * HD:512 + (g + 1) * HD],
                                   hidden[:, 1, f, g * NCMP:(g + 1) * NCMP], w2[:, 1, f, 0:HD],
                                   start=(f == 0), stop=(f == 1))
            mm.then_inc(psum_full, 1)
            kcT, vc = small[:, 200:230], small[:, 232:360]
            await_freed(pe, U["cmp_kv"])
            u = U["cmp_scores"]
            open_unit(pe, u)
            for b in range(TB):
                for g in range(2):
                    rows = slice(64 * g, 64 * g + 64)
                    for j in range(4):
                        at = 512 * g + (b * 4 + j) * 16
                        mm = pe.matmul(unit(u)[:, at:at + NCMP], zT[rows, Z_QC + j, b * P:(b + 1) * P],
                                       kcT[rows, g * NCMP:(g + 1) * NCMP], start=True, stop=True)
            mm.then_inc(psum_full, 1)
            pe.wait_ge(sem("cmp_probs"), 1)
            for b in range(TB):
                u = U["cmp_turn"] + b
                open_unit(pe, u)
                for h in range(8):
                    mm = pe.transpose(unit(u)[0:NCMP, h * P:(h + 1) * P], cmpP[:, b * 8 + h, 0:NCMP], ident)
                mm.then_inc(psum_full, 1)
            u = U["cmp_out"]
            open_unit(pe, u)
            for b in range(TB):
                await_freed(pe, U["cmp_turn"] + b)
                for h in range(8):
                    g = h // 4
                    mm = pe.matmul(unit(u)[:, b * 512 + h * HD:b * 512 + (h + 1) * HD],
                                   cmpPT[0:NCMP, (b * 8 + h) * P:(b * 8 + h + 1) * P],
                                   vc[0:NCMP, g * HD:(g + 1) * HD], start=True, stop=True)
            mm.then_inc(psum_full, 1)

            def scores(s):
                kind, blk, g = ATT[s]
                u = U[f"scores{s}"]
                rows = slice(64 * g, 64 * g + 64)
                open_unit(pe, u)
                for j in range(4):
                    qz, kz = {"swa": (Z_QA + j, Z_KA), "slc": (Z_QC + j, Z_KSL), "win": (Z_QC + j, Z_KWN),
                              "diff": (Z_QB + j, Z_KB + j)}[kind]
                    mm = pe.matmul(unit(u)[:, j * T:j * T + P * (blk + 1)], zT[rows, qz, blk * P:(blk + 1) * P],
                                   zT[rows, kz, 0:P * (blk + 1)], start=True, stop=True)
                mm.then_inc(psum_full, 1)

            def turn_and_apply(s):
                kind, blk, g = ATT[s]
                nb = blk + 1
                u = U[f"turn{s}"]
                await_freed(pe, U[f"scores{s}"])
                open_unit(pe, u)
                for j in range(4):
                    for kb in range(nb):
                        mm = pe.transpose(unit(u)[:, (j * nb + kb) * P:(j * nb + kb + 1) * P],
                                          probs[:, s % 2, j * T + kb * P:j * T + (kb + 1) * P], ident)
                mm.then_inc(psum_full, 1)
                await_freed(pe, u)
                u = U[f"out{s}"]
                open_unit(pe, u)
                dv = P if kind == "diff" else HD
                for j in range(4):
                    col = {"swa": HD * g, "slc": 5 * P + HD * g, "win": 6 * P + HD * g, "diff": P * (1 + j)}[kind]
                    for kb in range(nb):
                        mm = pe.matmul(unit(u)[:, j * dv:(j + 1) * dv], probsT[:, (j * nb + kb) * P:(j * nb + kb + 1) * P],
                                       vnat[:, kb, col:col + dv], start=(kb == 0), stop=(kb == nb - 1))
                mm.then_inc(psum_full, 1)

            scores(0)
            for s in range(len(ATT)):
                if s + 1 < len(ATT):
                    scores(s + 1)
                turn_and_apply(s)
                for n in mods_ending(*ATT_MOD_SLOTS[s:s + 2]):
                    mod_sum(n)
            pe.wait_ge(sem("branches_ready"), 1)
            for br in range(3):
                u = U["branch_turn"] + br
                open_unit(pe, u)
                for c in range(4):
                    for b in range(TB):
                        mm = pe.transpose(unit(u)[:, c * T + b * P:c * T + (b + 1) * P],
                                          o_nat[:, b, br, c * P:(c + 1) * P], ident)
                mm.then_inc(psum_full, 1)
            for br in range(3):
                gemm(f"merge{br}", DC, DC, [(h_rhs, 0, DC)])
                await_freed(pe, U["branch_turn"] + br)
                gemm(f"branch{br}", 4, DC, [(lambda k, br=br: oT[:, 4 * br + k, :], 0, DC)])
            pe.wait_ge(sem("merged_ready"), 1)
            gemm("w_out", DC, DC, [(lambda k: merged[:, k, :], 0, DC)])

            norm(1, hT)
            pe.wait_ge(sem("h_ready"), 2)
            for b in range(TB):
                u = U["h_turn"] + b
                open_unit(pe, u)
                for k in range(DC):
                    mm = pe.transpose(unit(u)[:, k * P:(k + 1) * P], hT[:, k, b * P:(b + 1) * P], ident)
                mm.then_inc(psum_full, 1)
            rw = vec("router_w").rearrange("p (k e) -> p k e", k=DC)
            u = U["logits"]
            open_unit(pe, u)
            for b in range(TB):
                for k in range(DC):
                    mm = pe.matmul(unit(u)[:, b * N_EXPERTS:(b + 1) * N_EXPERTS], hT[:, k, b * P:(b + 1) * P],
                                   rw[:, k, :], start=(k == 0), stop=(k == DC - 1))
            mm.then_inc(psum_full, 1)
            mask = small[:, 264:328]
            pe.wait_ge(sem("mask_ready"), 1)
            u = U["positions"]
            open_unit(pe, u)
            E = N_EXPERTS
            pe.matmul(unit(u)[:, 0:E], before, mask[:, 0:E], start=True, stop=True)
            pe.matmul(unit(u)[:, E:2 * E], ones, mask[:, 0:E], start=True, stop=False)
            pe.matmul(unit(u)[:, E:2 * E], before, mask[:, E:2 * E], start=False, stop=True)
            pe.matmul(unit(u)[:, 2 * E:3 * E], ones, mask[:, 0:E], start=True, stop=False)
            pe.matmul(unit(u)[:, 2 * E:3 * E], ones, mask[:, E:2 * E], start=False, stop=True).then_inc(psum_full, 1)
            for q in range(PLAN.moe_unit - U["positions"] - 1):
                open_unit(pe, U["positions"] + 1 + q)
                pe.matmul(unit(U["positions"] + 1 + q)[:, 0:E], before, mask[:, 0:E], start=True,
                          stop=True).then_inc(psum_full, 1)

            def experts(turn, u0, s_base, signals, full, free, used, land, x):
                def opened(k):
                    open_unit(pe, u0 + k, turn, 16, free)

                def freed(k):
                    await_freed(pe, u0 + k, turn, 16, free)

                def expert_gemm(j0, k_unit, rhs):
                    opened(k_unit)
                    u = unit(u0 + k_unit)
                    for k in range(DC):
                        j = j0 + k // 2
                        slot = (PLAN.moe_slot + j) % RING
                        if k % 2 == 0:
                            pe.wait_ge(land[slot], turn * 32 + 16 * ((s_base + j) // RING + 1))
                        w = slot_ap(PLAN.moe_slot + j)
                        for n in range(DC):
                            mm = pe.matmul(u[:, n * P:n * P + CAP], w[:, k % 2, n * P:(n + 1) * P], rhs[:, k, :],
                                           start=(k == 0 and n % 4 == 0), stop=(k == DC - 1),
                                           skip_group_check=True)
                        if k % 2 == 1:
                            mm.then_inc(used if k != DC - 1 else full, 1)

                pe.wait_ge(sem("sel_ready" + x), turn + 1)
                for e in range(2):
                    opened(e)
                    sel = moe_buf(("sel", e), TB)
                    for k in range(DC):
                        for b in range(TB):
                            mm = pe.matmul(unit(u0 + e)[:, k * P:k * P + CAP], h_nat[:, b, k * P:(k + 1) * P],
                                           sel[:, b, :], start=(b == 0), stop=(b == TB - 1))
                    mm.then_inc(full, 1)
                for e in range(2):
                    opened(2 + e)
                    sel = moe_buf(("selG", e), TB)
                    for b in range(TB):
                        mm = pe.transpose(unit(u0 + 2 + e)[0:CAP, b * P:(b + 1) * P], sel[:, b, :], ident)
                    mm.then_inc(full, 1)
                for e in range(2):
                    freed(e)
                    expert_gemm(8 * e, 4 + 2 * e, moe_buf(("xg", e), DC))
                    expert_gemm(8 * e + 4, 5 + 2 * e, moe_buf(("xg", e), DC))
                for e in range(2):
                    pe.wait_ge(sem("expert_hidden" + x), turn * 2 + (e + 1))
                    expert_gemm(16 + 4 * e, 8 + e, moe_buf(("hid", e), DC))
                for e in range(2):
                    freed(8 + e)
                    opened(10 + e)
                    y = moe_buf(("hid", e), DC)
                    for k in range(DC):
                        mm = pe.transpose(unit(u0 + 10 + e)[0:CAP, k * P:(k + 1) * P], y[:, k, :], ident)
                    mm.then_inc(full, 1)
                for e in range(2):
                    freed(2 + e)
                    freed(10 + e)
                    yN, selT = moe_buf(("yN", e)), moe_buf(("selT", e))
                    for k in range(DC):
                        c = 12 + 2 * e + k // 4
                        if k % 4 == 0:
                            opened(c)
                        mm = pe.matmul(unit(u0 + c)[:, (k % 4) * T:(k % 4 + 1) * T], yN[0:CAP, k * P:(k + 1) * P],
                                       selT[0:CAP, :], start=True, stop=True)
                        if k % 4 == 3:
                            mm.then_inc(full, 1)

            with pe.Fori(0, PAIRS) as i:
                experts(i, PLAN.moe_unit, PLAN.moe_slot, PLAN.moe_signals, psum_full, psum_free, slots_used, landed, "")
            with pe.If(many(pe) > CAP):
                for q in range(4):
                    pe.wait_ge(psum_free[q], (PLAN.moe_unit + 16 * PAIRS) // 4)
                pe.sem_inc(full_x, 16)
                pe.sem_inc(used_x, 18)
                rounds_loop(pe, lambda eng, i, turn: experts(turn, 16, 0, 18, full_x, free_x, used_x, landed_x, "_x"))
                for q in range(4):
                    pe.wait_ge(free_x[q], 4 + 4 * PAIRS * (ROUNDS - 1))

            norm(2, hT)

            def ffn(f, sets):
                rhs = [h_rhs, c_rhs][:sets]
                for ab in range(2):
                    for n, (c0, nc_) in enumerate(((0, 8), (8, 8), (16, 6))):
                        gemm(f"ffn{f}_{'ab'[ab]}{n}", DC, nc_, [(r, 0, nc_) for r in rhs])
                        if f == 0 and ab == 0:
                            for m in range(3):
                                mod_sum(6 + N_MOD + 3 * n + m)
                pe.wait_ge(sem("ffn_hidden"), f + 1)
                gemm(f"ffn{f}_out", FC, DC, [(lambda k, t=t: hm[:, t, k, :], 0, DC) for t in range(sets)])

            norm(3, hT)
            norm(4, hC)
            pe.wait_ge(sem("h_ready"), 5)
            ffn(0, 2)
            norm(5, hT)
            norm(6, hC)
            pe.wait_ge(sem("h_ready"), 7)
            gemm("even_qk", DC, DC, [(h_rhs, 0, 8), (c_rhs, 4, 4)])
            gemm("even_vu", DC, DC, [(h_rhs, 0, 8), (c_rhs, 0, 4)])
            await_freed(pe, U["even_vu"])
            await_freed(pe, U["even_vu"] + 2)
            for n in range(2):
                u = U["na_vturn"] + n
                open_unit(pe, u)
                for b in range(2):
                    for c in range(4):
                        at = (2 * n + b) * P
                        mm = pe.transpose(unit(u)[:, b * 512 + c * P:b * 512 + (c + 1) * P], z2v[:, c, at:at + P],
                                          ident)
                mm.then_inc(psum_full, 1)
            await_freed(pe, U["even_vu"] + 1)
            pw = vec("pool_w").rearrange("p (g n) -> p g n", g=4)
            u = U["pool_map"]
            open_unit(pe, u)
            for b in range(TB):
                for g in range(4):
                    mm = pe.matmul(unit(u)[:, b * 512 + g * P:b * 512 + (g + 1) * P], z2u[:, g, b * P:(b + 1) * P],
                                   pw[:, g, :], start=True, stop=True)
            mm.then_inc(psum_full, 1)
            await_freed(pe, u)
            pe.wait_ge(sem("band_landed"), 16)
            u = U["pool_out"]
            open_unit(pe, u)
            for g in range(4):
                for b in range(TB):
                    mm = pe.matmul(unit(u)[:, g * T:(g + 1) * T], pool_mapped[:, b, g * P:(g + 1) * P],
                                   pool_band[:, b, g, :], start=(b == 0), stop=(b == TB - 1))
            mm.then_inc(psum_full, 1)

            def na_scores(s):
                blk, pair = NA_STEPS[s]
                u = U[f"na_scores{s}"]
                open_unit(pe, u)
                for j in range(2):
                    rows = slice(64 * j, 64 * j + 64)
                    mm = pe.matmul(unit(u)[:, 512 * j:512 * j + 512], z2q[rows, pair, blk * P:(blk + 1) * P],
                                   z2k[rows, pair, :], start=True, stop=True)
                mm.then_inc(psum_full, 1)

            await_freed(pe, U["even_qk"])
            await_freed(pe, U["even_qk"] + 1)
            await_freed(pe, U["even_qk"] + 2)
            na_scores(0)
            for s in range(len(NA_STEPS)):
                if s + 1 < len(NA_STEPS):
                    na_scores(s + 1)
                blk, pair = NA_STEPS[s]
                u = U[f"na_turn{s}"]
                await_freed(pe, U[f"na_scores{s}"])
                open_unit(pe, u)
                for j in range(2):
                    for kb in range(4):
                        mm = pe.transpose(unit(u)[:, (4 * j + kb) * P:(4 * j + kb + 1) * P],
                                          na_probs[:, j, kb * P:(kb + 1) * P], ident)
                mm.then_inc(psum_full, 1)
                await_freed(pe, u)
                u = U[f"na_out{s}"]
                open_unit(pe, u)
                for j in range(2):
                    h = 2 * pair + j
                    for kb in range(4):
                        mm = pe.matmul(unit(u)[:, j * HD:(j + 1) * HD], na_probsT[:, (4 * j + kb) * P:(4 * j + kb + 1) * P],
                                       vnat2[:, kb, h * HD:(h + 1) * HD], start=(kb == 0), stop=(kb == 3))
                mm.then_inc(psum_full, 1)
            await_freed(pe, U[f"na_out{len(NA_STEPS) - 1}"])
            u = U["na_oturn"]
            open_unit(pe, u)
            for c in range(4):
                for b in range(TB):
                    mm = pe.transpose(unit(u)[:, c * T + b * P:c * T + (b + 1) * P], na_o[:, b, c * P:(c + 1) * P],
                                      ident)
            mm.then_inc(psum_full, 1)
            await_freed(pe, u)
            await_freed(pe, U["pool_out"])
            gemm("even_out", DC, DC, [(lambda k: cat[:, k, :], 0, DC)])
            for f in (1, 2):
                norm(6 + f, hT)
                pe.wait_ge(sem("h_ready"), 7 + f)
                ffn(f, 1)
            norm(9, hT)
            pe.wait_ge(sem("h_ready"), 10)
            for n in range(3):
                gemm(f"conv{n}", DC, DC, [(h_rhs, 0, DC)])
            pe.wait_ge(sem("conv_ready"), 1)
            gemm("conv_out", DC, DC, [(lambda k: conv_y[:, k, :], 0, DC)])
            norm(10, hT)
            pe.wait_ge(sem("h_ready"), 11)
            ffn(3, 1)
            norm(11, hT)

        @block.vector
        def _(dve):
            steps = Steps(dve, dve_steps)
            link = steps.link

            def wide(v, n):
                return v[:, :, None].broadcast_to([v.shape[0], v.shape[1], n])

            def chunks(u, n=4, width=T):
                return unit(u)[:, 0:n * width].rearrange("p (c t) -> p c t", c=n)

            def free(ins_, u):
                ins_.then_inc(psum_free[u % 4], 1)

            def finish(ins_, u, done):
                free(ins_, u)
                await_freed(dve, u)
                dve.sem_inc(sem(done), 1)

            dve.wait_ge(sem("vecs_landed"), 16)
            lp = vec("lambda").rearrange("p (n d) -> p n d", n=4)
            lam = small[:, 414:415]
            link(dve.tensor_tensor(lp[:, 0::2, :], lp[:, 0::2, :], lp[:, 1::2, :], ALU.mult))
            dve.tensor_reduce(small[:, 410:412], lp[:, 0::2, :], AX_X, ALU.add).then_inc(sem("lambda_dots"), 1)
            dve.wait_ge(sem("lambda_exp"), 1)
            link(dve.tensor_tensor(lam, small[:, 413:414], small[:, 412:413], ALU.subtract))
            link(dve.tensor_scalar(lam, lam, -LAM_INIT, None, ALU.add))
            link(dve.tensor_scalar(vec("subln"), vec("subln"), 1.0 - LAM_INIT, None, ALU.mult))

            dve.wait_ge(sem("cond_ready"), 2)

            def mod_slot(i):
                n, pair = divmod(i, 4)
                block_, layer, g, conds = MODS[n]
                s = PLAN.mod_at[i]
                await_slot(dve, s)
                w = slot_ap(s)
                for c in range(conds):
                    last_group = MOD_BUFFER_BEFORE[n][c]
                    if pair == 0 and last_group is not None:
                        await_unit(dve, U[mod_unit(last_group)])
                for k in (2 * pair, 2 * pair + 1):
                    for c in range(conds):
                        part = mod_sums[:, MOD_BUFFERS[n][c], :]
                        cond = cs[:, k:k + 1] if block_ == 1 else cs2[:, k, c:c + 1]
                        if k == 0:
                            last = dve.tensor_scalar(part, w[:, k % 2, :], cond, None, ALU.mult)
                        else:
                            last = dve.scalar_tensor_tensor(part, w[:, k % 2, :], cond, part, ALU.mult, ALU.add)
                        if (k % 2, c) != (1, conds - 1):
                            steps.done(last)
                    if k % 2 == 0:
                        steps.settle()
                last.then_inc(sem("mod_slots_used"), 1)
                dve.wait_ge(sem("mod_slots_used"), i + 1)
                if pair == 3:
                    dve.sem_inc(sem("mod_partials"), 1)

            def modulation(n):
                block_, layer, g, conds = MODS[n]
                u = U[mod_unit(n)]
                await_unit(dve, u)
                if block_ == 1:
                    free(dve.tensor_tensor(mod1[:, g, :], unit(u)[:, 0:DC], vec("mod_b")[:, g * DC:(g + 1) * DC],
                                           ALU.add), u)
                    if g in (1, 4):
                        await_freed(dve, u)
                        link(dve.scalar_tensor_tensor(mod1[:, g, :], mod1[:, g, :], 1.0,
                                                      vec("norm1" if g == 1 else "norm2"), ALU.add, ALU.mult))
                    return
                m = mod2[:, layer, g, :, 0:conds]
                at = (layer * N_MOD + g) * DC
                free(dve.tensor_tensor(m, unit(u)[:, 0:conds * DC].rearrange("p (k s) -> p k s", s=conds),
                                       wide(vec("mod_b2")[:, at:at + DC], conds), ALU.add), u)
                if g % 3 == 1:
                    await_freed(dve, u)
                    at = (layer * 3 + g // 3) * DC
                    link(dve.scalar_tensor_tensor(m, m, 1.0, wide(vec("norm_g2")[:, at:at + DC], conds), ALU.add,
                                                  ALU.mult))
                if g in (2, 8):
                    await_freed(dve, u)
                    link(dve.tensor_scalar(m, m, 0.5, None, ALU.mult))

            for i in range(8):
                mod_slot(i)
            modulation(0)
            modulation(1)

            def norm(n, src, dst, scale, shift, eps):
                u = U[f"norm{n}"]
                await_unit(dve, u)
                free(dve.tensor_scalar(rstd[:, 0, :], unit(u)[:, 0:T], 1.0 / D, eps, ALU.mult, ALU.add), u)
                dve.wait_ge(sem("root_ready"), n + 1)
                link(dve.reciprocal(rstd[:, 0, :], rstd[:, 1, :]))
                link(dve.tensor_tensor(dst, src, rstd[:, 0:1, :].broadcast_to([P, DC, T]), ALU.mult))
                for k in range(DC):
                    if shift is None:
                        last = dve.tensor_scalar(dst[:, k, :], dst[:, k, :], scale[:, k:k + 1], None, ALU.mult)
                    else:
                        last = dve.tensor_scalar(dst[:, k, :], dst[:, k, :], scale[:, k:k + 1], shift[:, k:k + 1],
                                                 ALU.mult, ALU.add)
                last.then_inc(sem("h_ready"), 1)

            norm(0, xT[:, :, :], hT[:, :, :], mod1[:, 1, :], mod1[:, 0, :], EPS1)
            for n, (c0, nc_) in enumerate(Z_PASSES):
                for i in range(8 + 4 * n, 12 + 4 * n):
                    mod_slot(i)
                for half in range(-(-nc_ // 4)):
                    u, k = U[f"z{n}"] + half, min(4, nc_ - 4 * half)
                    z = c0 + 4 * half
                    await_unit(dve, u)
                    last = dve.tensor_tensor(zT[:, z:z + k, :], chunks(u, k), wide(vec("b_in")[:, z:z + k], T), ALU.add)
                    if half == 0:
                        free(last, u)
                finish(last, u, "z_ready")
                modulation(2 + n)
            for m, z in enumerate((Z_KCM, Z_VCM)):
                dst = blocks[:, m, :].rearrange("p (j c) -> p j c", j=16)
                for g in range(2):
                    for odd in range(2):
                        for late in range(2):
                            src = zT[64 * g:64 * g + 64, z, 16 * late:16 * late + 16 * NCMP]
                            src = src.rearrange("p (c x) -> p x c", x=16)[:, odd::2, :]
                            dve.tensor_copy(dst[64 * odd:64 * odd + 64, 8 * late:8 * late + 8,
                                                g * NCMP:(g + 1) * NCMP], src)
                last = dve.tensor_copy(dst[:, :, 30:31], vec("cmp_pos")[:, 16 * m:16 * m + 16, None])
            last.then_inc(sem("blocks_ready"), 1)
            u = U["cmp_hidden"]
            await_unit(dve, u)
            dve.tensor_tensor(small[:, 192:196], unit(u)[:, 30:128:32], vec("cmp_b1"), ALU.add).then_inc(
                sem("cmp_bias_ready"), 1)
            u = U["cmp_kv"]
            await_unit(dve, u)
            dve.tensor_scalar(small[:, 200:230], unit(u)[:, 0:2 * NCMP], vec("cmp_b2k"), None, ALU.add)
            b2v = vec("cmp_b2v")[0:NCMP, None, :].broadcast_to([NCMP, 2, HD])
            free(dve.tensor_tensor(small[0:NCMP, 232:360].rearrange("p (g d) -> p g d", g=2),
                                   unit(u)[0:NCMP, 512:640].rearrange("p (g d) -> p g d", g=2), b2v, ALU.add), u)
            u = U["cmp_scores"]
            await_unit(dve, u)
            for b in range(TB):
                cb = const("cmp_bias")[:, None, 16 * b:16 * b + NCMP].broadcast_to([P, 4, NCMP])
                for g in range(2):
                    src = unit(u)[:, 512 * g + 64 * b:512 * g + 64 * b + 64]
                    src = src.rearrange("p (h c) -> p h c", h=4)[:, :, 0:NCMP]
                    last = dve.scalar_tensor_tensor(cmpP[:, 8 * b + 4 * g:8 * b + 4 * g + 4, 0:NCMP], src, HD ** -0.5,
                                                    cb, ALU.mult, ALU.add)
            free(last, u)
            await_freed(dve, u)
            cp = cmpP[:, :, 0:NCMP]
            link(dve.tensor_reduce(small[:, 360:376], cp, AX_X, ALU.max))
            dve.tensor_tensor(cp, cp, wide(small[:, 360:376], NCMP), ALU.subtract).then_inc(sem("cmp_shifted"), 1)
            dve.wait_ge(sem("cmp_exp"), 1)
            link(dve.tensor_reduce(small[:, 376:392], cp, AX_X, ALU.add))
            link(dve.reciprocal(small[:, 376:392], small[:, 376:392]))
            link(dve.tensor_tensor(cp, cp, wide(small[:, 376:392], NCMP), ALU.mult))
            for b in range(TB):
                cv = const("cmp_valid")[:, None, 16 * b:16 * b + NCMP].broadcast_to([P, 8, NCMP])
                last = dve.tensor_tensor(cmpP[:, 8 * b:8 * b + 8, 0:NCMP], cmpP[:, 8 * b:8 * b + 8, 0:NCMP], cv,
                                         ALU.mult)
            last.then_inc(sem("cmp_probs"), 1)
            u = U["cmp_out"]
            await_unit(dve, u)
            for b in range(TB):
                await_freed(dve, U["vnat"] + b)
                gates = small[:, 24 * b:24 * b + 24].rearrange("p (h r) -> p h r", h=8)
                last = dve.tensor_tensor(o_nat[:, b, 2, :].rearrange("p (h d) -> p h d", h=8),
                                         unit(u)[:, 512 * b:512 * b + 512].rearrange("p (h d) -> p h d", h=8),
                                         gates[:, :, 0:1].broadcast_to([P, 8, HD]), ALU.mult)
            free(last, u)

            dve.wait_ge(sem("alibi_landed"), 32)

            def soft(s):
                kind, blk, g = ATT[s]
                kw = P * (blk + 1)
                u = U[f"scores{s}"]
                table = alibi_near if kind == "swa" else alibi_full
                table = table[:, 1::2, T - kw:T] if kind == "diff" else table[:, 4 * g:4 * g + 4, T - kw:T]
                sc = chunks(u)[:, :, 0:kw]
                await_unit(dve, u)
                link(dve.scalar_tensor_tensor(sc, sc, HD ** -0.5, table, ALU.mult, ALU.add))
                link(dve.tensor_reduce(stats[:, 0, s, :], sc, AX_X, ALU.max))
                if kind == "swa":
                    sinks = vec("sinks")[:, 4 * g:4 * g + 4]
                    link(dve.tensor_tensor(stats[:, 0, s, :], stats[:, 0, s, :], sinks, ALU.max))
                    dve.tensor_tensor(stats[:, 3, s, :], sinks, stats[:, 0, s, :], ALU.subtract)
                dve.tensor_scalar(stats[:, 1, s, :], stats[:, 0, s, :], -1.0, None, ALU.mult).then_inc(
                    sem("row_max_ready"), 1)

            tmp = rstd[:, :, :].rearrange("p a t -> p (a t)")

            def attended(s):
                kind, blk, g = ATT[s]
                u = U[f"out{s}"]
                await_freed(dve, U[f"scores{s}"])
                if kind == "swa":
                    dve.wait_ge(sem("sink_exp"), [a[0] for a in ATT[:s + 1]].count("swa"))
                    link(dve.tensor_tensor(stats[:, 2, s, :], stats[:, 2, s, :], stats[:, 3, s, :], ALU.add))
                link(dve.reciprocal(stats[:, 2, s, :], stats[:, 2, s, :]))
                if kind in ("slc", "win"):
                    gates = small[:, 24 * blk:24 * blk + 24].rearrange("p (h r) -> p h r", h=8)
                    br = 1 if kind == "slc" else 2
                    link(dve.tensor_tensor(stats[:, 2, s, :, None], stats[:, 2, s, :, None],
                                           gates[:, 4 * g:4 * g + 4, br:br + 1], ALU.mult))
                if kind == "diff" and g == 1:
                    link(dve.tensor_scalar(stats[:, 2, s, :], stats[:, 2, s, :], lam, None, ALU.mult))
                dv = P if kind == "diff" else HD
                branch = {"swa": 0, "diff": 1, "slc": 2, "win": 2}[kind]
                at = 0 if kind == "diff" else 256 * g
                dst = o_nat[:, blk, branch, at:at + 4 * dv]
                adds = kind in ("slc", "win") or (kind == "diff" and g == 1)
                await_unit(dve, u)
                to = tmp[:, 0:4 * dv] if adds else dst
                free(dve.tensor_tensor(to.rearrange("p (h d) -> p h d", h=4), chunks(u, 4, dv),
                                       wide(stats[:, 2, s, :], dv), ALU.mult), u)
                if adds:
                    await_freed(dve, u)
                    link(dve.tensor_tensor(dst, dst, to, ALU.add))

            soft(0)
            for s in range(len(ATT)):
                if s + 1 < len(ATT):
                    soft(s + 1)
                if s:
                    for n in mods_ending(*ATT_MOD_SLOTS[s - 1:s + 1]):
                        modulation(n)
                for i in range(*ATT_MOD_SLOTS[s:s + 2]):
                    mod_slot(24 + i)
                attended(s)
            for n in mods_ending(*ATT_MOD_SLOTS[-2:]):
                modulation(n)
            for b in range(TB):
                link(dve.tensor_tensor(tmp, o_nat[:, b, 1, :], o_nat[:, b, 1, :], ALU.mult))
                link(dve.tensor_reduce(small[:, 400 + 4 * b:404 + 4 * b], tmp.rearrange("p (h d) -> p h d", h=4),
                                       AX_X, ALU.add))
            dve.tensor_scalar(small[:, 400:408], small[:, 400:408], 1.0 / P, EPS1, ALU.mult, ALU.add).then_inc(
                sem("subln_mean"), 1)
            dve.wait_ge(sem("subln_root"), 1)
            link(dve.reciprocal(small[:, 400:408], small[:, 400:408]))
            for b in range(TB):
                ob = o_nat[:, b, 1, :].rearrange("p (h d) -> p h d", h=4)
                link(dve.tensor_tensor(ob, ob, wide(small[:, 400 + 4 * b:404 + 4 * b], P), ALU.mult))
                last = dve.tensor_tensor(ob, ob, vec("subln")[:, None, :].broadcast_to([P, 4, P]), ALU.mult)
            last.then_inc(sem("branches_ready"), 1)

            for br in range(3):
                for half in range(2):
                    u = U[f"branch{br}"] + half
                    gate = gm[:, br * DC + 4 * half:br * DC + 4 * half + 4, :]
                    dst = merged[:, 4 * half:4 * half + 4, :]
                    await_freed(dve, U[f"merge{br}"] + half)
                    await_unit(dve, u)
                    if br == 0:
                        free(dve.tensor_tensor(dst, chunks(u), gate, ALU.mult), u)
                        await_freed(dve, u)
                    else:
                        free(dve.tensor_tensor(merge_tmp, chunks(u), gate, ALU.mult), u)
                        await_freed(dve, u)
                        last = dve.tensor_tensor(dst, dst, merge_tmp, ALU.add)
                        if (br, half) == (2, 1):
                            last.then_inc(sem("merged_ready"), 1)
                        else:
                            link(last)

            def add_to(dst, u0, gate):
                for k in range(DC):
                    u = u0 + k // 4
                    if k % 4 == 0:
                        await_unit(dve, u)
                    last = dve.scalar_tensor_tensor(dst[:, k, :], unit(u)[:, (k % 4) * T:(k % 4 + 1) * T],
                                                    gate[:, k:k + 1], dst[:, k, :], ALU.mult, ALU.add)
                    if k == 3:
                        free(last, u)
                return last, u

            finish(*add_to(xT, U["w_out"], mod1[:, 2, :]), "x_ready")
            norm(1, xT[:, :, :], hT[:, :, :], mod1[:, 4, :], mod1[:, 3, :], EPS1)

            E = N_EXPERTS
            vals, top, negmax = small[:, 0:72], small[:, 72:88], small[:, 88:90]
            total, expd, replaced = small[:, 92:94], small[:, 128:192], small[:, 192:264]
            mask, gate, place = small[:, 264:328], small[:, 328:392], small[:, 392:456]
            u = U["logits"]
            await_unit(dve, u)
            for b in range(TB):
                last = dve.tensor_tensor(vals[:, 36 * b:36 * b + E], unit(u)[:, E * b:E * b + E], vec("router_b"),
                                         ALU.add)
            free(last, u)
            await_freed(dve, u)
            for b in range(TB):
                link(dve.max(top[:, 8 * b:8 * b + 8], vals[:, 36 * b:36 * b + E]))
            for b in range(TB):
                dve.tensor_scalar(negmax[:, b:b + 1], top[:, 8 * b:8 * b + 1], -1.0, None, ALU.mult).then_inc(
                    sem("top_ready"), 1)
            for n in range(4):
                for b in range(TB):
                    link(dve.memset(vals[:, 36 * b + E + n:36 * b + E + n + 1], -(n + 1.0) * 1e37))
                    link(dve.memset(top[:, 8 * b + 4 + n:8 * b + 5 + n], -(n + 1.0) * 1e37))
            for b in range(TB):
                v, r = vals[:, 36 * b:36 * b + 36], replaced[:, 36 * b:36 * b + 36]
                link(dve.match_replace(r, top[:, 8 * b:8 * b + 8], v, 3e38))
                last = dve.tensor_tensor(mask[:, E * b:E * b + E], r[:, 0:E], v[:, 0:E], ALU.not_equal)
                link(last) if b == 0 else last.then_inc(sem("mask_ready"), 1)
            dve.wait_ge(sem("mask_ready"), 1)
            dve.wait_ge(sem("route_exp"), 2)
            link(dve.tensor_tensor(gate, expd, mask, ALU.mult))
            link(dve.tensor_reduce(total, gate.rearrange("p (b e) -> p b e", b=TB), AX_X, ALU.add))
            link(dve.reciprocal(total, total))
            link(dve.tensor_tensor(gate.rearrange("p (b e) -> p b e", b=TB), gate.rearrange("p (b e) -> p b e", b=TB),
                                   wide(total, E), ALU.mult))
            u = U["positions"]
            await_unit(dve, u)
            dve.scalar_tensor_tensor(place, unit(u)[:, 0:2 * E], 1.0, mask, ALU.add, ALU.mult)
            free(dve.tensor_reduce(small[:, 460:461], unit(u)[:, 2 * E:3 * E], AX_X, ALU.max), u)
            await_freed(dve, u)
            link(dve.tensor_scalar(place, place, -1.0, None, ALU.add))
            dve.tensor_copy(count_max[:, :], small[:, 460:461]).then_inc(sem("count_ready"), 1)
            for q in range(PLAN.moe_unit - U["positions"] - 1):
                u = U["positions"] + 1 + q
                await_unit(dve, u)
                free(dve.tensor_copy(small[:, 461:462], unit(u)[:, 0:1]), u)
                await_freed(dve, u)
            link(dve.memset(acc, 0.0))

            def experts(turn, steps, u0, full, free_, x):
                def un(k):
                    return unit(u0 + k).rearrange("p (k c) -> p k c", k=DC)[:, :, 0:CAP]

                def ready(k):
                    await_unit(dve, u0 + k, turn, 16, full)

                def freeing(ins_, k):
                    ins_.then_inc(free_[(u0 + k) % 4], 1)

                def freed(k):
                    await_freed(dve, u0 + k, turn, 16, free_)

                slot_no = const("iota")[:, 0:CAP]
                for e in range(2):
                    sel, sg = moe_buf(("sel", e), TB), moe_buf(("selG", e), TB)
                    for b in range(TB):
                        p_ = small[:, bass.ds(x_turn(turn) * 2 + (392 + E * b + e), 1)]
                        g_ = small[:, bass.ds(x_turn(turn) * 2 + (328 + E * b + e), 1)]
                        dve.tensor_scalar(sel[:, b, :], slot_no, p_, None, ALU.is_equal)
                        last = dve.tensor_scalar(sg[:, b, :], slot_no, p_, g_, ALU.is_equal, ALU.mult)
                last.then_inc(sem("sel_ready" + x), 1)
                gb, ub, sig = moe_buf("g", DC), moe_buf("u", DC), moe_buf("sig", DC)
                b1, b2 = VEC_AT["exp_b1"][0], VEC_AT["exp_b2"][0]
                for e in range(2):
                    ready(4 + 2 * e)
                    freeing(dve.tensor_tensor(gb, un(4 + 2 * e), bias_of(turn, b1 + 16 * e, 32), ALU.add), 4 + 2 * e)
                    freed(4 + 2 * e)
                    dve.tensor_scalar(gb, gb, LIMIT, None, ALU.min).then_inc(sem("gate_clamped" + x), 1)
                    ready(5 + 2 * e)
                    freeing(dve.tensor_tensor(ub, un(5 + 2 * e), bias_of(turn, b1 + 16 * e + DC, 32), ALU.add),
                            5 + 2 * e)
                    freed(5 + 2 * e)
                    steps.link(dve.tensor_scalar(ub, ub, LIMIT, -LIMIT, ALU.min, ALU.max))
                    dve.wait_ge(sem("gate_sigmoid" + x), turn * 2 + (e + 1))
                    steps.link(dve.tensor_tensor(gb, gb, sig, ALU.mult))
                    dve.scalar_tensor_tensor(moe_buf(("hid", e), DC), ub, 1.0, gb, ALU.add, ALU.mult).then_inc(
                        sem("expert_hidden" + x), 1)
                    dve.wait_ge(sem("expert_hidden" + x), turn * 2 + (e + 1))
                for e in range(2):
                    ready(8 + e)
                    freeing(dve.tensor_tensor(moe_buf(("hid", e), DC), un(8 + e), bias_of(turn, b2 + DC * e, 16),
                                              ALU.add), 8 + e)
                for k in range(12, 16):
                    ready(k)
                    half = k % 2
                    freeing(dve.tensor_tensor(acc[:, 4 * half:4 * half + 4, :], chunks(u0 + k),
                                              acc[:, 4 * half:4 * half + 4, :], ALU.add), k)
                    freed(k)

            pair_of = {}

            def x_turn(turn):
                return pair_of.get("pair", turn)

            def bias_of(turn, base, per_pair):
                return wide(vecs[:, bass.ds(x_turn(turn) * per_pair + base, DC)], CAP)

            with dve.Fori(0, PAIRS) as i:
                steps.enter(i, 4)
                experts(i, steps, PLAN.moe_unit, psum_full, psum_free, "")
                steps.leave(PAIRS)
            with dve.If(many(dve) > CAP):
                for q in range(4):
                    dve.sem_inc(free_x[q], 4)
                steps_x = Steps(dve, sem("dve_steps_x"))
                with dve.Fori(0, ROUNDS - 1) as r:
                    dve.tensor_scalar(place, place, -float(CAP), None, ALU.add).then_inc(sem("round_shifted"), 1)
                    dve.wait_ge(sem("round_shifted"), r + 1)
                    dve.memset(small[:, 463:464], 0.0)
                    with dve.Fori(0, PAIRS) as i:
                        pair_of["pair"] = i
                        turn = r * PAIRS + i
                        steps_x.enter(turn, 4)
                        experts(turn, steps_x, 16, full_x, free_x, "_x")
            pair_of.clear()
            for k in range(DC):
                last = dve.scalar_tensor_tensor(xT[:, k, :], acc[:, k, :], mod1[:, 5, k:k + 1], xT[:, k, :],
                                                ALU.mult, ALU.add)
            last.then_inc(sem("x_ready"), 1)
            dve.wait_ge(sem("x_ready"), 2)
            norm(2, xT[:, :, :], xT[:, :, :], vec("final1"), None, EPS1)

            def norm2(n, layer, which, t=0):
                src, dst = ((xT[:, :, :], hT[:, :, :]), (cT, hC))[t]
                norm(n, src, dst, mod2[:, layer, 3 * which + 1, :, t], mod2[:, layer, 3 * which, :, t], EPS2)

            def ffn(f, sets, layer, which):
                if f == 0:
                    for n in range(N_MOD):
                        for i in range(4):
                            mod_slot(4 * (6 + N_MOD + n) + i)
                        if n % 3 == 2:
                            for m in range(n - 2, n + 1):
                                modulation(6 + N_MOD + m)
                for n, (c0, nc_) in enumerate(((0, 8), (8, 8), (16, 6))):
                    for t in range(sets):
                        for half in range(2):
                            k = min(4, nc_ - 4 * half)
                            u = U[f"ffn{f}_b{n}"] + 2 * t + half
                            dst = hm[:, t, c0 + 4 * half:c0 + 4 * half + k, :]
                            await_freed(dve, U[f"ffn{f}_a{n}"] + 2 * t + half)
                            await_unit(dve, u)
                            last = dve.tensor_tensor(dst, chunks(u, k), dst, ALU.mult)
                            if (n, t, half) != (2, sets - 1, 1):
                                free(last, u)
                finish(last, u, "ffn_hidden")
                for t in range(sets):
                    last, u = add_to((xT, cT)[t], U[f"ffn{f}_out"] + 2 * t, mod2[:, layer, 3 * which + 2, :, t])
                    if t != sets - 1:
                        free(last, u)
                finish(last, u, "x_ready")

            dve.wait_ge(sem("h_ready"), 3)
            norm2(3, 0, 0)
            norm2(4, 0, 0, 1)
            ffn(0, 2, 0, 0)
            norm2(5, 0, 1)
            norm2(6, 0, 1, 1)
            u = U["pool_out"]
            await_unit(dve, u)
            for g in range(4):
                last = dve.tensor_scalar(cat[:, 4 + g, :], unit(u)[:, g * T:(g + 1) * T],
                                         vec("pool_scale")[:, g:g + 1], None, ALU.mult)
            free(last, u)
            dve.wait_ge(sem("rpb_masked"), 1)

            def na_soft(s):
                blk, pair = NA_STEPS[s]
                u = U[f"na_scores{s}"]
                sc = unit(u).rearrange("p (j k) -> p j k", j=2)
                await_unit(dve, u)
                link(dve.tensor_tensor(sc[:, :, 0:T], sc[:, :, 0:T],
                                       rpb[:, 8 * blk + 2 * pair:8 * blk + 2 * pair + 2, :], ALU.add))
                link(dve.tensor_reduce(stats[:, 0, s, 0:2], sc, AX_X, ALU.max))
                dve.tensor_scalar(stats[:, 1, s, 0:2], stats[:, 0, s, 0:2], -1.0, None, ALU.mult).then_inc(
                    sem("na_max_ready"), 1)

            na_soft(0)
            for s in range(len(NA_STEPS)):
                if s + 1 < len(NA_STEPS):
                    na_soft(s + 1)
                blk, pair = NA_STEPS[s]
                u = U[f"na_out{s}"]
                await_freed(dve, U[f"na_scores{s}"])
                link(dve.reciprocal(stats[:, 2, s, 0:2], stats[:, 2, s, 0:2]))
                await_unit(dve, u)
                free(dve.tensor_tensor(na_o[:, blk, P * pair:P * pair + P].rearrange("p (h d) -> p h d", h=2),
                                       chunks(u, 2, HD), wide(stats[:, 2, s, 0:2], HD), ALU.mult), u)
            finish(*add_to(xT, U["even_out"], mod2[:, 0, 5, :, 0]), "x_ready")
            norm2(7, 0, 2)
            ffn(1, 1, 0, 2)
            norm2(8, 1, 0)
            ffn(2, 1, 1, 0)
            norm2(9, 1, 1)
            dve.wait_ge(sem("conv_edges"), 2)
            for half in range(2):
                u = U["conv2"] + half
                await_freed(dve, U["conv1"] + half)
                await_unit(dve, u)
                free(dve.tensor_tensor(conv_z[:, 4 * half:4 * half + 4, 1:T + 1], chunks(u),
                                       conv_c[:, 4 * half:4 * half + 4, :], ALU.mult), u)
            await_freed(dve, U["conv2"])
            await_freed(dve, U["conv2"] + 1)
            taps = vec("conv_w").rearrange("p (n k) -> p n k", n=3)
            for k in range(DC):
                last = dve.tensor_scalar(conv_y[:, k, :], conv_z[:, k, 0:T], taps[:, 0, k:k + 1], None, ALU.mult)
            link(last)
            for n in (1, 2):
                for k in range(DC):
                    last = dve.scalar_tensor_tensor(conv_y[:, k, :], conv_z[:, k, n:n + T], taps[:, n, k:k + 1],
                                                    conv_y[:, k, :], ALU.mult, ALU.add)
                link(last)
            await_freed(dve, U["conv0"])
            await_freed(dve, U["conv0"] + 1)
            dve.tensor_tensor(conv_y, conv_y, conv_b, ALU.mult).then_inc(sem("conv_ready"), 1)
            finish(*add_to(xT, U["conv_out"], mod2[:, 1, 5, :, 0]), "x_ready")
            norm2(10, 1, 2)
            ffn(3, 1, 1, 2)
            norm(11, xT[:, :, :], hT[:, :, :], vec("final2"), None, EPS2)


def shape_constants():
    q = np.arange(P)
    c = {}
    c["ident"] = np.eye(P, dtype=np.float32)
    c["ones"] = np.ones((P, P), np.float32)
    c["before"] = (q[:, None] < q[None, :]).astype(np.float32)
    c["iota"] = np.tile(np.arange(P, dtype=np.float32), (P, 1))
    col = np.arange(GRID_W)
    start = np.clip(col - KW // 2, 0, GRID_W - KW)
    ok = (col[None, :] >= start[:, None]) & (col[None, :] < start[:, None] + KW)
    c["col_mask"] = np.tile(np.where(ok, 0.0, NEG).astype(np.float32), (2, 1))
    valid = np.zeros((P, 2, 16), np.float32)
    for b in range(TB):
        t = b * P + q
        valid[:, b, :NCMP] = (np.arange(NCMP)[None, :] * 16 + 31) <= t[:, None]
    c["cmp_valid"] = valid.reshape(P, 32)
    c["cmp_bias"] = np.where(valid > 0, 0.0, NEG).astype(np.float32).reshape(P, 32)
    packed = np.concatenate([c[name] for name, _ in CONSTS], axis=1)
    dist = (q[:, None] + P - np.arange(T)[None, :]).astype(np.float32)
    slopes = 2.0 ** -np.arange(1, 9, dtype=np.float32)
    full = np.where(dist[:, None, :] >= 0, -slopes[None, :, None] * dist[:, None, :], NEG)
    near = np.where(dist[:, None, :] < 128, full, NEG)
    band = np.zeros((P, TB, 4, T), np.float32)
    t = np.arange(T)
    for g, w in enumerate((2, 4, 8, 16)):
        lo, hi = np.clip(t - w // 2, 0, T), np.clip(t - w // 2 + w, 0, T)
        m = ((t[:, None] >= lo[None, :]) & (t[:, None] < hi[None, :])) / (hi - lo)[None, :]
        m = (m - np.eye(T)).astype(np.float32)
        band[:, :, g, :] = m.reshape(TB, P, T).transpose(1, 0, 2)
    return packed, full, near, band


def kernel(**inputs):
    import ml_dtypes
    import concourse.bacc as bacc
    from concourse.bass_utils import run_bass_kernel_spmd

    a = {k: np.asarray(v) for k, v in inputs.items()}

    def cols(v):
        v = v.reshape(-1, P)
        return np.ascontiguousarray(v.T)

    def rows(v):
        return np.broadcast_to(v.reshape(1, -1), (P, v.size))

    def pairs_of_heads(w):
        h = w.reshape(w.shape[0], 2, 4, HD)
        return h.transpose(0, 2, 1, 3).reshape(w.shape[0], 512)

    def mixer_columns(w):
        at = np.cumsum([512, 128, 128, 512, 512, 512, 512, 128, 128, 128, 128, 128, 128, 24])
        qa, ka, va, qb, kb, vb, qc, kcm, vcm, ksl, vsl, kwn, vwn, gates, merge = np.split(w, at, axis=1)
        pad = np.zeros((w.shape[0], P - 24), w.dtype)
        return np.concatenate([pairs_of_heads(qa), pairs_of_heads(qc), qb, kb, ka, va, vb, kcm, vcm, ksl, vsl,
                               kwn, vwn, gates, pad, merge], axis=1)

    w2 = a["cmp_w2"][0].reshape(2, 2, P, HD)
    w2 = np.concatenate([w2, w2], axis=3).transpose(2, 0, 1, 3).reshape(P, 4 * P)
    vec = {
        "c": cols(a["c"]), "mod_b": cols(a["mod_b"]), "norm1": cols(a["norm1_g"]), "norm2": cols(a["norm2_g"]),
        "b_in": cols(mixer_columns(a["b_in"])), "final1": cols(a["final_g"]),
        "exp_b1": cols(a["exp_b1"]), "exp_b2": cols(a["exp_b2"]),
        "cmp_pos": cols(a["cmp_pos"]), "cmp_b1": cols(a["cmp_b1"]),
        "cmp_b2k": np.concatenate([a["cmp_b2"][0, 0]] * 2)[:, None], "cmp_b2v": rows(a["cmp_b2"][0, 1]),
        "cmp_w2": w2, "sinks": rows(a["sinks"]), "lambda": rows(a["diff_lambda"]), "subln": rows(a["diff_subln_g"]),
        "router_w": a["router_w"][0].reshape(DC, P, N_EXPERTS).transpose(1, 0, 2).reshape(P, -1),
        "router_b": rows(a["router_b"]),
        "cond2": np.stack([cols(a["c_2"]), cols(a["c_ctx_2"])], axis=2).reshape(P, -1),
        "mod_b2": cols(a["mod_b_2"]), "norm_g2": cols(a["norm_g_2"]),
        "pool_w": a["pool_w_2"][0].transpose(1, 0, 2).reshape(P, -1), "pool_scale": cols(a["pool_scale_2"]),
        "conv_w": cols(a["conv_w_2"]), "final2": cols(a["final_g_2"]),
    }
    packed, full, near, band = shape_constants()
    padded = np.zeros((8, 15, 2 * GRID_W), np.float32)
    padded[:, :, 48:79] = a["na_rpb_2"][0]
    first = GRID_W - 1 - np.arange(GRID_W)
    rpb = np.stack([padded[:, :, f:f + GRID_W] for f in first]).reshape(GRID_W, 8, 15 * GRID_W)
    arrays = {
        "vecs": np.concatenate([vec[name] for name, _ in VECS], axis=1), "consts": packed,
        "xT": np.ascontiguousarray(a["x"][0].T), "ctxT": np.ascontiguousarray(a["ctx_2"][0].T),
        "alibi_full": full.astype(ml_dtypes.bfloat16), "alibi_near": near.astype(ml_dtypes.bfloat16),
        "pool_band": band, "rpb": rpb,
        "mod_w": a["mod_w"], "w_in": mixer_columns(a["w_in"][0])[None], "cmp_w1": a["cmp_w1"][0],
        "w_branch": a["w_branch"][0], "w_out": a["w_out"], "exp_w1": a["exp_w1"][0], "exp_w2": a["exp_w2"][0],
        "mod_w_2": a["mod_w_2"], "ffn_w13": a["ffn_w13_2"].reshape(4, D, 2 * FF),
        "ffn_w2": a["ffn_w2_2"].reshape(4, FF, D), "even_w_in": a["even_w_in_2"], "even_w_out": a["even_w_out_2"],
        "conv_w_in": a["conv_w_in_2"], "conv_w_out": a["conv_w_out_2"],
    }
    nc = bacc.Bacc("TRN2", target_bir_lowering=False, num_devices=1, dynamic_dma_scratch_size=1024)
    ins = {}
    for name, v in arrays.items():
        arrays[name] = v = np.ascontiguousarray(v)
        ins[name] = nc.dram_tensor(f"in_{name}", v.shape, mybir.dt.from_np(v.dtype), kind="ExternalInput").ap()
    out = nc.dram_tensor("out_y", (D, T), F32, kind="ExternalOutput").ap()
    build(nc, ins, out)
    r = run_bass_kernel_spmd(nc, [{f"in_{n}": v for n, v in arrays.items()}], core_ids=[0])
    return np.ascontiguousarray(r.results[0]["out_y"].T)[None]
```

```python
from contextlib import ExitStack

import numpy as np

import concourse.bass as bass
from concourse import mybir

ALU = mybir.AluOpType
ACT = mybir.ActivationFunctionType
F32 = mybir.dt.float32
F32R = mybir.dt.float32r
BF16 = mybir.dt.bfloat16
I32 = mybir.dt.int32
AX_X = mybir.AxisListType.X

P = 128
D = 1024
T = 256
DC = D // P
TB = T // P
EPS1, EPS2 = 1e-5, 1e-6
HD = 64
N_EXPERTS, TOP_K = 32, 4
LIMIT, ALPHA = 7.0, 1.702
NCMP = (T - 32) // 16 + 1
LAM_INIT = 0.8 - 0.6 * 1.0
NEG = -1e30
FF = 2816
FC = FF // P
N_MOD = 9
GRID_W, ROWS = 64, T // 64
KW = 16

Z_QA, Z_QC, Z_QB, Z_KB, Z_KA, Z_VA, Z_VB, Z_KCM, Z_VCM, Z_KSL, Z_VSL, Z_KWN, Z_VWN, Z_GATE, Z_MERGE = (
    0, 4, 8, 12, 16, 17, 18, 22, 23, 24, 25, 26, 27, 28, 29)
Z_ALL = Z_MERGE + 3 * DC
Z_V = [Z_VA, Z_VB, Z_VB + 1, Z_VB + 2, Z_VB + 3, Z_VSL, Z_VWN]
Z_PASSES = [(0, 8), (8, 8), (16, 8), (24, 5)]

RING = 12
SLOT = 2 * D
RING2, HIGHS = 8, 4
FFN_PASSES = ((0, 8), (8, 8), (16, 6))
FFNS = [(0, 0), (0, 1), (1, 0), (2, 0), (3, 0)]

CAP = 96
ROUNDS = -(-T // CAP)
PAIRS = N_EXPERTS // 2

VECS = [
    ("c", DC), ("mod_b", 6 * DC), ("norm1", DC), ("norm2", DC), ("b_in", Z_ALL), ("final1", DC),
    ("exp_b1", N_EXPERTS * 2 * DC), ("exp_b2", N_EXPERTS * DC), ("cmp_pos", 2 * 16), ("cmp_b1", 4),
    ("cmp_b2k", 1), ("cmp_b2v", HD), ("cmp_w2", 4 * P), ("sinks", 8), ("lambda", 4 * HD), ("subln", P),
    ("router_w", DC * N_EXPERTS), ("router_b", N_EXPERTS), ("cond2", 2 * DC), ("mod_b2", 2 * N_MOD * DC),
    ("norm_g2", 2 * 3 * DC), ("pool_w", 4 * P), ("pool_scale", 4), ("conv_w", 3 * DC), ("final2", DC),
]
VEC_AT = {}
_at = 0
for _name, _width in VECS:
    VEC_AT[_name] = (_at, _width)
    _at += _width
VEC_COLS = _at

CONSTS = [("ident", P), ("ones", P), ("before", P), ("iota", P), ("col_mask", GRID_W),
          ("cmp_bias", 2 * 16), ("cmp_valid", 2 * 16)]
CONST_AT = {}
_at = 0
for _name, _width in CONSTS:
    CONST_AT[_name] = (_at, _width)
    _at += _width
CONST_COLS = _at

ATT = [(kind, blk, g) for kind in ("swa", "slc", "win", "diff") for blk in range(TB) for g in range(2)]
NA_STEPS = [(blk, pair) for blk in range(TB) for pair in range(4)]


MODS = [(1, 0, g, 1) for g in range(6)] + [(2, layer, g, 2 if (layer, g) < (0, 5) else 1)
                                           for layer in range(2) for g in range(N_MOD)]
MOD_SUMS = 3
ATT_MOD_SLOTS = [4 * N_MOD * s // len(ATT) for s in range(len(ATT) + 1)]


L1_MODS = 6 + N_MOD

MOE_SLOTS = [("exp_w1", e, k, half) for e in range(2) for half in range(2) for k in range(0, DC, 2)] + \
            [("exp_w2", e, k, 0) for e in range(2) for k in range(0, DC, 2)]
MOE_RELEASE = [("units", 4 + j // 4 + 1) if j % 4 == 3 else ("slots", j // 4 * 3 + j % 4 + 1) for j in range(24)]


def mod_unit(n):
    return f"mod{n}"


def mods_ending(lo, hi):
    return [6 + s // 4 for s in range(lo, hi) if s % 4 == 3]


class Plan:

    def __init__(self):
        self.units, self.n_units = {}, 0
        self.slots, self.stream = {}, []
        self.released = {}
        self.n_slot_signals = 0
        self.mod_at, self.n_mod_slots = [], 0
        self.place, self.landing, self.before = [], [], []
        self.holder, self.times, self.places = {}, {}, RING
        self.split_at, self.split_no = [], {}

    def placed(self):
        while len(self.place) < len(self.stream):
            s = len(self.place)
            self.next = (self.next + 1) % self.places if s else 0
            self.place.append(self.next)
            self.before.append(self.holder.get(self.next))
            self.times[self.next] = self.times.get(self.next, 0) + 1
            self.landing.append(self.times[self.next])
            self.holder[self.next] = s

    def unit(self, name, n=1):
        self.units[name] = self.n_units
        self.n_units += n

    def load(self, name, sources):
        self.slots[name] = len(self.stream)
        self.stream += sources

    def gemm(self, name, tensor, index, k_chunks, col0, cols, n_units, mods_between=0, split=False):
        self.unit(name, n_units)
        self.slots[name] = []
        for k in range(0, k_chunks, 2):
            self.slots[name].append(len(self.stream))
            if k + 2 < k_chunks:
                self.n_slot_signals += 1
                self.released[len(self.stream)] = ("slots", self.n_slot_signals)
            else:
                self.released[len(self.stream)] = ("units", self.n_units)
            if split:
                self.split_no[len(self.stream)] = len(self.split_at)
                self.split_at.append(len(self.stream))
            self.stream.append((tensor, index, k, 2, col0, cols))
            self.mod_slots(min(mods_between, 4 * len(MODS) - self.n_mod_slots))

    def mod_slots(self, n):
        for _ in range(n):
            block_, layer, g, _ = MODS[self.n_mod_slots // 4]
            self.mod_at.append(len(self.stream))
            self.n_mod_slots += 1
            self.released[len(self.stream)] = ("mods", self.n_mod_slots)
            k = 2 * ((self.n_mod_slots - 1) % 4)
            self.stream.append(("mod_w" if block_ == 1 else "mod_w_2", layer, k, 2, g * D, D))


def make_plan():
    p = Plan()
    p.mod_slots(8)
    p.unit(mod_unit(0))
    p.unit(mod_unit(1))
    p.unit("norm0")
    for n, (c0, nc_) in enumerate(Z_PASSES):
        p.gemm(f"z{n}", "w_in", 0, DC, c0 * P, nc_ * P, 2, mods_between=1)
        p.unit(mod_unit(2 + n))
    p.unit("vnat", 2)
    p.load("cmp_w1", [("cmp_w1", kv, 8 * half, 8, 0, 256) for kv in range(2) for half in range(2)])
    p.unit("cmp_hidden")
    for s in range(4):
        p.released[p.slots["cmp_w1"] + s] = ("units", p.n_units)
    p.unit("cmp_kv")
    p.unit("cmp_scores")
    p.unit("cmp_turn", 2)
    p.unit("cmp_out")
    p.unit("scores0")
    for s in range(len(ATT)):
        if s + 1 < len(ATT):
            p.unit(f"scores{s + 1}")
        p.mod_slots(ATT_MOD_SLOTS[s + 1] - ATT_MOD_SLOTS[s])
        p.unit(f"turn{s}")
        p.unit(f"out{s}")
        for n in mods_ending(*ATT_MOD_SLOTS[s:s + 2]):
            p.unit(mod_unit(n))
    p.unit("branch_turn", 3)
    for b in range(3):
        p.gemm(f"merge{b}", "w_in", 0, DC, (Z_MERGE + b * DC) * P, D, 2)
        p.gemm(f"branch{b}", "w_branch", b, 4, 0, D, 2)
    p.gemm("w_out", "w_out", 0, DC, 0, D, 2)
    p.unit("norm1")
    p.unit("h_turn", 2)
    p.unit("logits")
    p.unit("positions")
    while p.n_units % 4:
        p.unit("pad")
        p.n_pad = p.n_units
    p.moe_unit, p.moe_slot, p.moe_signals = p.n_units, len(p.stream), p.n_slot_signals
    p.n_units += 16 * PAIRS
    p.stream += [None] * (24 * PAIRS)
    p.n_slot_signals += 18 * PAIRS
    for j in range(24):
        kind, n = MOE_RELEASE[j]
        base = p.moe_unit + 16 * (PAIRS - 1) if kind == "units" else p.moe_signals + 18 * (PAIRS - 1)
        p.released[len(p.stream) - 24 + j] = (kind, base + n)
    p.placed()
    p.places = RING2
    p.next = RING2 - 1
    p.unit("norm2")
    p.unit("norm3")
    for e, (f, _) in enumerate(FFNS):
        if e >= 2:
            p.unit(f"norm{(7, 8, 10)[e - 2]}")
        for ab in range(2):
            for n, (c0, nc_) in enumerate(FFN_PASSES):
                p.gemm(f"ffn{e}_{'ab'[ab]}{n}", "ffn_w13", f, DC, ab * FF + c0 * P, nc_ * P, 2,
                       mods_between=1 if e < 2 else 0, split=True)
                if e == 0 or (e, ab, n) == (1, 0, 0):
                    p.unit(mod_unit(L1_MODS + (3 * ab + n if e == 0 else N_MOD - 1)))
        if e < 2:
            p.unit(f"norm{4 + e}")
        p.gemm(f"ffn{e}_out", "ffn_w2", f, FC, 0, D, 2, mods_between=1 if e < 2 else 0, split=True)
        if e == 0:
            p.unit(mod_unit(L1_MODS + 6))
            p.unit(mod_unit(L1_MODS + 7))
        if e == 1:
            p.gemm("even_qk", "even_w_in", 0, DC, 0, D, 2, split=True)
            p.gemm("even_vu", "even_w_in", 0, DC, D, D, 2, split=True)
            p.unit("norm6")
            p.gemm("even_ctx", "even_w_in", 0, DC, 512, D, 2, split=True)
            p.unit("na_vturn", 2)
            p.unit("pool_map")
            p.unit("pool_out")
            p.unit("na_scores0")
            for s in range(len(NA_STEPS)):
                if s + 1 < len(NA_STEPS):
                    p.unit(f"na_scores{s + 1}")
                p.unit(f"na_turn{s}")
                p.unit(f"na_out{s}")
            p.unit("na_oturn")
            p.gemm("even_out", "even_w_out", 0, DC, 0, D, 2)
        if e == 3:
            p.unit("norm9")
            for n in range(3):
                p.gemm(f"conv{n}", "conv_w_in", 0, DC, n * D, D, 2, split=True)
            p.gemm("conv_out", "conv_w_out", 0, DC, 0, D, 2)
    p.unit("norm11")
    p.placed()
    return p


def mod_buffers():
    at, holder, buffers, earlier = 0, [None] * MOD_SUMS, [], []
    for n, (_, _, _, conds) in enumerate(MODS):
        mine = [(at + c) % MOD_SUMS for c in range(conds)]
        buffers.append(mine)
        earlier.append([holder[b] for b in mine])
        for b in mine:
            holder[b] = n
        at += conds
    return buffers, earlier


MOD_BUFFERS, MOD_BUFFER_BEFORE = mod_buffers()
PLAN = make_plan()
U = PLAN.units
N_NORMS = 12


class Steps:

    def __init__(self, eng, sem):
        self.eng, self.sem, self.n, self.per_turn, self.turn, self.first = eng, sem, 0, 0, None, 0

    def done(self, ins):
        ins.then_inc(self.sem, 1)
        self.n += 1

    def settle(self):
        self.eng.wait_ge(self.sem, self.n if self.turn is None else self.turn * self.per_turn + self.n)

    def link(self, ins):
        self.done(ins)
        self.settle()

    def enter(self, turn, per_turn):
        self.turn, self.per_turn, self.first = turn, per_turn, self.n

    def leave(self, turns):
        assert self.n - self.first == self.per_turn, (self.n - self.first, self.per_turn)
        self.n, self.turn = self.first + turns * self.per_turn, None


def build(nc, ins, out):
    with ExitStack() as ctx:
        def sb(name, shape, dt=F32):
            return ctx.enter_context(nc.sbuf_tensor(name, shape, dt))

        sems = {}

        def sem(name):
            if name not in sems:
                sems[name] = ctx.enter_context(nc.semaphore(name))
            return sems[name]

        def sb_at(name, shape, dt, offset):
            return nc.alloc_sbuf_tensor_at(name, shape, dt, offset=offset)

        ring_at = -(-nc.sbuf_base // 32) * 32
        ring = sb("ring", [P, RING, SLOT])
        vecs = sb("vecs", [P, VEC_COLS])
        consts = sb("consts", [P, CONST_COLS])
        xT = sb("xT", [P, DC, T])
        hT_at = -(-nc.sbuf_base // 32) * 32
        hT = sb("hT", [P, DC, T])
        rstd = sb("rstd", [P, 2, T])
        cs = sb("cs", [P, DC])
        cs2 = sb("cs2", [P, DC, 2])
        mod1 = sb("mod1", [P, 6, DC])
        mod2 = sb("mod2", [P, 2, N_MOD, DC, 2])
        mod_sums = sb("mod_sums", [P, MOD_SUMS, D])
        stats = sb("stats", [P, 4, len(ATT), 4])
        small = sb("small", [P, 512])
        count_max = sb("count_max", [P, 1], I32)
        ARENA = 19456
        arena_at = -(-nc.sbuf_base // 32) * 32
        arena = sb("arena", [P, ARENA])
        psum = ctx.enter_context(nc.psum_tensor("psum", [P, 4, 1024], F32))

        def vec(name, *dims):
            at, width = VEC_AT[name]
            v = vecs[:, at:at + width]
            return v

        def const(name):
            at, width = CONST_AT[name]
            return consts[:, at:at + width]

        ident, ones, before = const("ident"), const("ones"), const("before")

        def area(at, *dims):
            n = int(np.prod(dims))
            assert at + n <= ARENA, (at, n)
            v = arena[:, at:at + n]
            if len(dims) == 2:
                v = v.rearrange("p (a b) -> p a b", a=dims[0])
            if len(dims) == 3:
                v = v.rearrange("p (a b c) -> p a b c", a=dims[0], b=dims[1])
            return v

        zT = area(0, 29, T)
        vnat = area(7424, TB, 7 * P)
        alibi_full = area(9216, 1024).bitcast(BF16).rearrange("p (h k) -> p h k", h=8)
        alibi_near = area(10240, 1024).bitcast(BF16).rearrange("p (h k) -> p h k", h=8)
        o_nat = area(13312, TB, 3, 512)
        probs = area(16384, 2, 1024)
        probsT = area(18432, 1024)
        blocks = area(13312, 2, 16 * 32)
        cmpP = area(14336, TB * 8, 16)
        cmpPT = area(16384, 2048)
        gm = area(0, 3 * DC, T)
        oT = area(9216, 12, T)
        merged = area(13312, DC, T)
        merge_tmp = area(15360, 4, T)
        cT = area(0, DC, T)
        acc = area(2048, DC, T)
        h_nat = area(4096, TB, D)
        moe = {}
        at = 6144
        for name, n in (("xg", DC * CAP), ("hid", DC * CAP), ("yN", D), ("selT", T),
                        ("sel", TB * CAP), ("selG", TB * CAP)):
            for e in range(2):
                moe[name, e] = (at, n)
                at += n
        for name in ("g", "u", "sig"):
            moe[name] = (at, DC * CAP)
            at += DC * CAP
        assert at <= ARENA

        def moe_buf(key, a=None):
            at_, n = moe[key]
            return area(at_, n) if a is None else area(at_, a, n // a)

        hm = area(4096, FC, T)
        rpb = area(15360, TB * 8, T)
        z2q, z2k, z2v, z2u = area(4096, 4, T), area(5120, 4, 2 * T), area(7168, 4, 2 * T), area(9216, 4, T)
        vnat2 = area(10240, 4, 512)
        pool_band = area(12288, TB, 4, T)
        cat = area(7168, DC, T)
        na_probs = area(0, 2, 512)
        na_probsT = area(1024, 1024)
        pool_mapped = area(2048, TB, 512)
        na_o = area(3072, TB, 512)
        conv_b, conv_c, conv_y = area(4096, DC, T), area(6144, DC, T), area(8192, DC, T)
        conv_z = area(10240, DC, T + 2)

        w_low = sb_at("w_low", [P, RING2, SLOT], F32R, ring_at)
        w_high = sb_at("w_high", [P, HIGHS, SLOT], F32R, ring_at + 4 * RING2 * SLOT)
        h_low = sb_at("h_low", [P, DC, T], F32R, hT_at)
        h_high = sb_at("h_high", [P, DC, T], F32R, arena_at + 4 * 2048)
        m_low = sb_at("m_low", [P, FC, T], F32R, arena_at + 4 * 4096)
        m_high = sb_at("m_high", [P, FC, T], F32R, arena_at + 4 * (4096 + FC * T))

        landed = [sem(f"slot_landed{i}") for i in range(RING)]
        slots_used = sem("slots_used")
        psum_full = sem("psum_full")
        psum_free = [sem(f"psum_free{i}") for i in range(4)]
        dve_steps = sem("dve_steps")

        def unit(u):
            return psum[:, u % 4, :]

        def open_unit(pe, u, turn=None, per_turn=0, free=None):
            n = u // 4
            if turn is not None:
                pe.wait_ge((free or psum_free)[u % 4], turn * (per_turn // 4) + n)
            elif n:
                pe.wait_ge((free or psum_free)[u % 4], n)

        def await_unit(eng, u, turn=None, per_turn=0, full=None):
            eng.wait_ge(full or psum_full, u + 1 if turn is None else turn * per_turn + (u + 1))

        def await_freed(eng, u, turn=None, per_turn=0, free=None):
            n = u // 4 + 1
            eng.wait_ge((free or psum_free)[u % 4], n if turn is None else turn * (per_turn // 4) + n)

        def await_slot(pe, s):
            pe.wait_ge(landed[PLAN.place[s]], 16 * PLAN.landing[s])

        def await_release(eng, s):
            kind, n = PLAN.released[s]
            eng.wait_ge({"slots": slots_used, "units": psum_full, "mods": sem("mod_slots_used")}[kind], n)

        def slot_ap(s, rows=2, cols=D):
            return ring[:, PLAN.place[s], 0:rows * cols].rearrange("p (k n) -> p k n", k=rows)

        def high_ap(m, cols):
            return w_high[:, m % HIGHS, 0:2 * cols].rearrange("p (k n) -> p k n", k=2)

        def low_ap(s, cols):
            return w_low[:, PLAN.place[s], 0:2 * cols].rearrange("p (k n) -> p k n", k=2)

        def ahead_of(name):
            last = PLAN.slots[name][-1]
            later = [s for s in PLAN.split_at if s > last][:HIGHS]
            return (later[-1] if later else last) + 1

        def source(entry):
            name, index, k0, rows, c0, cols = entry
            t = ins[name][index]
            return t.rearrange("(k p) n -> p k n", p=P)[:, k0:k0 + rows, c0:c0 + cols]

        moe_end = PLAN.moe_slot + 24 * PAIRS
        block = ctx.enter_context(nc.Block())

        def load_pairs(sp, turn, base_slot, signals, units, full, used, land, land_base, first_waits):
            for j, (name, e, k, half) in enumerate(MOE_SLOTS):
                if j >= RING:
                    kind, n = MOE_RELEASE[j - RING]
                    if kind == "units":
                        sp.wait_ge(full, turn * 16 + (units + n))
                    else:
                        sp.wait_ge(used, turn * 18 + (signals + n))
                else:
                    first_waits(j)
                w = ins[name][turn * 2 + e] if name == "exp_w1" else ins[name][turn * 2 + e]
                src = w.rearrange("(k p) n -> p k n", p=P)[:, k:k + 2, half * D:(half + 1) * D]
                sp.dma_start(slot_ap(base_slot + j), src).then_inc(land[(base_slot + j) % RING], 16)

        def rounds_loop(eng, body):
            with eng.Fori(0, ROUNDS - 1) as r:
                with eng.Fori(0, PAIRS) as i:
                    body(eng, i, r * PAIRS + i)

        full_x, used_x = sem("psum_full_x"), sem("slots_used_x")
        free_x = [sem(f"psum_free_x{i}") for i in range(4)]
        landed_x = [sem(f"slot_landed_x{i}") for i in range(RING)]

        def many(eng):
            eng.wait_ge(sem("count_ready"), 1)
            return eng.value_load(count_max[0:1, 0:1], min_val=0, max_val=T)

        @block.sync
        def _(sp):
            def stream(s0, s1):
                for s in range(s0, s1):
                    if PLAN.before[s] is not None:
                        await_release(sp, PLAN.before[s])
                    entry = PLAN.stream[s]
                    sp.dma_start(slot_ap(s, entry[3], entry[5]), source(entry)).then_inc(landed[PLAN.place[s]], 16)

            stream(0, PLAN.moe_slot)

            def ahead(j):
                await_release(sp, PLAN.moe_slot + j - RING)

            load_pairs(sp, 0, PLAN.moe_slot, PLAN.moe_signals, PLAN.moe_unit, psum_full, slots_used, landed, 0, ahead)
            with sp.Fori(1, PAIRS) as i:
                def before_turn(j, i=i):
                    kind, n = MOE_RELEASE[j + RING]
                    if kind == "units":
                        sp.wait_ge(psum_full, i * 16 + (PLAN.moe_unit + n - 16))
                    else:
                        sp.wait_ge(slots_used, i * 18 + (PLAN.moe_signals + n - 18))
                load_pairs(sp, i, PLAN.moe_slot, PLAN.moe_signals, PLAN.moe_unit, psum_full, slots_used, landed, 0,
                           before_turn)
            with sp.If(many(sp) > CAP):
                sp.wait_ge(psum_full, PLAN.moe_unit + 16 * PAIRS)

                def pair(sp, i, turn):
                    def before_turn(j):
                        kind, n = MOE_RELEASE[j + RING]
                        if kind == "units":
                            sp.wait_ge(full_x, turn * 16 + n)
                        else:
                            sp.wait_ge(used_x, turn * 18 + n)
                    for j, (name, e, k, half) in enumerate(MOE_SLOTS):
                        if j >= RING:
                            kind, n = MOE_RELEASE[j - RING]
                            if kind == "units":
                                sp.wait_ge(full_x, turn * 16 + (16 + n))
                            else:
                                sp.wait_ge(used_x, turn * 18 + (18 + n))
                        else:
                            before_turn(j)
                        src = ins[name][i * 2 + e].rearrange("(k p) n -> p k n", p=P)[:, k:k + 2, half * D:(half + 1) * D]
                        sp.dma_start(slot_ap(PLAN.moe_slot + j), src).then_inc(
                            landed_x[(PLAN.moe_slot + j) % RING], 16)
                rounds_loop(sp, pair)
                sp.wait_ge(full_x, 16 + 16 * PAIRS * (ROUNDS - 1))
            stream(moe_end, len(PLAN.stream))
            sp.wait_ge(sem("h_ready"), N_NORMS)
            sp.dma_start(out.rearrange("(k p) t -> p k t", p=P), hT[:, :, :]).then_inc(sem("stored"), 16)
            sp.wait_ge(sem("stored"), 16)

        @block.gpsimd
        def _(pool):
            pool.wait_ge(sem("rpb_landed"), 16 * ROWS)
            mask = const("col_mask")[:, None, :].broadcast_to([P, TB * 8 * ROWS, GRID_W])
            view = area(15360, TB * 8 * ROWS, GRID_W)
            pool.tensor_tensor(view, view, mask, ALU.add).then_inc(sem("rpb_masked"), 1)
            pool.wait_ge(sem("x_ready"), 7)
            pool.memset(conv_z[:, :, 0:1], 0.0).then_inc(sem("conv_edges"), 1)
            pool.memset(conv_z[:, :, T + 1:T + 2], 0.0).then_inc(sem("conv_edges"), 1)

        @block.scalar
        def _(act):
            act.dma_start(vecs[:, :], ins["vecs"]).then_inc(sem("vecs_landed"), 16)
            act.dma_start(consts[:, :], ins["consts"]).then_inc(sem("consts_landed"), 16)
            act.dma_start(xT[:, :, :], ins["xT"].rearrange("(k p) t -> p k t", p=P)).then_inc(sem("x_landed"), 16)
            act.dma_start(alibi_full, ins["alibi_full"]).then_inc(sem("alibi_landed"), 16)
            act.dma_start(alibi_near, ins["alibi_near"]).then_inc(sem("alibi_landed"), 16)

            act.wait_ge(sem("vecs_landed"), 16)
            act.activation(cs[:, :], vec("c"), ACT.Silu).then_inc(sem("cond_ready"), 1)
            act.activation(cs2[:, :, :], vec("cond2").rearrange("p (k s) -> p k s", s=2), ACT.Silu).then_inc(
                sem("cond_ready"), 1)

            act.wait_ge(sem("lambda_dots"), 1)
            act.activation(small[:, 412:414], small[:, 410:412], ACT.Exp).then_inc(sem("lambda_exp"), 1)

            def norm(n, src, squares):
                act.activation(squares, src, ACT.Square).then_inc(sem("squares_ready"), 1)
                await_freed(act, U[f"norm{n}"])
                act.activation(rstd[:, 1, :], rstd[:, 0, :], ACT.Sqrt).then_inc(sem("root_ready"), 1)

            act.wait_ge(sem("x_landed"), 16)
            norm(0, xT[:, :, :], hT[:, :, :])

            for b in range(TB):
                u = U["vnat"] + b
                await_unit(act, u)
                act.activation(vnat[:, b, :], unit(u)[:, 0:7 * P], ACT.Copy)
                act.activation(small[:, 24 * b:24 * b + 24], unit(u)[:, 7 * P:7 * P + 24],
                               ACT.Sigmoid).then_inc(psum_free[u % 4], 1)

            hidden = small[:, 64:192].rearrange("p (m f c) -> p m f c", m=2, f=2)
            cmp_bias = small[:, 192:196]
            act.wait_ge(sem("cmp_bias_ready"), 1)
            for m in range(2):
                for f in range(2):
                    last = act.activation(hidden[:, m, f, 0:2 * NCMP],
                                          unit(U["cmp_hidden"])[:, (2 * m + f) * 32:(2 * m + f) * 32 + 2 * NCMP],
                                          ACT.Gelu_apprx_tanh, bias=cmp_bias[:, 2 * m + f:2 * m + f + 1])
            last.then_inc(psum_free[U["cmp_hidden"] % 4], 1)
            act.wait_ge(sem("cmp_shifted"), 1)
            act.activation(cmpP[:, :, 0:NCMP], cmpP[:, :, 0:NCMP], ACT.Exp).then_inc(sem("cmp_exp"), 1)
            for n in range(2):
                u = U["cmp_turn"] + n
                await_unit(act, u)
                act.activation(cmpPT[0:NCMP, 1024 * n:1024 * n + 1024], unit(u)[0:NCMP, :], ACT.Copy).then_inc(
                    psum_free[u % 4], 1)
            await_unit(act, U["cmp_out"])

            def exps(s):
                kind, blk, g = ATT[s]
                kw = P * (blk + 1)
                u = U[f"scores{s}"]
                act.wait_ge(sem("row_max_ready"), s + 1)
                for j in range(4):
                    src = unit(u)[:, j * T:j * T + kw]
                    last = act.activation(probs[:, s % 2, j * T:j * T + kw], src, ACT.Exp,
                                          bias=stats[:, 1, s, j:j + 1], accum_out=stats[:, 2, s, j:j + 1])
                last.then_inc(psum_free[u % 4], 1)
                if kind == "swa":
                    act.activation(stats[:, 3, s, :], stats[:, 3, s, :], ACT.Exp).then_inc(sem("sink_exp"), 1)

            def turned(s):
                kind, blk, g = ATT[s]
                u = U[f"turn{s}"]
                n = 4 * (blk + 1) * P
                await_unit(act, u)
                act.activation(probsT[:, 0:n], unit(u)[:, 0:n], ACT.Copy).then_inc(psum_free[u % 4], 1)

            exps(0)
            for s in range(len(ATT)):
                if s + 1 < len(ATT):
                    exps(s + 1)
                turned(s)

            act.wait_ge(sem("subln_mean"), 1)
            act.activation(small[:, 400:408], small[:, 400:408], ACT.Sqrt).then_inc(sem("subln_root"), 1)

            for b in range(3):
                u = U["branch_turn"] + b
                await_unit(act, u)
                act.activation(oT[:, 4 * b:4 * b + 4, :], unit(u).rearrange("p (c t) -> p c t", c=4),
                               ACT.Copy).then_inc(psum_free[u % 4], 1)
            for b in range(3):
                for n in range(DC):
                    u = U[f"merge{b}"] + n // 4
                    z = Z_MERGE + b * DC + n
                    await_unit(act, u)
                    last = act.activation(gm[:, b * DC + n, :], unit(u)[:, (n % 4) * T:(n % 4 + 1) * T],
                                          ACT.Sigmoid, bias=vec("b_in")[:, z:z + 1])
                    if n % 4 == 3:
                        last.then_inc(psum_free[u % 4], 1)

            act.wait_ge(sem("x_ready"), 1)
            act.dma_start(cT, ins["ctxT"].rearrange("(k p) t -> p k t", p=P)).then_inc(sem("ctx_landed"), 16)
            for r in range(ROWS):
                half, blk = r % 2, r // 2
                act.dma_start(rpb[64 * half:64 * half + 64, 8 * blk:8 * blk + 8, :],
                              ins["rpb"][:, :, (7 - r) * GRID_W:(7 - r + ROWS) * GRID_W]).then_inc(
                    sem("rpb_landed"), 16)
            norm(1, xT[:, :, :], hT[:, :, :])

            for n in range(2):
                u = U["h_turn"] + n
                await_unit(act, u)
                act.activation(h_nat[:, n, :], unit(u)[:, :], ACT.Copy).then_inc(psum_free[u % 4], 1)
            route = small[:, 0:448]
            for b in range(TB):
                act.wait_ge(sem("top_ready"), b + 1)
                act.activation(route[:, 128 + 32 * b:160 + 32 * b], route[:, 36 * b:36 * b + 32], ACT.Exp,
                               bias=route[:, 88 + b:89 + b]).then_inc(sem("route_exp"), 1)

            def experts(turn, u0, full, free, x):
                def un(k):
                    return unit(u0 + k)

                def ready(k):
                    await_unit(act, u0 + k, turn, 16, full)
                for e in range(2):
                    ready(e)
                    act.activation(moe_buf(("xg", e), DC), un(e).rearrange("p (k c) -> p k c", k=DC)[:, :, 0:CAP],
                                   ACT.Copy).then_inc(free[(u0 + e) % 4], 1)
                for e in range(2):
                    ready(2 + e)
                    act.activation(moe_buf(("selT", e))[0:CAP, :], un(2 + e)[0:CAP, 0:T], ACT.Copy).then_inc(
                        free[(u0 + 2 + e) % 4], 1)
                for e in range(2):
                    act.wait_ge(sem("gate_clamped" + x), turn * 2 + (e + 1))
                    act.activation(moe_buf("sig"), moe_buf("g"), ACT.Sigmoid, scale=ALPHA).then_inc(
                        sem("gate_sigmoid" + x), 1)
                for e in range(2):
                    ready(10 + e)
                    act.activation(moe_buf(("yN", e))[0:CAP, :], un(10 + e)[0:CAP, :], ACT.Copy).then_inc(
                        free[(u0 + 10 + e) % 4], 1)

            with act.Fori(0, PAIRS) as i:
                experts(i, PLAN.moe_unit, psum_full, psum_free, "")
            with act.If(many(act) > CAP):
                rounds_loop(act, lambda eng, i, turn: experts(turn, 16, full_x, free_x, "_x"))

            act.wait_ge(sem("x_ready"), 2)
            norm(2, xT[:, :, :], hT[:, :, :])

            highs = [0]

            def high_parts(until):
                while highs[0] < len(PLAN.split_at) and PLAN.split_at[highs[0]] < until:
                    m = highs[0]
                    s = PLAN.split_at[m]
                    cols = PLAN.stream[s][5]
                    if m < HIGHS:
                        await_release(act, max(q for q in range(moe_end) if PLAN.place[q] == RING2 + m))
                    else:
                        await_release(act, PLAN.split_at[m - HIGHS])
                    await_slot(act, s)
                    act.activation(high_ap(m, cols), slot_ap(s, 2, cols), ACT.Copy).then_inc(sem("w_high_ready"), 1)
                    highs[0] += 1

            def split_h(n):
                act.wait_ge(sem("h_whole"), n - 2)
                act.activation(h_high[:, :, :], hT[:, :, :], ACT.Copy).then_inc(sem("h_high_ready"), 1)

            def ffn(e, before_out=None):
                for n, (c0, nc_) in enumerate(FFN_PASSES):
                    name = f"ffn{e}_a{n}"
                    high_parts(ahead_of(name))
                    for half in range(2):
                        u = U[name] + half
                        k = min(4, nc_ - 4 * half)
                        await_unit(act, u)
                        act.activation(hm[:, c0 + 4 * half:c0 + 4 * half + k, :],
                                       unit(u)[:, 0:k * T].rearrange("p (c t) -> p c t", c=k),
                                       ACT.Silu).then_inc(psum_free[u % 4], 1)
                for n, (c0, nc_) in enumerate(FFN_PASSES):
                    name = f"ffn{e}_b{n}"
                    high_parts(ahead_of(name))
                    for half in range(2):
                        k = min(4, nc_ - 4 * half)
                        c = c0 + 4 * half
                        await_freed(act, U[name] + half)
                        act.activation(m_high[:, c:c + k, :], hm[:, c:c + k, :], ACT.Copy).then_inc(
                            sem("m_high_ready"), 1)
                if before_out:
                    before_out()
                high_parts(ahead_of(f"ffn{e}_out"))

            high_parts(PLAN.split_at[HIGHS])
            act.wait_ge(sem("h_ready"), 3)
            norm(3, xT[:, :, :], hT[:, :, :])
            split_h(3)

            def norm_ctx():
                act.wait_ge(sem("ctx_landed"), 16)
                norm(4, cT, hT[:, :, :])
                split_h(4)

            def norm_tokens():
                act.wait_ge(sem("x_ready"), 3)
                norm(5, xT[:, :, :], hT[:, :, :])
                split_h(5)

            ffn(0, norm_ctx)
            ffn(1, norm_tokens)
            def projected(name, *parts):
                high_parts(ahead_of(name))
                for half, (dst, scale) in enumerate(parts):
                    u = U[name] + half
                    await_unit(act, u)
                    act.activation(dst, unit(u).rearrange("p (c t) -> p c t", c=4), ACT.Copy, scale=scale).then_inc(
                        psum_free[u % 4], 1)

            projected("even_qk", (z2q, HD ** -0.5), (z2k[:, :, 0:T], 1.0))
            projected("even_vu", (z2v[:, :, 0:T], 1.0), (z2u, 1.0))
            act.wait_ge(sem("x_ready"), 4)
            act.dma_start(pool_band, ins["pool_band"]).then_inc(sem("band_landed"), 16)
            norm(6, cT, hT[:, :, :])
            split_h(6)
            projected("even_ctx", (z2k[:, :, T:2 * T], 1.0), (z2v[:, :, T:2 * T], 1.0))
            for n in range(2):
                u = U["na_vturn"] + n
                await_unit(act, u)
                act.activation(vnat2[:, 2 * n:2 * n + 2, :], unit(u).rearrange("p (b c) -> p b c", b=2),
                               ACT.Copy).then_inc(psum_free[u % 4], 1)
            u = U["pool_map"]
            await_unit(act, u)
            act.activation(pool_mapped, unit(u).rearrange("p (b c) -> p b c", b=2), ACT.Copy).then_inc(
                psum_free[u % 4], 1)

            def na_exps(s):
                u = U[f"na_scores{s}"]
                act.wait_ge(sem("na_max_ready"), s + 1)
                if s >= 1:
                    await_unit(act, U[f"na_turn{s - 1}"])
                for j in range(2):
                    last = act.activation(na_probs[:, j, :], unit(u)[:, 512 * j:512 * j + 512], ACT.Exp,
                                          bias=stats[:, 1, s, j:j + 1], accum_out=stats[:, 2, s, j:j + 1])
                last.then_inc(psum_free[u % 4], 1)

            def na_turned(s):
                u = U[f"na_turn{s}"]
                await_unit(act, u)
                act.activation(na_probsT, unit(u), ACT.Copy).then_inc(psum_free[u % 4], 1)

            na_exps(0)
            for s in range(len(NA_STEPS)):
                na_turned(s)
                if s + 1 < len(NA_STEPS):
                    na_exps(s + 1)
            u = U["na_oturn"]
            await_unit(act, u)
            act.activation(cat[:, 0:4, :], unit(u).rearrange("p (c t) -> p c t", c=4), ACT.Copy).then_inc(
                psum_free[u % 4], 1)
            for n, e in ((7, 2), (8, 3)):
                act.wait_ge(sem("x_ready"), n - 2)
                norm(n, xT[:, :, :], hT[:, :, :])
                split_h(n)
                ffn(e)
            act.wait_ge(sem("x_ready"), 7)
            norm(9, xT[:, :, :], hT[:, :, :])
            split_h(9)
            for n, dst in enumerate((conv_b, conv_c)):
                projected(f"conv{n}", (dst[:, 0:4, :], 1.0), (dst[:, 4:8, :], 1.0))
            high_parts(ahead_of("conv2"))
            act.wait_ge(sem("x_ready"), 8)
            norm(10, xT[:, :, :], hT[:, :, :])
            split_h(10)
            ffn(4)
            act.wait_ge(sem("x_ready"), 9)
            norm(11, xT[:, :, :], hT[:, :, :])

        @block.tensor
        def _(pe):
            def gemm(name, k_chunks, n_chunks, operands):
                slots, u0 = PLAN.slots[name], U[name]
                n_units = sum(-(-n // 4) for _, _, n in operands)
                for u in range(n_units):
                    open_unit(pe, u0 + u)
                for k in range(k_chunks):
                    s = slots[k // 2]
                    if k % 2 == 0:
                        await_slot(pe, s)
                    w = slot_ap(s, 2, n_chunks * P)
                    u = u0
                    for rhs, c0, n in operands:
                        for j in range(n):
                            mm = pe.matmul(unit(u + j // 4)[:, (j % 4) * T:(j % 4 + 1) * T],
                                           w[:, k % 2, (c0 + j) * P:(c0 + j + 1) * P], rhs(k),
                                           start=(k == 0 and j % 2 == 0), stop=(k == k_chunks - 1),
                                           skip_group_check=True)
                            if k == k_chunks - 1 and (j % 4 == 3 or j == n - 1):
                                mm.then_inc(psum_full, 1)
                        u += -(-n // 4)
                    if k % 2 == 1 and k != k_chunks - 1:
                        mm.then_inc(slots_used, 1)

            def split_gemm(name, k_chunks, n_chunks, high, low, parts_ready=None):
                slots, u0 = PLAN.slots[name], U[name]
                for half in range(2):
                    open_unit(pe, u0 + half)
                for k in range(k_chunks):
                    s = slots[k // 2]
                    if k % 2 == 0:
                        pe.wait_ge(sem("w_split"), PLAN.split_no[s] + 1)
                    if parts_ready and k % 4 == 0:
                        parts_ready(k // 4)
                    wh, wl = high_ap(PLAN.split_no[s], n_chunks * P), low_ap(s, n_chunks * P)
                    for j in range(n_chunks):
                        dst = unit(u0 + j // 4)[:, (j % 4) * T:(j % 4 + 1) * T]
                        cols = slice(j * P, (j + 1) * P)
                        first, last = k == 0 and j % 2 == 0, k == k_chunks - 1
                        pe.matmul(dst, wh[:, k % 2, cols], high[:, k, :], start=first, stop=False,
                                  skip_group_check=True)
                        pe.matmul(dst, wh[:, k % 2, cols], low[:, k, :], start=False, stop=False,
                                  skip_group_check=True)
                        mm = pe.matmul(dst, wl[:, k % 2, cols], high[:, k, :], start=False, stop=last,
                                       skip_group_check=True)
                        if last and j in (3, n_chunks - 1):
                            mm.then_inc(psum_full, 1)
                    if k % 2 == 1 and k != k_chunks - 1:
                        mm.then_inc(slots_used, 1)

            def mod_sum(n):
                conds = MODS[n][3]
                u = U[mod_unit(n)]
                pe.wait_ge(sem("mod_partials"), n + 1)
                open_unit(pe, u)
                for c in range(conds):
                    for j in range(DC):
                        at = j * conds + c
                        mm = pe.matmul(unit(u)[:, at:at + 1], mod_sums[:, MOD_BUFFERS[n][c], j * P:(j + 1) * P],
                                       ones[:, 0:1], start=True, stop=True)
                mm.then_inc(psum_full, 1)

            def norm(n, squares):
                pe.wait_ge(sem("squares_ready"), n + 1)
                u = U[f"norm{n}"]
                open_unit(pe, u)
                for k in range(DC):
                    mm = pe.matmul(unit(u)[:, 0:T], ones, squares[:, k, :], start=(k == 0), stop=(k == DC - 1))
                mm.then_inc(psum_full, 1)

            def h_rhs(k):
                return hT[:, k, :]

            pe.wait_ge(sem("consts_landed"), 16)
            mod_sum(0)
            mod_sum(1)
            norm(0, hT)
            pe.wait_ge(sem("h_ready"), 1)
            for n, (c0, nc_) in enumerate(Z_PASSES):
                gemm(f"z{n}", DC, nc_, [(h_rhs, 0, nc_)])
                mod_sum(2 + n)
            pe.wait_ge(sem("z_ready"), len(Z_PASSES))
            for b in range(TB):
                u = U["vnat"] + b
                open_unit(pe, u)
                for n, z in enumerate(Z_V + [Z_GATE]):
                    mm = pe.transpose(unit(u)[:, n * P:(n + 1) * P], zT[:, z, b * P:(b + 1) * P], ident)
                mm.then_inc(psum_full, 1)
            pe.wait_ge(sem("blocks_ready"), 1)
            u = U["cmp_hidden"]
            open_unit(pe, u)
            for m in range(2):
                for half in range(2):
                    await_slot(pe, PLAN.slots["cmp_w1"] + 2 * m + half)
                for f in range(2):
                    for j in range(16):
                        w = slot_ap(PLAN.slots["cmp_w1"] + 2 * m + j // 8, 8, 256)
                        mm = pe.matmul(unit(u)[:, (2 * m + f) * 32:(2 * m + f) * 32 + 31],
                                       w[:, j % 8, f * P:(f + 1) * P],
                                       blocks[:, m, j * 32:j * 32 + 31], start=(j == 0), stop=(j == 15))
            mm.then_inc(psum_full, 1)
            hidden = small[:, 64:192].rearrange("p (m f c) -> p m f c", m=2, f=2)
            w2 = vec("cmp_w2").rearrange("p (m f c) -> p m f c", m=2, f=2)
            await_freed(pe, U["cmp_hidden"])
            u = U["cmp_kv"]
            open_unit(pe, u)
            for f in range(2):
                pe.matmul(unit(u)[:, 0:2 * NCMP], w2[:, 0, f, :], hidden[:, 0, f, 0:2 * NCMP],
                          start=(f == 0), stop=(f == 1))
            for g in range(2):
                for f in range(2):
                    mm = pe.matmul(unit(u)[0:NCMP, 512 + g * HD:512 + (g + 1) * HD],
                                   hidden[:, 1, f, g * NCMP:(g + 1) * NCMP], w2[:, 1, f, 0:HD],
                                   start=(f == 0), stop=(f == 1))
            mm.then_inc(psum_full, 1)
            kcT, vc = small[:, 200:230], small[:, 232:360]
            await_freed(pe, U["cmp_kv"])
            u = U["cmp_scores"]
            open_unit(pe, u)
            for b in range(TB):
                for g in range(2):
                    rows = slice(64 * g, 64 * g + 64)
                    for j in range(4):
                        at = 512 * g + (b * 4 + j) * 16
                        mm = pe.matmul(unit(u)[:, at:at + NCMP], zT[rows, Z_QC + j, b * P:(b + 1) * P],
                                       kcT[rows, g * NCMP:(g + 1) * NCMP], start=True, stop=True)
            mm.then_inc(psum_full, 1)
            pe.wait_ge(sem("cmp_probs"), 1)
            for b in range(TB):
                u = U["cmp_turn"] + b
                open_unit(pe, u)
                for h in range(8):
                    mm = pe.transpose(unit(u)[0:NCMP, h * P:(h + 1) * P], cmpP[:, b * 8 + h, 0:NCMP], ident)
                mm.then_inc(psum_full, 1)
            u = U["cmp_out"]
            open_unit(pe, u)
            for b in range(TB):
                await_freed(pe, U["cmp_turn"] + b)
                for h in range(8):
                    g = h // 4
                    mm = pe.matmul(unit(u)[:, b * 512 + h * HD:b * 512 + (h + 1) * HD],
                                   cmpPT[0:NCMP, (b * 8 + h) * P:(b * 8 + h + 1) * P],
                                   vc[0:NCMP, g * HD:(g + 1) * HD], start=True, stop=True)
            mm.then_inc(psum_full, 1)

            def scores(s):
                kind, blk, g = ATT[s]
                u = U[f"scores{s}"]
                rows = slice(64 * g, 64 * g + 64)
                open_unit(pe, u)
                for j in range(4):
                    qz, kz = {"swa": (Z_QA + j, Z_KA), "slc": (Z_QC + j, Z_KSL), "win": (Z_QC + j, Z_KWN),
                              "diff": (Z_QB + j, Z_KB + j)}[kind]
                    mm = pe.matmul(unit(u)[:, j * T:j * T + P * (blk + 1)], zT[rows, qz, blk * P:(blk + 1) * P],
                                   zT[rows, kz, 0:P * (blk + 1)], start=True, stop=True)
                mm.then_inc(psum_full, 1)

            def turn_and_apply(s):
                kind, blk, g = ATT[s]
                nb = blk + 1
                u = U[f"turn{s}"]
                await_freed(pe, U[f"scores{s}"])
                open_unit(pe, u)
                for j in range(4):
                    for kb in range(nb):
                        mm = pe.transpose(unit(u)[:, (j * nb + kb) * P:(j * nb + kb + 1) * P],
                                          probs[:, s % 2, j * T + kb * P:j * T + (kb + 1) * P], ident)
                mm.then_inc(psum_full, 1)
                await_freed(pe, u)
                u = U[f"out{s}"]
                open_unit(pe, u)
                dv = P if kind == "diff" else HD
                for j in range(4):
                    col = {"swa": HD * g, "slc": 5 * P + HD * g, "win": 6 * P + HD * g, "diff": P * (1 + j)}[kind]
                    for kb in range(nb):
                        mm = pe.matmul(unit(u)[:, j * dv:(j + 1) * dv], probsT[:, (j * nb + kb) * P:(j * nb + kb + 1) * P],
                                       vnat[:, kb, col:col + dv], start=(kb == 0), stop=(kb == nb - 1))
                mm.then_inc(psum_full, 1)

            scores(0)
            for s in range(len(ATT)):
                if s + 1 < len(ATT):
                    scores(s + 1)
                turn_and_apply(s)
                for n in mods_ending(*ATT_MOD_SLOTS[s:s + 2]):
                    mod_sum(n)
            pe.wait_ge(sem("branches_ready"), 1)
            for br in range(3):
                u = U["branch_turn"] + br
                open_unit(pe, u)
                for c in range(4):
                    for b in range(TB):
                        mm = pe.transpose(unit(u)[:, c * T + b * P:c * T + (b + 1) * P],
                                          o_nat[:, b, br, c * P:(c + 1) * P], ident)
                mm.then_inc(psum_full, 1)
            for br in range(3):
                gemm(f"merge{br}", DC, DC, [(h_rhs, 0, DC)])
                await_freed(pe, U["branch_turn"] + br)
                gemm(f"branch{br}", 4, DC, [(lambda k, br=br: oT[:, 4 * br + k, :], 0, DC)])
            pe.wait_ge(sem("merged_ready"), 1)
            gemm("w_out", DC, DC, [(lambda k: merged[:, k, :], 0, DC)])

            norm(1, hT)
            pe.wait_ge(sem("h_ready"), 2)
            for b in range(TB):
                u = U["h_turn"] + b
                open_unit(pe, u)
                for k in range(DC):
                    mm = pe.transpose(unit(u)[:, k * P:(k + 1) * P], hT[:, k, b * P:(b + 1) * P], ident)
                mm.then_inc(psum_full, 1)
            rw = vec("router_w").rearrange("p (k e) -> p k e", k=DC)
            u = U["logits"]
            open_unit(pe, u)
            for b in range(TB):
                for k in range(DC):
                    mm = pe.matmul(unit(u)[:, b * N_EXPERTS:(b + 1) * N_EXPERTS], hT[:, k, b * P:(b + 1) * P],
                                   rw[:, k, :], start=(k == 0), stop=(k == DC - 1))
            mm.then_inc(psum_full, 1)
            mask = small[:, 264:328]
            pe.wait_ge(sem("mask_ready"), 1)
            u = U["positions"]
            open_unit(pe, u)
            E = N_EXPERTS
            pe.matmul(unit(u)[:, 0:E], before, mask[:, 0:E], start=True, stop=True)
            pe.matmul(unit(u)[:, E:2 * E], ones, mask[:, 0:E], start=True, stop=False)
            pe.matmul(unit(u)[:, E:2 * E], before, mask[:, E:2 * E], start=False, stop=True)
            pe.matmul(unit(u)[:, 2 * E:3 * E], ones, mask[:, 0:E], start=True, stop=False)
            pe.matmul(unit(u)[:, 2 * E:3 * E], ones, mask[:, E:2 * E], start=False, stop=True).then_inc(psum_full, 1)
            for q in range(PLAN.moe_unit - U["positions"] - 1):
                open_unit(pe, U["positions"] + 1 + q)
                pe.matmul(unit(U["positions"] + 1 + q)[:, 0:E], before, mask[:, 0:E], start=True,
                          stop=True).then_inc(psum_full, 1)

            def experts(turn, u0, s_base, signals, full, free, used, land, x):
                def opened(k):
                    open_unit(pe, u0 + k, turn, 16, free)

                def freed(k):
                    await_freed(pe, u0 + k, turn, 16, free)

                def expert_gemm(j0, k_unit, rhs):
                    opened(k_unit)
                    u = unit(u0 + k_unit)
                    for k in range(DC):
                        j = j0 + k // 2
                        slot = PLAN.place[PLAN.moe_slot + j]
                        if k % 2 == 0:
                            pe.wait_ge(land[slot], turn * 32 + 16 * ((s_base + j) // RING + 1))
                        w = slot_ap(PLAN.moe_slot + j)
                        for n in range(DC):
                            mm = pe.matmul(u[:, n * P:n * P + CAP], w[:, k % 2, n * P:(n + 1) * P], rhs[:, k, :],
                                           start=(k == 0 and n % 4 == 0), stop=(k == DC - 1),
                                           skip_group_check=True)
                        if k % 2 == 1:
                            mm.then_inc(used if k != DC - 1 else full, 1)

                pe.wait_ge(sem("sel_ready" + x), turn + 1)
                for e in range(2):
                    opened(e)
                    sel = moe_buf(("sel", e), TB)
                    for k in range(DC):
                        for b in range(TB):
                            mm = pe.matmul(unit(u0 + e)[:, k * P:k * P + CAP], h_nat[:, b, k * P:(k + 1) * P],
                                           sel[:, b, :], start=(b == 0), stop=(b == TB - 1))
                    mm.then_inc(full, 1)
                for e in range(2):
                    opened(2 + e)
                    sel = moe_buf(("selG", e), TB)
                    for b in range(TB):
                        mm = pe.transpose(unit(u0 + 2 + e)[0:CAP, b * P:(b + 1) * P], sel[:, b, :], ident)
                    mm.then_inc(full, 1)
                for e in range(2):
                    freed(e)
                    expert_gemm(8 * e, 4 + 2 * e, moe_buf(("xg", e), DC))
                    expert_gemm(8 * e + 4, 5 + 2 * e, moe_buf(("xg", e), DC))
                for e in range(2):
                    pe.wait_ge(sem("expert_hidden" + x), turn * 2 + (e + 1))
                    expert_gemm(16 + 4 * e, 8 + e, moe_buf(("hid", e), DC))
                for e in range(2):
                    freed(8 + e)
                    opened(10 + e)
                    y = moe_buf(("hid", e), DC)
                    for k in range(DC):
                        mm = pe.transpose(unit(u0 + 10 + e)[0:CAP, k * P:(k + 1) * P], y[:, k, :], ident)
                    mm.then_inc(full, 1)
                for e in range(2):
                    freed(2 + e)
                    freed(10 + e)
                    yN, selT = moe_buf(("yN", e)), moe_buf(("selT", e))
                    for k in range(DC):
                        c = 12 + 2 * e + k // 4
                        if k % 4 == 0:
                            opened(c)
                        mm = pe.matmul(unit(u0 + c)[:, (k % 4) * T:(k % 4 + 1) * T], yN[0:CAP, k * P:(k + 1) * P],
                                       selT[0:CAP, :], start=True, stop=True)
                        if k % 4 == 3:
                            mm.then_inc(full, 1)

            with pe.Fori(0, PAIRS) as i:
                experts(i, PLAN.moe_unit, PLAN.moe_slot, PLAN.moe_signals, psum_full, psum_free, slots_used, landed, "")
            with pe.If(many(pe) > CAP):
                for q in range(4):
                    pe.wait_ge(psum_free[q], (PLAN.moe_unit + 16 * PAIRS) // 4)
                pe.sem_inc(full_x, 16)
                pe.sem_inc(used_x, 18)
                rounds_loop(pe, lambda eng, i, turn: experts(turn, 16, 0, 18, full_x, free_x, used_x, landed_x, "_x"))
                for q in range(4):
                    pe.wait_ge(free_x[q], 4 + 4 * PAIRS * (ROUNDS - 1))

            norm(2, hT)

            def ffn(e, norm_between=None):
                for ab in range(2):
                    for n, (c0, nc_) in enumerate(FFN_PASSES):
                        split_gemm(f"ffn{e}_{'ab'[ab]}{n}", DC, nc_, h_high, h_low)
                        if e == 0:
                            mod_sum(L1_MODS + 3 * ab + n)
                        if (e, ab, n) == (1, 0, 0):
                            mod_sum(L1_MODS + N_MOD - 1)
                if norm_between is not None:
                    norm(norm_between, hT)
                split_gemm(f"ffn{e}_out", FC, DC, m_high, m_low,
                           lambda n: pe.wait_ge(sem("ffn_hidden"), 6 * e + n + 1))
                if e == 0:
                    mod_sum(L1_MODS + 6)
                    mod_sum(L1_MODS + 7)

            norm(3, hT)
            pe.wait_ge(sem("h_ready"), 4)
            ffn(0, 4)
            pe.wait_ge(sem("h_ready"), 5)
            ffn(1, 5)
            pe.wait_ge(sem("h_ready"), 6)
            split_gemm("even_qk", DC, DC, h_high, h_low)
            split_gemm("even_vu", DC, DC, h_high, h_low)
            norm(6, hT)
            pe.wait_ge(sem("h_ready"), 7)
            split_gemm("even_ctx", DC, DC, h_high, h_low)
            await_freed(pe, U["even_vu"])
            await_freed(pe, U["even_ctx"] + 1)
            for n in range(2):
                u = U["na_vturn"] + n
                open_unit(pe, u)
                for b in range(2):
                    for c in range(4):
                        at = (2 * n + b) * P
                        mm = pe.transpose(unit(u)[:, b * 512 + c * P:b * 512 + (c + 1) * P], z2v[:, c, at:at + P],
                                          ident)
                mm.then_inc(psum_full, 1)
            await_freed(pe, U["even_vu"] + 1)
            pw = vec("pool_w").rearrange("p (g n) -> p g n", g=4)
            u = U["pool_map"]
            open_unit(pe, u)
            for b in range(TB):
                for g in range(4):
                    mm = pe.matmul(unit(u)[:, b * 512 + g * P:b * 512 + (g + 1) * P], z2u[:, g, b * P:(b + 1) * P],
                                   pw[:, g, :], start=True, stop=True)
            mm.then_inc(psum_full, 1)
            await_freed(pe, u)
            pe.wait_ge(sem("band_landed"), 16)
            u = U["pool_out"]
            open_unit(pe, u)
            for g in range(4):
                for b in range(TB):
                    mm = pe.matmul(unit(u)[:, g * T:(g + 1) * T], pool_mapped[:, b, g * P:(g + 1) * P],
                                   pool_band[:, b, g, :], start=(b == 0), stop=(b == TB - 1))
            mm.then_inc(psum_full, 1)

            def na_scores(s):
                blk, pair = NA_STEPS[s]
                u = U[f"na_scores{s}"]
                open_unit(pe, u)
                for j in range(2):
                    rows = slice(64 * j, 64 * j + 64)
                    mm = pe.matmul(unit(u)[:, 512 * j:512 * j + 512], z2q[rows, pair, blk * P:(blk + 1) * P],
                                   z2k[rows, pair, :], start=True, stop=True)
                mm.then_inc(psum_full, 1)

            await_freed(pe, U["even_qk"])
            await_freed(pe, U["even_qk"] + 1)
            await_freed(pe, U["even_ctx"])
            na_scores(0)
            for s in range(len(NA_STEPS)):
                if s + 1 < len(NA_STEPS):
                    na_scores(s + 1)
                blk, pair = NA_STEPS[s]
                u = U[f"na_turn{s}"]
                await_freed(pe, U[f"na_scores{s}"])
                open_unit(pe, u)
                for j in range(2):
                    for kb in range(4):
                        mm = pe.transpose(unit(u)[:, (4 * j + kb) * P:(4 * j + kb + 1) * P],
                                          na_probs[:, j, kb * P:(kb + 1) * P], ident)
                mm.then_inc(psum_full, 1)
                await_freed(pe, u)
                u = U[f"na_out{s}"]
                open_unit(pe, u)
                for j in range(2):
                    h = 2 * pair + j
                    for kb in range(4):
                        mm = pe.matmul(unit(u)[:, j * HD:(j + 1) * HD], na_probsT[:, (4 * j + kb) * P:(4 * j + kb + 1) * P],
                                       vnat2[:, kb, h * HD:(h + 1) * HD], start=(kb == 0), stop=(kb == 3))
                mm.then_inc(psum_full, 1)
            await_freed(pe, U[f"na_out{len(NA_STEPS) - 1}"])
            u = U["na_oturn"]
            open_unit(pe, u)
            for c in range(4):
                for b in range(TB):
                    mm = pe.transpose(unit(u)[:, c * T + b * P:c * T + (b + 1) * P], na_o[:, b, c * P:(c + 1) * P],
                                      ident)
            mm.then_inc(psum_full, 1)
            await_freed(pe, u)
            await_freed(pe, U["pool_out"])
            gemm("even_out", DC, DC, [(lambda k: cat[:, k, :], 0, DC)])
            for e in (2, 3):
                norm(5 + e, hT)
                pe.wait_ge(sem("h_ready"), 6 + e)
                ffn(e)
            norm(9, hT)
            pe.wait_ge(sem("h_ready"), 10)
            for n in range(3):
                split_gemm(f"conv{n}", DC, DC, h_high, h_low)
            pe.wait_ge(sem("conv_ready"), 1)
            gemm("conv_out", DC, DC, [(lambda k: conv_y[:, k, :], 0, DC)])
            norm(10, hT)
            pe.wait_ge(sem("h_ready"), 11)
            ffn(4)
            norm(11, hT)

        @block.vector
        def _(dve):
            steps = Steps(dve, dve_steps)
            link = steps.link

            def wide(v, n):
                return v[:, :, None].broadcast_to([v.shape[0], v.shape[1], n])

            def chunks(u, n=4, width=T):
                return unit(u)[:, 0:n * width].rearrange("p (c t) -> p c t", c=n)

            def free(ins_, u):
                ins_.then_inc(psum_free[u % 4], 1)

            def finish(ins_, u, done):
                free(ins_, u)
                await_freed(dve, u)
                dve.sem_inc(sem(done), 1)

            dve.wait_ge(sem("vecs_landed"), 16)
            lp = vec("lambda").rearrange("p (n d) -> p n d", n=4)
            lam = small[:, 414:415]
            link(dve.tensor_tensor(lp[:, 0::2, :], lp[:, 0::2, :], lp[:, 1::2, :], ALU.mult))
            dve.tensor_reduce(small[:, 410:412], lp[:, 0::2, :], AX_X, ALU.add).then_inc(sem("lambda_dots"), 1)
            dve.wait_ge(sem("lambda_exp"), 1)
            link(dve.tensor_tensor(lam, small[:, 413:414], small[:, 412:413], ALU.subtract))
            link(dve.tensor_scalar(lam, lam, -LAM_INIT, None, ALU.add))
            link(dve.tensor_scalar(vec("subln"), vec("subln"), 1.0 - LAM_INIT, None, ALU.mult))

            dve.wait_ge(sem("cond_ready"), 2)

            def mod_slot(i):
                n, pair = divmod(i, 4)
                block_, layer, g, conds = MODS[n]
                s = PLAN.mod_at[i]
                await_slot(dve, s)
                w = slot_ap(s)
                for c in range(conds):
                    last_group = MOD_BUFFER_BEFORE[n][c]
                    if pair == 0 and last_group is not None:
                        await_unit(dve, U[mod_unit(last_group)])
                for k in (2 * pair, 2 * pair + 1):
                    for c in range(conds):
                        part = mod_sums[:, MOD_BUFFERS[n][c], :]
                        cond = cs[:, k:k + 1] if block_ == 1 else cs2[:, k, c:c + 1]
                        if k == 0:
                            last = dve.tensor_scalar(part, w[:, k % 2, :], cond, None, ALU.mult)
                        else:
                            last = dve.scalar_tensor_tensor(part, w[:, k % 2, :], cond, part, ALU.mult, ALU.add)
                        if (k % 2, c) != (1, conds - 1):
                            steps.done(last)
                    if k % 2 == 0:
                        steps.settle()
                last.then_inc(sem("mod_slots_used"), 1)
                dve.wait_ge(sem("mod_slots_used"), i + 1)
                if pair == 3:
                    dve.sem_inc(sem("mod_partials"), 1)

            def modulation(n):
                block_, layer, g, conds = MODS[n]
                u = U[mod_unit(n)]
                await_unit(dve, u)
                if block_ == 1:
                    free(dve.tensor_tensor(mod1[:, g, :], unit(u)[:, 0:DC], vec("mod_b")[:, g * DC:(g + 1) * DC],
                                           ALU.add), u)
                    if g in (1, 4):
                        await_freed(dve, u)
                        link(dve.scalar_tensor_tensor(mod1[:, g, :], mod1[:, g, :], 1.0,
                                                      vec("norm1" if g == 1 else "norm2"), ALU.add, ALU.mult))
                    return
                m = mod2[:, layer, g, :, 0:conds]
                at = (layer * N_MOD + g) * DC
                free(dve.tensor_tensor(m, unit(u)[:, 0:conds * DC].rearrange("p (k s) -> p k s", s=conds),
                                       wide(vec("mod_b2")[:, at:at + DC], conds), ALU.add), u)
                if g % 3 == 1:
                    await_freed(dve, u)
                    at = (layer * 3 + g // 3) * DC
                    link(dve.scalar_tensor_tensor(m, m, 1.0, wide(vec("norm_g2")[:, at:at + DC], conds), ALU.add,
                                                  ALU.mult))
                if g in (2, 8):
                    await_freed(dve, u)
                    link(dve.tensor_scalar(m, m, 0.5, None, ALU.mult))

            for i in range(8):
                mod_slot(i)
            modulation(0)
            modulation(1)

            def norm(n, src, dst, scale, shift, eps):
                u = U[f"norm{n}"]
                await_unit(dve, u)
                free(dve.tensor_scalar(rstd[:, 0, :], unit(u)[:, 0:T], 1.0 / D, eps, ALU.mult, ALU.add), u)
                dve.wait_ge(sem("root_ready"), n + 1)
                link(dve.reciprocal(rstd[:, 0, :], rstd[:, 1, :]))
                link(dve.tensor_tensor(dst, src, rstd[:, 0:1, :].broadcast_to([P, DC, T]), ALU.mult))
                for k in range(DC):
                    if shift is None:
                        last = dve.tensor_scalar(dst[:, k, :], dst[:, k, :], scale[:, k:k + 1], None, ALU.mult)
                    else:
                        last = dve.tensor_scalar(dst[:, k, :], dst[:, k, :], scale[:, k:k + 1], shift[:, k:k + 1],
                                                 ALU.mult, ALU.add)
                if 3 <= n <= 10:
                    last.then_inc(sem("h_whole"), 1)
                    dve.wait_ge(sem("h_high_ready"), n - 2)
                    last = dve.tensor_tensor(h_low[:, :, :], dst, h_high[:, :, :].bitcast(F32), ALU.subtract)
                last.then_inc(sem("h_ready"), 1)

            norm(0, xT[:, :, :], hT[:, :, :], mod1[:, 1, :], mod1[:, 0, :], EPS1)
            for n, (c0, nc_) in enumerate(Z_PASSES):
                for i in range(8 + 4 * n, 12 + 4 * n):
                    mod_slot(i)
                for half in range(-(-nc_ // 4)):
                    u, k = U[f"z{n}"] + half, min(4, nc_ - 4 * half)
                    z = c0 + 4 * half
                    await_unit(dve, u)
                    last = dve.tensor_tensor(zT[:, z:z + k, :], chunks(u, k), wide(vec("b_in")[:, z:z + k], T), ALU.add)
                    if half == 0:
                        free(last, u)
                finish(last, u, "z_ready")
                modulation(2 + n)
            for m, z in enumerate((Z_KCM, Z_VCM)):
                dst = blocks[:, m, :].rearrange("p (j c) -> p j c", j=16)
                for g in range(2):
                    for odd in range(2):
                        for late in range(2):
                            src = zT[64 * g:64 * g + 64, z, 16 * late:16 * late + 16 * NCMP]
                            src = src.rearrange("p (c x) -> p x c", x=16)[:, odd::2, :]
                            dve.tensor_copy(dst[64 * odd:64 * odd + 64, 8 * late:8 * late + 8,
                                                g * NCMP:(g + 1) * NCMP], src)
                last = dve.tensor_copy(dst[:, :, 30:31], vec("cmp_pos")[:, 16 * m:16 * m + 16, None])
            last.then_inc(sem("blocks_ready"), 1)
            u = U["cmp_hidden"]
            await_unit(dve, u)
            dve.tensor_tensor(small[:, 192:196], unit(u)[:, 30:128:32], vec("cmp_b1"), ALU.add).then_inc(
                sem("cmp_bias_ready"), 1)
            u = U["cmp_kv"]
            await_unit(dve, u)
            dve.tensor_scalar(small[:, 200:230], unit(u)[:, 0:2 * NCMP], vec("cmp_b2k"), None, ALU.add)
            b2v = vec("cmp_b2v")[0:NCMP, None, :].broadcast_to([NCMP, 2, HD])
            free(dve.tensor_tensor(small[0:NCMP, 232:360].rearrange("p (g d) -> p g d", g=2),
                                   unit(u)[0:NCMP, 512:640].rearrange("p (g d) -> p g d", g=2), b2v, ALU.add), u)
            u = U["cmp_scores"]
            await_unit(dve, u)
            for b in range(TB):
                cb = const("cmp_bias")[:, None, 16 * b:16 * b + NCMP].broadcast_to([P, 4, NCMP])
                for g in range(2):
                    src = unit(u)[:, 512 * g + 64 * b:512 * g + 64 * b + 64]
                    src = src.rearrange("p (h c) -> p h c", h=4)[:, :, 0:NCMP]
                    last = dve.scalar_tensor_tensor(cmpP[:, 8 * b + 4 * g:8 * b + 4 * g + 4, 0:NCMP], src, HD ** -0.5,
                                                    cb, ALU.mult, ALU.add)
            free(last, u)
            await_freed(dve, u)
            cp = cmpP[:, :, 0:NCMP]
            link(dve.tensor_reduce(small[:, 360:376], cp, AX_X, ALU.max))
            dve.tensor_tensor(cp, cp, wide(small[:, 360:376], NCMP), ALU.subtract).then_inc(sem("cmp_shifted"), 1)
            dve.wait_ge(sem("cmp_exp"), 1)
            link(dve.tensor_reduce(small[:, 376:392], cp, AX_X, ALU.add))
            link(dve.reciprocal(small[:, 376:392], small[:, 376:392]))
            link(dve.tensor_tensor(cp, cp, wide(small[:, 376:392], NCMP), ALU.mult))
            for b in range(TB):
                cv = const("cmp_valid")[:, None, 16 * b:16 * b + NCMP].broadcast_to([P, 8, NCMP])
                last = dve.tensor_tensor(cmpP[:, 8 * b:8 * b + 8, 0:NCMP], cmpP[:, 8 * b:8 * b + 8, 0:NCMP], cv,
                                         ALU.mult)
            last.then_inc(sem("cmp_probs"), 1)
            u = U["cmp_out"]
            await_unit(dve, u)
            for b in range(TB):
                await_freed(dve, U["vnat"] + b)
                gates = small[:, 24 * b:24 * b + 24].rearrange("p (h r) -> p h r", h=8)
                last = dve.tensor_tensor(o_nat[:, b, 2, :].rearrange("p (h d) -> p h d", h=8),
                                         unit(u)[:, 512 * b:512 * b + 512].rearrange("p (h d) -> p h d", h=8),
                                         gates[:, :, 0:1].broadcast_to([P, 8, HD]), ALU.mult)
            free(last, u)

            dve.wait_ge(sem("alibi_landed"), 32)

            def soft(s):
                kind, blk, g = ATT[s]
                kw = P * (blk + 1)
                u = U[f"scores{s}"]
                table = alibi_near if kind == "swa" else alibi_full
                table = table[:, 1::2, T - kw:T] if kind == "diff" else table[:, 4 * g:4 * g + 4, T - kw:T]
                sc = chunks(u)[:, :, 0:kw]
                await_unit(dve, u)
                link(dve.scalar_tensor_tensor(sc, sc, HD ** -0.5, table, ALU.mult, ALU.add))
                link(dve.tensor_reduce(stats[:, 0, s, :], sc, AX_X, ALU.max))
                if kind == "swa":
                    sinks = vec("sinks")[:, 4 * g:4 * g + 4]
                    link(dve.tensor_tensor(stats[:, 0, s, :], stats[:, 0, s, :], sinks, ALU.max))
                    dve.tensor_tensor(stats[:, 3, s, :], sinks, stats[:, 0, s, :], ALU.subtract)
                dve.tensor_scalar(stats[:, 1, s, :], stats[:, 0, s, :], -1.0, None, ALU.mult).then_inc(
                    sem("row_max_ready"), 1)

            tmp = rstd[:, :, :].rearrange("p a t -> p (a t)")

            def attended(s):
                kind, blk, g = ATT[s]
                u = U[f"out{s}"]
                await_freed(dve, U[f"scores{s}"])
                if kind == "swa":
                    dve.wait_ge(sem("sink_exp"), [a[0] for a in ATT[:s + 1]].count("swa"))
                    link(dve.tensor_tensor(stats[:, 2, s, :], stats[:, 2, s, :], stats[:, 3, s, :], ALU.add))
                link(dve.reciprocal(stats[:, 2, s, :], stats[:, 2, s, :]))
                if kind in ("slc", "win"):
                    gates = small[:, 24 * blk:24 * blk + 24].rearrange("p (h r) -> p h r", h=8)
                    br = 1 if kind == "slc" else 2
                    link(dve.tensor_tensor(stats[:, 2, s, :, None], stats[:, 2, s, :, None],
                                           gates[:, 4 * g:4 * g + 4, br:br + 1], ALU.mult))
                if kind == "diff" and g == 1:
                    link(dve.tensor_scalar(stats[:, 2, s, :], stats[:, 2, s, :], lam, None, ALU.mult))
                dv = P if kind == "diff" else HD
                branch = {"swa": 0, "diff": 1, "slc": 2, "win": 2}[kind]
                at = 0 if kind == "diff" else 256 * g
                dst = o_nat[:, blk, branch, at:at + 4 * dv]
                adds = kind in ("slc", "win") or (kind == "diff" and g == 1)
                await_unit(dve, u)
                to = tmp[:, 0:4 * dv] if adds else dst
                free(dve.tensor_tensor(to.rearrange("p (h d) -> p h d", h=4), chunks(u, 4, dv),
                                       wide(stats[:, 2, s, :], dv), ALU.mult), u)
                if adds:
                    await_freed(dve, u)
                    link(dve.tensor_tensor(dst, dst, to, ALU.add))

            soft(0)
            for s in range(len(ATT)):
                if s + 1 < len(ATT):
                    soft(s + 1)
                if s:
                    for n in mods_ending(*ATT_MOD_SLOTS[s - 1:s + 1]):
                        modulation(n)
                for i in range(*ATT_MOD_SLOTS[s:s + 2]):
                    mod_slot(24 + i)
                attended(s)
            for n in mods_ending(*ATT_MOD_SLOTS[-2:]):
                modulation(n)
            for b in range(TB):
                link(dve.tensor_tensor(tmp, o_nat[:, b, 1, :], o_nat[:, b, 1, :], ALU.mult))
                link(dve.tensor_reduce(small[:, 400 + 4 * b:404 + 4 * b], tmp.rearrange("p (h d) -> p h d", h=4),
                                       AX_X, ALU.add))
            dve.tensor_scalar(small[:, 400:408], small[:, 400:408], 1.0 / P, EPS1, ALU.mult, ALU.add).then_inc(
                sem("subln_mean"), 1)
            dve.wait_ge(sem("subln_root"), 1)
            link(dve.reciprocal(small[:, 400:408], small[:, 400:408]))
            for b in range(TB):
                ob = o_nat[:, b, 1, :].rearrange("p (h d) -> p h d", h=4)
                link(dve.tensor_tensor(ob, ob, wide(small[:, 400 + 4 * b:404 + 4 * b], P), ALU.mult))
                last = dve.tensor_tensor(ob, ob, vec("subln")[:, None, :].broadcast_to([P, 4, P]), ALU.mult)
            last.then_inc(sem("branches_ready"), 1)

            for br in range(3):
                for half in range(2):
                    u = U[f"branch{br}"] + half
                    gate = gm[:, br * DC + 4 * half:br * DC + 4 * half + 4, :]
                    dst = merged[:, 4 * half:4 * half + 4, :]
                    await_freed(dve, U[f"merge{br}"] + half)
                    await_unit(dve, u)
                    if br == 0:
                        free(dve.tensor_tensor(dst, chunks(u), gate, ALU.mult), u)
                        await_freed(dve, u)
                    else:
                        free(dve.tensor_tensor(merge_tmp, chunks(u), gate, ALU.mult), u)
                        await_freed(dve, u)
                        last = dve.tensor_tensor(dst, dst, merge_tmp, ALU.add)
                        if (br, half) == (2, 1):
                            last.then_inc(sem("merged_ready"), 1)
                        else:
                            link(last)

            def add_to(dst, u0, gate):
                for k in range(DC):
                    u = u0 + k // 4
                    if k % 4 == 0:
                        await_unit(dve, u)
                    last = dve.scalar_tensor_tensor(dst[:, k, :], unit(u)[:, (k % 4) * T:(k % 4 + 1) * T],
                                                    gate[:, k:k + 1], dst[:, k, :], ALU.mult, ALU.add)
                    if k == 3:
                        free(last, u)
                return last, u

            finish(*add_to(xT, U["w_out"], mod1[:, 2, :]), "x_ready")
            norm(1, xT[:, :, :], hT[:, :, :], mod1[:, 4, :], mod1[:, 3, :], EPS1)

            E = N_EXPERTS
            vals, top, negmax = small[:, 0:72], small[:, 72:88], small[:, 88:90]
            total, expd, replaced = small[:, 92:94], small[:, 128:192], small[:, 192:264]
            mask, gate, place = small[:, 264:328], small[:, 328:392], small[:, 392:456]
            u = U["logits"]
            await_unit(dve, u)
            for b in range(TB):
                last = dve.tensor_tensor(vals[:, 36 * b:36 * b + E], unit(u)[:, E * b:E * b + E], vec("router_b"),
                                         ALU.add)
            free(last, u)
            await_freed(dve, u)
            for b in range(TB):
                link(dve.max(top[:, 8 * b:8 * b + 8], vals[:, 36 * b:36 * b + E]))
            for b in range(TB):
                dve.tensor_scalar(negmax[:, b:b + 1], top[:, 8 * b:8 * b + 1], -1.0, None, ALU.mult).then_inc(
                    sem("top_ready"), 1)
            for n in range(4):
                for b in range(TB):
                    link(dve.memset(vals[:, 36 * b + E + n:36 * b + E + n + 1], -(n + 1.0) * 1e37))
                    link(dve.memset(top[:, 8 * b + 4 + n:8 * b + 5 + n], -(n + 1.0) * 1e37))
            for b in range(TB):
                v, r = vals[:, 36 * b:36 * b + 36], replaced[:, 36 * b:36 * b + 36]
                link(dve.match_replace(r, top[:, 8 * b:8 * b + 8], v, 3e38))
                last = dve.tensor_tensor(mask[:, E * b:E * b + E], r[:, 0:E], v[:, 0:E], ALU.not_equal)
                link(last) if b == 0 else last.then_inc(sem("mask_ready"), 1)
            dve.wait_ge(sem("mask_ready"), 1)
            dve.wait_ge(sem("route_exp"), 2)
            link(dve.tensor_tensor(gate, expd, mask, ALU.mult))
            link(dve.tensor_reduce(total, gate.rearrange("p (b e) -> p b e", b=TB), AX_X, ALU.add))
            link(dve.reciprocal(total, total))
            link(dve.tensor_tensor(gate.rearrange("p (b e) -> p b e", b=TB), gate.rearrange("p (b e) -> p b e", b=TB),
                                   wide(total, E), ALU.mult))
            u = U["positions"]
            await_unit(dve, u)
            dve.scalar_tensor_tensor(place, unit(u)[:, 0:2 * E], 1.0, mask, ALU.add, ALU.mult)
            free(dve.tensor_reduce(small[:, 460:461], unit(u)[:, 2 * E:3 * E], AX_X, ALU.max), u)
            await_freed(dve, u)
            link(dve.tensor_scalar(place, place, -1.0, None, ALU.add))
            dve.tensor_copy(count_max[:, :], small[:, 460:461]).then_inc(sem("count_ready"), 1)
            for q in range(PLAN.moe_unit - U["positions"] - 1):
                u = U["positions"] + 1 + q
                await_unit(dve, u)
                free(dve.tensor_copy(small[:, 461:462], unit(u)[:, 0:1]), u)
                await_freed(dve, u)
            link(dve.memset(acc, 0.0))

            def experts(turn, steps, u0, full, free_, x):
                def un(k):
                    return unit(u0 + k).rearrange("p (k c) -> p k c", k=DC)[:, :, 0:CAP]

                def ready(k):
                    await_unit(dve, u0 + k, turn, 16, full)

                def freeing(ins_, k):
                    ins_.then_inc(free_[(u0 + k) % 4], 1)

                def freed(k):
                    await_freed(dve, u0 + k, turn, 16, free_)

                slot_no = const("iota")[:, 0:CAP]
                for e in range(2):
                    sel, sg = moe_buf(("sel", e), TB), moe_buf(("selG", e), TB)
                    for b in range(TB):
                        p_ = small[:, bass.ds(x_turn(turn) * 2 + (392 + E * b + e), 1)]
                        g_ = small[:, bass.ds(x_turn(turn) * 2 + (328 + E * b + e), 1)]
                        dve.tensor_scalar(sel[:, b, :], slot_no, p_, None, ALU.is_equal)
                        last = dve.tensor_scalar(sg[:, b, :], slot_no, p_, g_, ALU.is_equal, ALU.mult)
                last.then_inc(sem("sel_ready" + x), 1)
                gb, ub, sig = moe_buf("g", DC), moe_buf("u", DC), moe_buf("sig", DC)
                b1, b2 = VEC_AT["exp_b1"][0], VEC_AT["exp_b2"][0]
                for e in range(2):
                    ready(4 + 2 * e)
                    freeing(dve.tensor_tensor(gb, un(4 + 2 * e), bias_of(turn, b1 + 16 * e, 32), ALU.add), 4 + 2 * e)
                    freed(4 + 2 * e)
                    dve.tensor_scalar(gb, gb, LIMIT, None, ALU.min).then_inc(sem("gate_clamped" + x), 1)
                    ready(5 + 2 * e)
                    freeing(dve.tensor_tensor(ub, un(5 + 2 * e), bias_of(turn, b1 + 16 * e + DC, 32), ALU.add),
                            5 + 2 * e)
                    freed(5 + 2 * e)
                    steps.link(dve.tensor_scalar(ub, ub, LIMIT, -LIMIT, ALU.min, ALU.max))
                    dve.wait_ge(sem("gate_sigmoid" + x), turn * 2 + (e + 1))
                    steps.link(dve.tensor_tensor(gb, gb, sig, ALU.mult))
                    dve.scalar_tensor_tensor(moe_buf(("hid", e), DC), ub, 1.0, gb, ALU.add, ALU.mult).then_inc(
                        sem("expert_hidden" + x), 1)
                    dve.wait_ge(sem("expert_hidden" + x), turn * 2 + (e + 1))
                for e in range(2):
                    ready(8 + e)
                    freeing(dve.tensor_tensor(moe_buf(("hid", e), DC), un(8 + e), bias_of(turn, b2 + DC * e, 16),
                                              ALU.add), 8 + e)
                for k in range(12, 16):
                    ready(k)
                    half = k % 2
                    freeing(dve.tensor_tensor(acc[:, 4 * half:4 * half + 4, :], chunks(u0 + k),
                                              acc[:, 4 * half:4 * half + 4, :], ALU.add), k)
                    freed(k)

            pair_of = {}

            def x_turn(turn):
                return pair_of.get("pair", turn)

            def bias_of(turn, base, per_pair):
                return wide(vecs[:, bass.ds(x_turn(turn) * per_pair + base, DC)], CAP)

            with dve.Fori(0, PAIRS) as i:
                steps.enter(i, 4)
                experts(i, steps, PLAN.moe_unit, psum_full, psum_free, "")
                steps.leave(PAIRS)
            with dve.If(many(dve) > CAP):
                for q in range(4):
                    dve.sem_inc(free_x[q], 4)
                steps_x = Steps(dve, sem("dve_steps_x"))
                with dve.Fori(0, ROUNDS - 1) as r:
                    dve.tensor_scalar(place, place, -float(CAP), None, ALU.add).then_inc(sem("round_shifted"), 1)
                    dve.wait_ge(sem("round_shifted"), r + 1)
                    dve.memset(small[:, 463:464], 0.0)
                    with dve.Fori(0, PAIRS) as i:
                        pair_of["pair"] = i
                        turn = r * PAIRS + i
                        steps_x.enter(turn, 4)
                        experts(turn, steps_x, 16, full_x, free_x, "_x")
            pair_of.clear()
            for k in range(DC):
                last = dve.scalar_tensor_tensor(xT[:, k, :], acc[:, k, :], mod1[:, 5, k:k + 1], xT[:, k, :],
                                                ALU.mult, ALU.add)
            last.then_inc(sem("x_ready"), 1)
            dve.wait_ge(sem("x_ready"), 2)
            norm(2, xT[:, :, :], xT[:, :, :], vec("final1"), None, EPS1)

            def norm2(n, layer, which, t=0):
                norm(n, (xT[:, :, :], cT)[t], hT[:, :, :], mod2[:, layer, 3 * which + 1, :, t],
                     mod2[:, layer, 3 * which, :, t], EPS2)

            lows, mods_done, at = [0], [4 * L1_MODS], [moe_end]

            def low_parts(until):
                for s in range(at[0], until):
                    if s in PLAN.split_no:
                        m, cols = PLAN.split_no[s], PLAN.stream[s][5]
                        dve.wait_ge(sem("w_high_ready"), m + 1)
                        dve.tensor_tensor(low_ap(s, cols), slot_ap(s, 2, cols), high_ap(m, cols).bitcast(F32),
                                          ALU.subtract).then_inc(sem("w_split"), 1)
                    elif mods_done[0] < len(PLAN.mod_at) and PLAN.mod_at[mods_done[0]] == s:
                        mod_slot(mods_done[0])
                        mods_done[0] += 1
                at[0] = max(at[0], until)

            def ffn(e, layer, which, between=None):
                t = FFNS[e][1]
                for n in range(len(FFN_PASSES)):
                    low_parts(ahead_of(f"ffn{e}_a{n}"))
                    if e == 0:
                        modulation(L1_MODS + n)
                    if (e, n) == (1, 0):
                        modulation(L1_MODS + N_MOD - 1)
                for n, (c0, nc_) in enumerate(FFN_PASSES):
                    low_parts(ahead_of(f"ffn{e}_b{n}"))
                    for half in range(2):
                        k = min(4, nc_ - 4 * half)
                        u = U[f"ffn{e}_b{n}"] + half
                        dst = hm[:, c0 + 4 * half:c0 + 4 * half + k, :]
                        await_freed(dve, U[f"ffn{e}_a{n}"] + half)
                        await_unit(dve, u)
                        free(dve.tensor_tensor(dst, chunks(u, k), dst, ALU.mult), u)
                    for half in range(2):
                        k = min(4, nc_ - 4 * half)
                        c = c0 + 4 * half
                        dve.wait_ge(sem("m_high_ready"), 6 * e + 2 * n + half + 1)
                        dve.tensor_tensor(m_low[:, c:c + k, :], hm[:, c:c + k, :],
                                          m_high[:, c:c + k, :].bitcast(F32), ALU.subtract).then_inc(
                            sem("ffn_hidden"), 1)
                    if e == 0:
                        modulation(L1_MODS + 3 + n)
                if between:
                    between()
                low_parts(ahead_of(f"ffn{e}_out"))
                finish(*add_to((xT, cT)[t], U[f"ffn{e}_out"], mod2[:, layer, 3 * which + 2, :, t]), "x_ready")
                if e == 0:
                    modulation(L1_MODS + 6)
                    modulation(L1_MODS + 7)

            dve.wait_ge(sem("h_ready"), 3)
            low_parts(PLAN.split_at[HIGHS - 1] + 1)
            norm2(3, 0, 0)
            ffn(0, 0, 0, lambda: norm2(4, 0, 0, 1))
            ffn(1, 0, 0, lambda: norm2(5, 0, 1))
            low_parts(ahead_of("even_qk"))
            low_parts(ahead_of("even_vu"))
            norm2(6, 0, 1, 1)
            low_parts(ahead_of("even_ctx"))
            u = U["pool_out"]
            await_unit(dve, u)
            for g in range(4):
                last = dve.tensor_scalar(cat[:, 4 + g, :], unit(u)[:, g * T:(g + 1) * T],
                                         vec("pool_scale")[:, g:g + 1], None, ALU.mult)
            free(last, u)
            dve.wait_ge(sem("rpb_masked"), 1)

            def na_soft(s):
                blk, pair = NA_STEPS[s]
                u = U[f"na_scores{s}"]
                sc = unit(u).rearrange("p (j k) -> p j k", j=2)
                await_unit(dve, u)
                link(dve.tensor_tensor(sc[:, :, 0:T], sc[:, :, 0:T],
                                       rpb[:, 8 * blk + 2 * pair:8 * blk + 2 * pair + 2, :], ALU.add))
                link(dve.tensor_reduce(stats[:, 0, s, 0:2], sc, AX_X, ALU.max))
                dve.tensor_scalar(stats[:, 1, s, 0:2], stats[:, 0, s, 0:2], -1.0, None, ALU.mult).then_inc(
                    sem("na_max_ready"), 1)

            na_soft(0)
            for s in range(len(NA_STEPS)):
                if s + 1 < len(NA_STEPS):
                    na_soft(s + 1)
                blk, pair = NA_STEPS[s]
                u = U[f"na_out{s}"]
                await_freed(dve, U[f"na_scores{s}"])
                link(dve.reciprocal(stats[:, 2, s, 0:2], stats[:, 2, s, 0:2]))
                await_unit(dve, u)
                free(dve.tensor_tensor(na_o[:, blk, P * pair:P * pair + P].rearrange("p (h d) -> p h d", h=2),
                                       chunks(u, 2, HD), wide(stats[:, 2, s, 0:2], HD), ALU.mult), u)
            finish(*add_to(xT, U["even_out"], mod2[:, 0, 5, :, 0]), "x_ready")
            norm2(7, 0, 2)
            ffn(2, 0, 2)
            norm2(8, 1, 0)
            ffn(3, 1, 0)
            norm2(9, 1, 1)
            low_parts(ahead_of("conv0"))
            low_parts(ahead_of("conv1"))
            low_parts(ahead_of("conv2"))
            dve.wait_ge(sem("conv_edges"), 2)
            for half in range(2):
                u = U["conv2"] + half
                await_freed(dve, U["conv1"] + half)
                await_unit(dve, u)
                free(dve.tensor_tensor(conv_z[:, 4 * half:4 * half + 4, 1:T + 1], chunks(u),
                                       conv_c[:, 4 * half:4 * half + 4, :], ALU.mult), u)
            await_freed(dve, U["conv2"])
            await_freed(dve, U["conv2"] + 1)
            taps = vec("conv_w").rearrange("p (n k) -> p n k", n=3)
            for k in range(DC):
                last = dve.tensor_scalar(conv_y[:, k, :], conv_z[:, k, 0:T], taps[:, 0, k:k + 1], None, ALU.mult)
            link(last)
            for n in (1, 2):
                for k in range(DC):
                    last = dve.scalar_tensor_tensor(conv_y[:, k, :], conv_z[:, k, n:n + T], taps[:, n, k:k + 1],
                                                    conv_y[:, k, :], ALU.mult, ALU.add)
                link(last)
            await_freed(dve, U["conv0"])
            await_freed(dve, U["conv0"] + 1)
            dve.tensor_tensor(conv_y, conv_y, conv_b, ALU.mult).then_inc(sem("conv_ready"), 1)
            finish(*add_to(xT, U["conv_out"], mod2[:, 1, 5, :, 0]), "x_ready")
            norm2(10, 1, 2)
            ffn(4, 1, 2)
            norm(11, xT[:, :, :], hT[:, :, :], vec("final2"), None, EPS2)


def shape_constants():
    q = np.arange(P)
    c = {}
    c["ident"] = np.eye(P, dtype=np.float32)
    c["ones"] = np.ones((P, P), np.float32)
    c["before"] = (q[:, None] < q[None, :]).astype(np.float32)
    c["iota"] = np.tile(np.arange(P, dtype=np.float32), (P, 1))
    col = np.arange(GRID_W)
    start = np.clip(col - KW // 2, 0, GRID_W - KW)
    ok = (col[None, :] >= start[:, None]) & (col[None, :] < start[:, None] + KW)
    c["col_mask"] = np.tile(np.where(ok, 0.0, NEG).astype(np.float32), (2, 1))
    valid = np.zeros((P, 2, 16), np.float32)
    for b in range(TB):
        t = b * P + q
        valid[:, b, :NCMP] = (np.arange(NCMP)[None, :] * 16 + 31) <= t[:, None]
    c["cmp_valid"] = valid.reshape(P, 32)
    c["cmp_bias"] = np.where(valid > 0, 0.0, NEG).astype(np.float32).reshape(P, 32)
    packed = np.concatenate([c[name] for name, _ in CONSTS], axis=1)
    dist = (q[:, None] + P - np.arange(T)[None, :]).astype(np.float32)
    slopes = 2.0 ** -np.arange(1, 9, dtype=np.float32)
    full = np.where(dist[:, None, :] >= 0, -slopes[None, :, None] * dist[:, None, :], NEG)
    near = np.where(dist[:, None, :] < 128, full, NEG)
    band = np.zeros((P, TB, 4, T), np.float32)
    t = np.arange(T)
    for g, w in enumerate((2, 4, 8, 16)):
        lo, hi = np.clip(t - w // 2, 0, T), np.clip(t - w // 2 + w, 0, T)
        m = ((t[:, None] >= lo[None, :]) & (t[:, None] < hi[None, :])) / (hi - lo)[None, :]
        m = (m - np.eye(T)).astype(np.float32)
        band[:, :, g, :] = m.reshape(TB, P, T).transpose(1, 0, 2)
    return packed, full, near, band


def kernel(**inputs):
    import ml_dtypes
    import concourse.bacc as bacc
    from concourse.bass_utils import run_bass_kernel_spmd

    a = {k: np.asarray(v) for k, v in inputs.items()}

    def cols(v):
        v = v.reshape(-1, P)
        return np.ascontiguousarray(v.T)

    def rows(v):
        return np.broadcast_to(v.reshape(1, -1), (P, v.size))

    def pairs_of_heads(w):
        h = w.reshape(w.shape[0], 2, 4, HD)
        return h.transpose(0, 2, 1, 3).reshape(w.shape[0], 512)

    def mixer_columns(w):
        at = np.cumsum([512, 128, 128, 512, 512, 512, 512, 128, 128, 128, 128, 128, 128, 24])
        qa, ka, va, qb, kb, vb, qc, kcm, vcm, ksl, vsl, kwn, vwn, gates, merge = np.split(w, at, axis=1)
        pad = np.zeros((w.shape[0], P - 24), w.dtype)
        return np.concatenate([pairs_of_heads(qa), pairs_of_heads(qc), qb, kb, ka, va, vb, kcm, vcm, ksl, vsl,
                               kwn, vwn, gates, pad, merge], axis=1)

    w2 = a["cmp_w2"][0].reshape(2, 2, P, HD)
    w2 = np.concatenate([w2, w2], axis=3).transpose(2, 0, 1, 3).reshape(P, 4 * P)
    vec = {
        "c": cols(a["c"]), "mod_b": cols(a["mod_b"]), "norm1": cols(a["norm1_g"]), "norm2": cols(a["norm2_g"]),
        "b_in": cols(mixer_columns(a["b_in"])), "final1": cols(a["final_g"]),
        "exp_b1": cols(a["exp_b1"]), "exp_b2": cols(a["exp_b2"]),
        "cmp_pos": cols(a["cmp_pos"]), "cmp_b1": cols(a["cmp_b1"]),
        "cmp_b2k": np.concatenate([a["cmp_b2"][0, 0]] * 2)[:, None], "cmp_b2v": rows(a["cmp_b2"][0, 1]),
        "cmp_w2": w2, "sinks": rows(a["sinks"]), "lambda": rows(a["diff_lambda"]), "subln": rows(a["diff_subln_g"]),
        "router_w": a["router_w"][0].reshape(DC, P, N_EXPERTS).transpose(1, 0, 2).reshape(P, -1),
        "router_b": rows(a["router_b"]),
        "cond2": np.stack([cols(a["c_2"]), cols(a["c_ctx_2"])], axis=2).reshape(P, -1),
        "mod_b2": cols(a["mod_b_2"]), "norm_g2": cols(a["norm_g_2"]),
        "pool_w": a["pool_w_2"][0].transpose(1, 0, 2).reshape(P, -1), "pool_scale": cols(a["pool_scale_2"]),
        "conv_w": cols(a["conv_w_2"]), "final2": cols(a["final_g_2"]),
    }
    packed, full, near, band = shape_constants()
    padded = np.zeros((8, 15, 2 * GRID_W), np.float32)
    padded[:, :, 48:79] = a["na_rpb_2"][0]
    first = GRID_W - 1 - np.arange(GRID_W)
    rpb = np.stack([padded[:, :, f:f + GRID_W] for f in first]).reshape(GRID_W, 8, 15 * GRID_W)
    arrays = {
        "vecs": np.concatenate([vec[name] for name, _ in VECS], axis=1), "consts": packed,
        "xT": np.ascontiguousarray(a["x"][0].T), "ctxT": np.ascontiguousarray(a["ctx_2"][0].T),
        "alibi_full": full.astype(ml_dtypes.bfloat16), "alibi_near": near.astype(ml_dtypes.bfloat16),
        "pool_band": band, "rpb": rpb,
        "mod_w": a["mod_w"], "w_in": mixer_columns(a["w_in"][0])[None], "cmp_w1": a["cmp_w1"][0],
        "w_branch": a["w_branch"][0], "w_out": a["w_out"], "exp_w1": a["exp_w1"][0], "exp_w2": a["exp_w2"][0],
        "mod_w_2": a["mod_w_2"], "ffn_w13": a["ffn_w13_2"].reshape(4, D, 2 * FF),
        "ffn_w2": a["ffn_w2_2"].reshape(4, FF, D), "even_w_in": a["even_w_in_2"], "even_w_out": a["even_w_out_2"],
        "conv_w_in": a["conv_w_in_2"], "conv_w_out": a["conv_w_out_2"],
    }
    nc = bacc.Bacc("TRN2", target_bir_lowering=False, num_devices=1, dynamic_dma_scratch_size=1024)
    ins = {}
    for name, v in arrays.items():
        arrays[name] = v = np.ascontiguousarray(v)
        ins[name] = nc.dram_tensor(f"in_{name}", v.shape, mybir.dt.from_np(v.dtype), kind="ExternalInput").ap()
    out = nc.dram_tensor("out_y", (D, T), F32, kind="ExternalOutput").ap()
    build(nc, ins, out)
    r = run_bass_kernel_spmd(nc, [{f"in_{n}": v for n, v in arrays.items()}], core_ids=[0])
    return np.ascontiguousarray(r.results[0]["out_y"].T)[None]
```

```python
from contextlib import ExitStack

import numpy as np

import concourse.bass as bass
from concourse import mybir

ALU = mybir.AluOpType
ACT = mybir.ActivationFunctionType
F32 = mybir.dt.float32
F32R = mybir.dt.float32r
BF16 = mybir.dt.bfloat16
I32 = mybir.dt.int32
AX_X = mybir.AxisListType.X

P = 128
D = 1024
T = 256
DC = D // P
TB = T // P
EPS1, EPS2 = 1e-5, 1e-6
HD = 64
N_EXPERTS, TOP_K = 32, 4
LIMIT, ALPHA = 7.0, 1.702
NCMP = (T - 32) // 16 + 1
LAM_INIT = 0.8 - 0.6 * 1.0
NEG = -1e30
FF = 2816
FC = FF // P
N_MOD = 9
GRID_W, ROWS = 64, T // 64
KW = 16

Z_QA, Z_QC, Z_QB, Z_KB, Z_KA, Z_VA, Z_VB, Z_KCM, Z_VCM, Z_KSL, Z_VSL, Z_KWN, Z_VWN, Z_GATE, Z_MERGE = (
    0, 4, 8, 12, 16, 17, 18, 22, 23, 24, 25, 26, 27, 28, 29)
Z_ALL = Z_MERGE + 3 * DC
Z_V = [Z_VA, Z_VB, Z_VB + 1, Z_VB + 2, Z_VB + 3, Z_VSL, Z_VWN]
Z_PASSES = [(0, 8), (8, 8), (16, 8), (24, 5)]

RING = 12
SLOT = 2 * D
RING2, HIGHS = 8, 4
FFN_PASSES = ((0, 8), (8, 8), (16, 6))
FFNS = [(0, 0), (0, 1), (1, 0), (2, 0), (3, 0)]

CAP = 96
ROUNDS = -(-T // CAP)
PAIRS = N_EXPERTS // 2

VECS = [
    ("c", DC), ("mod_b", 6 * DC), ("norm1", DC), ("norm2", DC), ("b_in", Z_ALL), ("final1", DC),
    ("exp_b1", N_EXPERTS * 2 * DC), ("cmp_pos", 2 * 16), ("cmp_b1", 4),
    ("cmp_b2k", 1), ("cmp_b2v", HD), ("cmp_w2", 4 * P), ("sinks", 8), ("lambda", 4 * HD), ("subln", P),
    ("router_w", DC * N_EXPERTS), ("router_b", N_EXPERTS), ("cond2", 2 * DC), ("mod_b2", 2 * N_MOD * DC),
    ("norm_g2", 2 * 3 * DC), ("pool_w", 4 * P), ("pool_scale", 4), ("conv_w", 3 * DC), ("final2", DC),
]
VEC_AT = {}
_at = 0
for _name, _width in VECS:
    VEC_AT[_name] = (_at, _width)
    _at += _width
VEC_COLS = _at

CONSTS = [("ident", P), ("ones", P), ("before", P), ("iota", P), ("col_mask", GRID_W),
          ("cmp_bias", 2 * 16), ("cmp_valid", 2 * 16)]
CONST_AT = {}
_at = 0
for _name, _width in CONSTS:
    CONST_AT[_name] = (_at, _width)
    _at += _width
CONST_COLS = _at

ATT = [(kind, blk, g) for kind in ("swa", "slc", "win", "diff") for blk in range(TB) for g in range(2)]
NA_STEPS = [(blk, pair) for blk in range(TB) for pair in range(4)]


MODS = [(1, 0, g, 1) for g in range(6)] + [(2, layer, g, 2 if (layer, g) < (0, 5) else 1)
                                           for layer in range(2) for g in range(N_MOD)]
MOD_SUMS = 3
ATT_MOD_SLOTS = [16 * s // len(ATT) for s in range(len(ATT) + 1)]


L1_MODS = 6 + N_MOD

MOE_SLOTS = [("exp_w1", e, k, half) for e in range(2) for half in range(2) for k in range(0, DC, 2)] + \
            [("exp_w2", e, k, 0) for e in range(2) for k in range(0, DC, 2)]
MOE_UNITS = ("gate0", "up0", "gate0_turn", "gate1", "up0_turn", "up1", "gate1_turn", "down0", "up1_turn",
             "gather0", "result0", "result0b", "down1", "gather1", "result1", "result1b")
MU = {name: n for n, name in enumerate(MOE_UNITS)}
TURN_UNITS, TURN_SLOTS, TURN_SIGNALS = len(MOE_UNITS), len(MOE_SLOTS), 18
NEXT_SLOTS = (TURN_SLOTS, TURN_SLOTS + 1, TURN_SLOTS + 2)
MOE_RELEASE = [("units", MU[("gate0", "up0", "gate1", "up1", "down0", "down1")[j // 4]] + 1) if j % 4 == 3
               else ("slots", j // 4 * 3 + j % 4 + 1) for j in range(TURN_SLOTS)]


def mod_unit(n):
    return f"mod{n}"


def mods_ending(lo, hi):
    return [6 + s // 4 for s in range(lo, hi) if s % 4 == 3]


class Plan:

    def __init__(self):
        self.units, self.n_units = {}, 0
        self.slots, self.stream = {}, []
        self.released = {}
        self.n_slot_signals = 0
        self.mod_at, self.n_mod_slots = [], 0
        self.place, self.landing, self.before = [], [], []
        self.since_mods = 0
        self.holder, self.times, self.places = {}, {}, RING
        self.split_at, self.split_no = [], {}
        self.mods_after = {}

    def placed(self):
        while len(self.place) < len(self.stream):
            s = len(self.place)
            self.next = (self.next + 1) % self.places if s else 0
            self.place.append(self.next)
            self.before.append(self.holder.get(self.next))
            self.times[self.next] = self.times.get(self.next, 0) + 1
            self.landing.append(self.times[self.next])
            self.holder[self.next] = s

    def unit(self, name, n=1):
        self.units[name] = self.n_units
        self.n_units += n

    def load(self, name, sources):
        self.slots[name] = len(self.stream)
        self.stream += sources

    def gemm(self, name, tensor, index, k_chunks, col0, cols, n_units, mods_every=0, mods_end=0, split=False):
        self.unit(name, n_units)
        self.slots[name] = []
        before = self.n_mod_slots
        for k in range(0, k_chunks, 2):
            self.slots[name].append(len(self.stream))
            if k + 2 < k_chunks:
                self.n_slot_signals += 1
                self.released[len(self.stream)] = ("slots", self.n_slot_signals)
            else:
                self.released[len(self.stream)] = ("units", self.n_units)
            if split:
                self.split_no[len(self.stream)] = len(self.split_at)
                self.split_at.append(len(self.stream))
            self.stream.append((tensor, index, k, 2, col0, cols))
            self.since_mods += 1
            if self.n_mod_slots < 4 * mods_end and self.since_mods >= mods_every:
                self.mod_slots(1)
                self.since_mods = 0
        self.mods_after[name] = [n for n in range(len(MODS)) if before < 4 * n + 4 <= self.n_mod_slots]
        for n in self.mods_after[name]:
            self.unit(mod_unit(n))

    def mod_slots(self, n):
        for _ in range(n):
            block_, layer, g, _ = MODS[self.n_mod_slots // 4]
            self.mod_at.append(len(self.stream))
            self.n_mod_slots += 1
            self.released[len(self.stream)] = ("mods", self.n_mod_slots)
            k = 2 * ((self.n_mod_slots - 1) % 4)
            self.stream.append(("mod_w" if block_ == 1 else "mod_w_2", layer, k, 2, g * D, D))


def make_plan():
    p = Plan()
    p.mod_slots(8)
    p.unit(mod_unit(0))
    p.unit(mod_unit(1))
    p.unit("norm0")
    for n, (c0, nc_) in enumerate(Z_PASSES):
        p.gemm(f"z{n}", "w_in", 0, DC, c0 * P, nc_ * P, 2, mods_every=1, mods_end=6)
    p.unit("vnat", 2)
    p.load("cmp_w1", [("cmp_w1", kv, 8 * half, 8, 0, 256) for kv in range(2) for half in range(2)])
    p.unit("cmp_hidden")
    for s in range(4):
        p.released[p.slots["cmp_w1"] + s] = ("units", p.n_units)
    p.unit("cmp_kv")
    p.unit("cmp_scores")
    p.unit("cmp_turn", 2)
    p.unit("cmp_out")
    p.unit("scores0")
    for s in range(len(ATT)):
        if s + 1 < len(ATT):
            p.unit(f"scores{s + 1}")
        p.mod_slots(ATT_MOD_SLOTS[s + 1] - ATT_MOD_SLOTS[s])
        p.unit(f"turn{s}")
        p.unit(f"out{s}")
        for n in mods_ending(*ATT_MOD_SLOTS[s:s + 2]):
            p.unit(mod_unit(n))
    p.unit("branch_turn", 3)
    for b in range(3):
        p.gemm(f"merge{b}", "w_in", 0, DC, (Z_MERGE + b * DC) * P, D, 2, mods_every=1, mods_end=L1_MODS)
        p.gemm(f"branch{b}", "w_branch", b, 4, 0, D, 2, mods_every=1, mods_end=L1_MODS)
    p.gemm("w_out", "w_out", 0, DC, 0, D, 2, mods_every=1, mods_end=L1_MODS)
    assert p.n_mod_slots == 4 * L1_MODS
    p.unit("norm1")
    p.unit("h_turn", 2)
    p.unit("logits")
    p.unit("positions")
    p.unit("gate_turn")
    p.unit("bias_sum", 2)
    p.pads = []
    while p.n_units % 4 != 2:
        p.pads.append(f"pad{len(p.pads)}")
        p.unit(p.pads[-1])
    p.unit("gather", 2)
    p.placed()
    p.high_before = [p.holder[RING2 + m] for m in range(HIGHS)]
    p.places, p.next = RING2, RING2 - 1
    p.moe_unit, p.moe_slot, p.moe_signals = p.n_units, len(p.stream), p.n_slot_signals
    p.n_units += TURN_UNITS * PAIRS
    p.stream += [None] * (TURN_SLOTS * PAIRS)
    p.n_slot_signals += TURN_SIGNALS * PAIRS
    for j in range(TURN_SLOTS):
        kind, n = MOE_RELEASE[j]
        base = p.moe_unit + TURN_UNITS * (PAIRS - 1) if kind == "units" else p.moe_signals + TURN_SIGNALS * (PAIRS - 1)
        p.released[len(p.stream) - TURN_SLOTS + j] = (kind, base + n)
    p.placed()
    p.unit("norm2")
    p.unit("norm3")
    for e, (f, _) in enumerate(FFNS):
        if e >= 2:
            p.unit(f"norm{(7, 8, 10)[e - 2]}")
            p.since_mods = -2
        for ab in range(2):
            for n, (c0, nc_) in enumerate(FFN_PASSES):
                p.gemm(f"ffn{e}_{'ab'[ab]}{n}", "ffn_w13", f, DC, ab * FF + c0 * P, nc_ * P, 2,
                       mods_every=3, mods_end=len(MODS), split=True)
        if e < 2:
            p.unit(f"norm{4 + e}")
        p.gemm(f"ffn{e}_out", "ffn_w2", f, FC, 0, D, 2, mods_every=3, mods_end=len(MODS), split=True)
        assert e < 3 or p.n_mod_slots == 4 * len(MODS)
        if e == 1:
            p.gemm("even_qk", "even_w_in", 0, DC, 0, D, 2, split=True)
            p.gemm("even_vu", "even_w_in", 0, DC, D, D, 2, split=True)
            p.unit("norm6")
            p.gemm("even_ctx", "even_w_in", 0, DC, 512, D, 2, split=True)
            p.unit("na_vturn", 2)
            p.unit("pool_map")
            p.unit("pool_out")
            p.unit("na_scores0")
            for s in range(len(NA_STEPS)):
                if s + 1 < len(NA_STEPS):
                    p.unit(f"na_scores{s + 1}")
                p.unit(f"na_turn{s}")
                p.unit(f"na_out{s}")
            p.unit("na_oturn")
            p.gemm("even_out", "even_w_out", 0, DC, 0, D, 2)
        if e == 3:
            p.unit("norm9")
            for n in range(3):
                p.gemm(f"conv{n}", "conv_w_in", 0, DC, n * D, D, 2, split=True)
            p.gemm("conv_out", "conv_w_out", 0, DC, 0, D, 2)
    p.unit("norm11")
    p.placed()
    return p


def mod_buffers():
    at, holder, buffers, earlier = 0, [None] * MOD_SUMS, [], []
    for n, (_, _, _, conds) in enumerate(MODS):
        mine = [(at + c) % MOD_SUMS for c in range(conds)]
        buffers.append(mine)
        earlier.append([holder[b] for b in mine])
        for b in mine:
            holder[b] = n
        at += conds
    return buffers, earlier


MOD_BUFFERS, MOD_BUFFER_BEFORE = mod_buffers()
PLAN = make_plan()
U = PLAN.units
N_NORMS = 12
NORM_AFTER = {5: "ffn0_out", 7: "even_out", 8: "ffn2_out", 9: "ffn3_out", 10: "conv_out", 11: "ffn4_out"}
PLAIN_NORMS = (0, 1, 2, N_NORMS - 1)
H_PARTS = 4


def squares_before(n):
    return sum(2 if m in NORM_AFTER else 1 for m in range(n))


class Steps:

    def __init__(self, eng, sem):
        self.eng, self.sem, self.n, self.per_turn, self.turn, self.first = eng, sem, 0, 0, None, 0

    def done(self, ins):
        ins.then_inc(self.sem, 1)
        self.n += 1

    def settle(self):
        self.eng.wait_ge(self.sem, self.n if self.turn is None else self.turn * self.per_turn + self.n)

    def link(self, ins):
        self.done(ins)
        self.settle()

    def enter(self, turn, per_turn):
        self.turn, self.per_turn, self.first = turn, per_turn, self.n

    def leave(self, turns):
        assert self.n - self.first == self.per_turn, (self.n - self.first, self.per_turn)
        self.n, self.turn = self.first + turns * self.per_turn, None


def build(nc, ins, out):
    with ExitStack() as ctx:
        def sb(name, shape, dt=F32):
            return ctx.enter_context(nc.sbuf_tensor(name, shape, dt))

        sems = {}

        def sem(name):
            if name not in sems:
                sems[name] = ctx.enter_context(nc.semaphore(name))
            return sems[name]

        def sb_at(name, shape, dt, offset):
            return nc.alloc_sbuf_tensor_at(name, shape, dt, offset=offset)

        ring_at = -(-nc.sbuf_base // 32) * 32
        ring = sb("ring", [P, RING, SLOT])
        vecs = sb("vecs", [P, VEC_COLS])
        consts = sb("consts", [P, CONST_COLS])
        xT = sb("xT", [P, DC, T])
        hT_at = -(-nc.sbuf_base // 32) * 32
        hT = sb("hT", [P, DC, T])
        rstd = sb("rstd", [P, 2, T])
        cs = sb("cs", [P, DC])
        cs2 = sb("cs2", [P, DC, 2])
        mod1 = sb("mod1", [P, 6, DC])
        mod2 = sb("mod2", [P, 2, N_MOD, DC, 2])
        mod_sums = sb("mod_sums", [P, MOD_SUMS, D])
        stats = sb("stats", [P, 4, len(ATT), 4])
        small = sb("small", [P, 512])
        count_max = sb("count_max", [P, 1], I32)
        ARENA = 19456
        arena_at = -(-nc.sbuf_base // 32) * 32
        arena = sb("arena", [P, ARENA])
        psum = ctx.enter_context(nc.psum_tensor("psum", [P, 4, 1024], F32))

        def vec(name, *dims):
            at, width = VEC_AT[name]
            v = vecs[:, at:at + width]
            return v

        def const(name):
            at, width = CONST_AT[name]
            return consts[:, at:at + width]

        ident, ones, before = const("ident"), const("ones"), const("before")

        def area(at, *dims):
            n = int(np.prod(dims))
            assert at + n <= ARENA, (at, n)
            v = arena[:, at:at + n]
            if len(dims) == 2:
                v = v.rearrange("p (a b) -> p a b", a=dims[0])
            if len(dims) == 3:
                v = v.rearrange("p (a b c) -> p a b c", a=dims[0], b=dims[1])
            return v

        zT = area(0, 29, T)
        vnat = area(7424, TB, 7 * P)
        alibi_full = area(9216, 1024).bitcast(BF16).rearrange("p (h k) -> p h k", h=8)
        alibi_near = area(10240, 1024).bitcast(BF16).rearrange("p (h k) -> p h k", h=8)
        o_nat = area(13312, TB, 3, 512)
        probs = area(16384, 2, 1024)
        probsT = area(18432, 1024)
        blocks = area(13312, 2, 16 * 32)
        cmpP = area(14336, TB * 8, 16)
        cmpPT = area(16384, 2048)
        gm = area(0, 3 * DC, T)
        oT = area(9216, 12, T)
        merged = area(13312, DC, T)
        merge_tmp = area(15360, 4, T)
        cT = area(0, DC, T)
        acc = area(2048, DC, T)
        h_nat = area(4096, TB, D)
        moe = {}
        at = 6144
        for name, n in (("xg_high", 2 * DC * CAP), ("xg_low", 2 * DC * CAP), ("hid_high", DC * CAP),
                        ("hid_low", DC * CAP), ("gate", DC * CAP), ("up", DC * CAP), ("sig", DC * CAP),
                        ("gate_rows", D), ("up_rows", D), ("y_rows0", D), ("y_rows1", D), ("selT0", T), ("selT1", T),
                        ("sel", 2 * TB * CAP), ("selG", 2 * TB * CAP)):
            moe[name] = (at, n)
            at += n
        assert at <= ARENA

        def moe_buf(key, a=None):
            at_, n = moe[key]
            return area(at_, n) if a is None else area(at_, a, n // a)

        gateT, b2_rows = moe_buf("selT0"), moe_buf("y_rows0")

        hm = area(4096, FC, T)
        rpb = area(15360, TB * 8, T)
        z2q, z2k, z2v, z2u = area(4096, 4, T), area(5120, 4, 2 * T), area(7168, 4, 2 * T), area(9216, 4, T)
        vnat2 = area(10240, 4, 512)
        pool_band = area(12288, TB, 4, T)
        cat = area(7168, DC, T)
        na_probs = area(0, 2, 512)
        na_probsT = area(1024, 1024)
        pool_mapped = area(2048, TB, 512)
        na_o = area(3072, TB, 512)
        conv_b, conv_c, conv_y = area(4096, DC, T), area(6144, DC, T), area(8192, DC, T)
        conv_z = area(10240, DC, T + 2)

        def parts_at(key, cols):
            return sb_at(key, [P, DC, cols], F32R, arena_at + 4 * moe[key][0])

        xg_high, xg_low = parts_at("xg_high", 2 * CAP), parts_at("xg_low", 2 * CAP)
        hid_high, hid_low = parts_at("hid_high", CAP), parts_at("hid_low", CAP)

        w_low = sb_at("w_low", [P, RING2, SLOT], F32R, ring_at)
        w_high = sb_at("w_high", [P, HIGHS, SLOT], F32R, ring_at + 4 * RING2 * SLOT)
        h_low = sb_at("h_low", [P, DC, T], F32R, hT_at)
        h_high = sb_at("h_high", [P, DC, T], F32R, arena_at + 4 * 2048)
        m_low = sb_at("m_low", [P, FC, T], F32R, arena_at + 4 * 4096)
        m_high = sb_at("m_high", [P, FC, T], F32R, arena_at + 4 * (4096 + FC * T))

        landed = [sem(f"slot_landed{i}") for i in range(RING)]
        slots_used = sem("slots_used")
        psum_full = sem("psum_full")
        psum_free = [sem(f"psum_free{i}") for i in range(4)]
        dve_steps = sem("dve_steps")

        def unit(u):
            return psum[:, u % 4, :]

        def open_unit(pe, u, turn=None, per_turn=0, free=None):
            n = u // 4
            if turn is not None:
                pe.wait_ge((free or psum_free)[u % 4], turn * (per_turn // 4) + n)
            elif n:
                pe.wait_ge((free or psum_free)[u % 4], n)

        def await_unit(eng, u, turn=None, per_turn=0, full=None):
            eng.wait_ge(full or psum_full, u + 1 if turn is None else turn * per_turn + (u + 1))

        def await_freed(eng, u, turn=None, per_turn=0, free=None):
            n = u // 4 + 1
            eng.wait_ge((free or psum_free)[u % 4], n if turn is None else turn * (per_turn // 4) + n)

        def await_slot(pe, s):
            pe.wait_ge(landed[PLAN.place[s]], 16 * PLAN.landing[s])

        def await_release(eng, s):
            kind, n = PLAN.released[s]
            eng.wait_ge({"slots": slots_used, "units": psum_full, "mods": sem("mod_slots_used")}[kind], n)

        def slot_ap(s, rows=2, cols=D):
            return ring[:, PLAN.place[s], 0:rows * cols].rearrange("p (k n) -> p k n", k=rows)

        def high_ap(m, cols):
            return w_high[:, m % HIGHS, 0:2 * cols].rearrange("p (k n) -> p k n", k=2)

        def low_ap(s, cols):
            return w_low[:, PLAN.place[s], 0:2 * cols].rearrange("p (k n) -> p k n", k=2)

        def ahead_of(name):
            last = PLAN.slots[name][-1]
            later = [s for s in PLAN.split_at if s > last][:HIGHS]
            return (later[-1] if later else last) + 1

        def four_chunks(bank_pair, per_bank, cols):
            v = bank_pair.rearrange("p (b n) -> p b n", b=2)[:, :, 0:per_bank * cols]
            return v.rearrange("p b (k n) -> p b k n", k=per_bank)

        def banked(ap, per_bank):
            return ap.rearrange("p (b k) n -> p b k n", k=per_bank)

        def source(entry):
            name, index, k0, rows, c0, cols = entry
            t = ins[name][index]
            return t.rearrange("(k p) n -> p k n", p=P)[:, k0:k0 + rows, c0:c0 + cols]

        moe_end = PLAN.moe_slot + TURN_SLOTS * PAIRS
        block = ctx.enter_context(nc.Block())

        class Turn:

            def __init__(self, turn, pair, units_turn, units_per, gathers, x):
                self.turn, self.pair, self.units_turn, self.units_per = turn, pair, units_turn, units_per
                self.gathers, self.x = gathers, x
                self.u0, self.signals = (PLAN.moe_unit, PLAN.moe_signals) if not x else (X_UNITS + 4, TURN_SIGNALS)
                self.full, self.used, self.free = (psum_full, slots_used, psum_free) if not x else \
                    (full_x, used_x, free_x)

            def unit(self, name):
                return unit(self.u0 + MU[name])

            def await_unit(self, eng, name):
                await_unit(eng, self.u0 + MU[name], self.units_turn, self.units_per, self.full)

            def await_freed(self, eng, name):
                await_freed(eng, self.u0 + MU[name], self.units_turn, self.units_per, self.free)

            def open_unit(self, eng, name):
                open_unit(eng, self.u0 + MU[name], self.units_turn, self.units_per, self.free)

            def free_unit(self, ins_, name):
                ins_.then_inc(self.free[(self.u0 + MU[name]) % 4], 1)

            def await_used(self, eng, j):
                kind, n = MOE_RELEASE[j % TURN_SLOTS]
                if kind == "units":
                    n = self.u0 + n - (TURN_UNITS if j < 0 else 0)
                    eng.wait_ge(self.full, self.units_turn * self.units_per + n)
                else:
                    n = self.signals + n - (TURN_SIGNALS if j < 0 else 0)
                    eng.wait_ge(self.used, self.turn * TURN_SIGNALS + n)

            def await_slot(self, eng, j):
                place = PLAN.place[PLAN.moe_slot + j]
                times = j // RING2 + 1 if self.x else PLAN.landing[PLAN.moe_slot + j]
                eng.wait_ge((landed_x if self.x else landed)[place],
                            self.turn * (16 * TURN_SLOTS // RING2) + 16 * times)

        def first_turn(i):
            return Turn(i, i, i, TURN_UNITS, i, "")

        def x_turn(r, i):
            turn = r * PAIRS + i
            return Turn(turn, i, turn * 4 + r, 4, r * (PAIRS + 1) + i, "_x")

        def load_pair(sp, c, before_turn=None):
            for j, (name, e, k, half) in enumerate(MOE_SLOTS):
                if j < RING2 and before_turn:
                    before_turn(j)
                else:
                    c.await_used(sp, j - RING2)
                src = ins[name][c.pair * 2 + e].rearrange("(k p) n -> p k n", p=P)[:, k:k + 2, half * D:(half + 1) * D]
                place = PLAN.place[PLAN.moe_slot + j]
                sp.dma_start(slot_ap(PLAN.moe_slot + j), src).then_inc((landed_x if c.x else landed)[place], 16)

        def rounds_loop(eng, before_pairs, body):
            with eng.Fori(0, ROUNDS - 1) as r:
                if before_pairs:
                    before_pairs(r)
                with eng.Fori(0, PAIRS - 1) as i:
                    body(x_turn(r, i))
                body(x_turn(r, PAIRS - 1), last=True)

        full_x, used_x = sem("psum_full_x"), sem("slots_used_x")
        free_x = [sem(f"psum_free_x{i}") for i in range(4)]
        landed_x = [sem(f"slot_landed_x{i}") for i in range(RING2)]
        X_UNITS = TURN_UNITS

        def many(eng):
            eng.wait_ge(sem("count_ready"), 1)
            return eng.value_load(count_max[0:1, 0:1], min_val=0, max_val=T)

        @block.sync
        def _(sp):
            def stream(s0, s1):
                for s in range(s0, s1):
                    if PLAN.before[s] is not None:
                        await_release(sp, PLAN.before[s])
                    entry = PLAN.stream[s]
                    sp.dma_start(slot_ap(s, entry[3], entry[5]), source(entry)).then_inc(landed[PLAN.place[s]], 16)

            stream(0, PLAN.moe_slot)

            def before_first(j):
                if PLAN.before[PLAN.moe_slot + j] is not None:
                    await_release(sp, PLAN.before[PLAN.moe_slot + j])

            load_pair(sp, first_turn(0), before_first)
            with sp.Fori(1, PAIRS) as i:
                load_pair(sp, first_turn(i))
            with sp.If(many(sp) > CAP):
                sp.wait_ge(psum_full, PLAN.moe_unit + TURN_UNITS * PAIRS)
                rounds_loop(sp, None, lambda c, last=False: load_pair(sp, c))
                sp.wait_ge(full_x, X_UNITS + (4 + TURN_UNITS * PAIRS) * (ROUNDS - 1))
            stream(moe_end, len(PLAN.stream))
            sp.wait_ge(sem("h_ready"), len(PLAIN_NORMS))
            sp.dma_start(out.rearrange("(k p) t -> p k t", p=P), hT[:, :, :]).then_inc(sem("stored"), 16)
            sp.wait_ge(sem("stored"), 16)

        @block.gpsimd
        def _(pool):
            pool.wait_ge(sem("rpb_landed"), 16 * ROWS)
            mask = const("col_mask")[:, None, :].broadcast_to([P, TB * 8 * ROWS, GRID_W])
            view = area(15360, TB * 8 * ROWS, GRID_W)
            pool.tensor_tensor(view, view, mask, ALU.add).then_inc(sem("rpb_masked"), 1)
            pool.wait_ge(sem("x_ready"), 7)
            pool.memset(conv_z[:, :, 0:1], 0.0).then_inc(sem("conv_edges"), 1)
            pool.memset(conv_z[:, :, T + 1:T + 2], 0.0).then_inc(sem("conv_edges"), 1)

        @block.scalar
        def _(act):
            act.dma_start(vecs[:, :], ins["vecs"]).then_inc(sem("vecs_landed"), 16)
            act.dma_start(consts[:, :], ins["consts"]).then_inc(sem("consts_landed"), 16)
            act.dma_start(xT[:, :, :], ins["xT"].rearrange("(k p) t -> p k t", p=P)).then_inc(sem("x_landed"), 16)
            act.dma_start(alibi_full, ins["alibi_full"]).then_inc(sem("alibi_landed"), 16)
            act.dma_start(alibi_near, ins["alibi_near"]).then_inc(sem("alibi_landed"), 16)

            act.wait_ge(sem("vecs_landed"), 16)
            act.activation(cs[:, :], vec("c"), ACT.Silu).then_inc(sem("cond_ready"), 1)
            act.activation(cs2[:, :, :], vec("cond2").rearrange("p (k s) -> p k s", s=2), ACT.Silu).then_inc(
                sem("cond_ready"), 1)

            act.wait_ge(sem("lambda_dots"), 1)
            act.activation(small[:, 412:414], small[:, 410:412], ACT.Exp).then_inc(sem("lambda_exp"), 1)

            def norm(n, src, squares):
                halves = [(slice(0, 4), 0), (slice(4, 8), 1)] if n in NORM_AFTER else [(slice(0, DC), None)]
                for chunks_, half in halves:
                    if half is not None:
                        await_freed(act, U[NORM_AFTER[n]] + half)
                    act.activation(squares[:, chunks_, :], src[:, chunks_, :], ACT.Square).then_inc(
                        sem("squares_ready"), 1)
                await_freed(act, U[f"norm{n}"])
                act.activation(rstd[:, 1, :], rstd[:, 0, :], ACT.Sqrt).then_inc(sem("root_ready"), 1)

            act.wait_ge(sem("x_landed"), 16)
            norm(0, xT[:, :, :], hT[:, :, :])

            for b in range(TB):
                u = U["vnat"] + b
                await_unit(act, u)
                act.activation(vnat[:, b, :], unit(u)[:, 0:7 * P], ACT.Copy)
                act.activation(small[:, 24 * b:24 * b + 24], unit(u)[:, 7 * P:7 * P + 24],
                               ACT.Sigmoid).then_inc(psum_free[u % 4], 1)

            hidden = small[:, 64:192].rearrange("p (m f c) -> p m f c", m=2, f=2)
            cmp_bias = small[:, 192:196]
            act.wait_ge(sem("cmp_bias_ready"), 1)
            for m in range(2):
                for f in range(2):
                    last = act.activation(hidden[:, m, f, 0:2 * NCMP],
                                          unit(U["cmp_hidden"])[:, (2 * m + f) * 32:(2 * m + f) * 32 + 2 * NCMP],
                                          ACT.Gelu_apprx_tanh, bias=cmp_bias[:, 2 * m + f:2 * m + f + 1])
            last.then_inc(psum_free[U["cmp_hidden"] % 4], 1)
            act.wait_ge(sem("cmp_shifted"), 1)
            act.activation(cmpP[:, :, 0:NCMP], cmpP[:, :, 0:NCMP], ACT.Exp).then_inc(sem("cmp_exp"), 1)
            for n in range(2):
                u = U["cmp_turn"] + n
                await_unit(act, u)
                act.activation(cmpPT[0:NCMP, 1024 * n:1024 * n + 1024], unit(u)[0:NCMP, :], ACT.Copy).then_inc(
                    psum_free[u % 4], 1)
            await_unit(act, U["cmp_out"])

            def exps(s):
                kind, blk, g = ATT[s]
                kw = P * (blk + 1)
                u = U[f"scores{s}"]
                act.wait_ge(sem("row_max_ready"), s + 1)
                for j in range(4):
                    src = unit(u)[:, j * T:j * T + kw]
                    last = act.activation(probs[:, s % 2, j * T:j * T + kw], src, ACT.Exp,
                                          bias=stats[:, 1, s, j:j + 1], accum_out=stats[:, 2, s, j:j + 1])
                last.then_inc(psum_free[u % 4], 1)
                if kind == "swa":
                    act.activation(stats[:, 3, s, :], stats[:, 3, s, :], ACT.Exp).then_inc(sem("sink_exp"), 1)

            def turned(s):
                kind, blk, g = ATT[s]
                u = U[f"turn{s}"]
                n = 4 * (blk + 1) * P
                await_unit(act, u)
                act.activation(probsT[:, 0:n], unit(u)[:, 0:n], ACT.Copy).then_inc(psum_free[u % 4], 1)

            exps(0)
            for s in range(len(ATT)):
                if s + 1 < len(ATT):
                    exps(s + 1)
                turned(s)

            act.wait_ge(sem("subln_mean"), 1)
            act.activation(small[:, 400:408], small[:, 400:408], ACT.Sqrt).then_inc(sem("subln_root"), 1)

            for b in range(3):
                u = U["branch_turn"] + b
                await_unit(act, u)
                act.activation(oT[:, 4 * b:4 * b + 4, :], unit(u).rearrange("p (c t) -> p c t", c=4),
                               ACT.Copy).then_inc(psum_free[u % 4], 1)
            for b in range(3):
                for n in range(DC):
                    u = U[f"merge{b}"] + n // 4
                    z = Z_MERGE + b * DC + n
                    await_unit(act, u)
                    last = act.activation(gm[:, b * DC + n, :], unit(u)[:, (n % 4) * T:(n % 4 + 1) * T],
                                          ACT.Sigmoid, bias=vec("b_in")[:, z:z + 1])
                    if n % 4 == 3:
                        last.then_inc(psum_free[u % 4], 1)

            act.wait_ge(sem("x_ready"), 1)
            act.dma_start(cT, ins["ctxT"].rearrange("(k p) t -> p k t", p=P)).then_inc(sem("ctx_landed"), 16)
            act.dma_start(b2_rows[0:N_EXPERTS, :], ins["exp_b2"]).then_inc(sem("b2_landed"), 16)
            norm(1, xT[:, :, :], hT[:, :, :])

            for n in range(2):
                u = U["h_turn"] + n
                await_unit(act, u)
                act.activation(h_nat[:, n, :], unit(u)[:, :], ACT.Copy).then_inc(psum_free[u % 4], 1)
            route = small[:, 0:448]
            for b in range(TB):
                act.wait_ge(sem("top_ready"), b + 1)
                act.activation(route[:, 128 + 32 * b:160 + 32 * b], route[:, 36 * b:36 * b + 32], ACT.Exp,
                               bias=route[:, 88 + b:89 + b]).then_inc(sem("route_exp"), 1)

            u = U["gate_turn"]
            await_unit(act, u)
            act.activation(gateT[0:N_EXPERTS, :], unit(u)[0:N_EXPERTS, 0:T], ACT.Copy).then_inc(psum_free[u % 4], 1)

            def gathered_high(half, src, x):
                act.activation(xg_high[:, 4 * half:4 * half + 4, :], four_chunks(src, 2, 2 * CAP),
                               ACT.Copy).then_inc(sem("xg_high_ready" + x), 1)

            for half in range(2):
                await_unit(act, U["gather"] + half)
                gathered_high(half, unit(U["gather"] + half), "")
            for q in PLAN.high_before:
                await_release(act, q)

            def high(c, *slots):
                for j in slots:
                    c.await_used(act, j - HIGHS)
                    c.await_slot(act, j)
                    act.activation(high_ap(j, D), slot_ap(PLAN.moe_slot + j), ACT.Copy).then_inc(
                        sem("expert_high_ready" + c.x), 1)

            def experts(c, last=False):
                def rows(name, dst):
                    c.await_unit(act, name)
                    c.free_unit(act.activation(moe_buf(dst)[0:CAP, :], c.unit(name)[0:CAP, :], ACT.Copy), name)

                def selection_turned(e):
                    name = f"gate{e}_turn"
                    c.await_unit(act, name)
                    act.activation(moe_buf(f"selT{e}")[0:CAP, :].rearrange("p (b t) -> p b t", b=TB),
                                   c.unit(name)[0:CAP, :].rearrange("p (b t) -> p b t", b=TB)[:, :, 4 * CAP:4 * CAP + P],
                                   ACT.Copy).then_inc(sem("selT_ready" + c.x), 1)

                def sigmoid(e):
                    act.wait_ge(sem("gate_clamped" + c.x), c.turn * 2 + (e + 1))
                    act.activation(moe_buf("sig"), moe_buf("gate"), ACT.Sigmoid, scale=ALPHA).then_inc(
                        sem("gate_sigmoid" + c.x), 1)

                high(c, 3, 4, 5, 6)
                rows("gate0", "gate_rows")
                high(c, 7, 8, 9, 10)
                rows("up0", "up_rows")
                selection_turned(0)
                high(c, 11)
                sigmoid(0)
                high(c, 12, 13, 14)
                rows("gate1", "gate_rows")
                high(c, 15, 16, 17, 18)
                rows("up1", "up_rows")
                high(c, 19)
                selection_turned(1)
                sigmoid(1)
                high(c, 20, 21, 22)
                rows("down0", "y_rows0")
                high(c, 23)
                c.await_unit(act, "gather0")
                gathered_high(0, c.unit("gather0"), c.x)
                if not last:
                    high(c, *NEXT_SLOTS)
                rows("down1", "y_rows1")
                c.await_unit(act, "gather1")
                gathered_high(1, c.unit("gather1"), c.x)

            high(first_turn(0), 0, 1, 2)
            with act.Fori(0, PAIRS - 1) as i:
                experts(first_turn(i))
            experts(first_turn(PAIRS - 1), last=True)
            with act.If(many(act) > CAP):
                act.wait_ge(psum_full, PLAN.moe_unit + TURN_UNITS * PAIRS)

                def before_pairs(r):
                    for half in range(2):
                        await_unit(act, X_UNITS + half, r * (4 * PAIRS + 1), 4, full_x)
                        gathered_high(half, unit(X_UNITS + half), "_x")
                    high(x_turn(r, 0), 0, 1, 2)
                rounds_loop(act, before_pairs, experts)

            act.wait_ge(sem("x_ready"), 2)
            for r in range(ROWS):
                half, blk = r % 2, r // 2
                act.dma_start(rpb[64 * half:64 * half + 64, 8 * blk:8 * blk + 8, :],
                              ins["rpb"][:, :, (7 - r) * GRID_W:(7 - r + ROWS) * GRID_W]).then_inc(
                    sem("rpb_landed"), 16)
            norm(2, xT[:, :, :], hT[:, :, :])

            highs = [0]

            def high_parts(until):
                while highs[0] < len(PLAN.split_at) and PLAN.split_at[highs[0]] < until:
                    m = highs[0]
                    s = PLAN.split_at[m]
                    cols = PLAN.stream[s][5]
                    if m < HIGHS:
                        await_release(act, moe_end - HIGHS + m)
                    else:
                        await_release(act, PLAN.split_at[m - HIGHS])
                    await_slot(act, s)
                    act.activation(high_ap(m, cols), slot_ap(s, 2, cols), ACT.Copy).then_inc(sem("w_high_ready"), 1)
                    highs[0] += 1

            def split_h(n):
                for part in range(H_PARTS):
                    act.wait_ge(sem("h_whole"), H_PARTS * (n - 3) + part + 1)
                    act.activation(h_high[:, 2 * part:2 * part + 2, :], hT[:, 2 * part:2 * part + 2, :],
                                   ACT.Copy).then_inc(sem("h_high_ready"), 1)

            def ffn(e, before_out=None):
                for n, (c0, nc_) in enumerate(FFN_PASSES):
                    name = f"ffn{e}_a{n}"
                    high_parts(ahead_of(name))
                    for half in range(2):
                        u = U[name] + half
                        k = min(4, nc_ - 4 * half)
                        await_unit(act, u)
                        act.activation(hm[:, c0 + 4 * half:c0 + 4 * half + k, :],
                                       unit(u)[:, 0:k * T].rearrange("p (c t) -> p c t", c=k),
                                       ACT.Silu).then_inc(psum_free[u % 4], 1)
                for n, (c0, nc_) in enumerate(FFN_PASSES):
                    name = f"ffn{e}_b{n}"
                    high_parts(ahead_of(name))
                    for half in range(2):
                        k = min(4, nc_ - 4 * half)
                        c = c0 + 4 * half
                        await_freed(act, U[name] + half)
                        act.activation(m_high[:, c:c + k, :], hm[:, c:c + k, :], ACT.Copy).then_inc(
                            sem("m_high_ready"), 1)
                if before_out:
                    before_out()
                high_parts(ahead_of(f"ffn{e}_out"))

            high_parts(PLAN.split_at[HIGHS])
            act.wait_ge(sem("h_ready"), 3)
            norm(3, xT[:, :, :], hT[:, :, :])
            split_h(3)

            def norm_ctx():
                act.wait_ge(sem("ctx_landed"), 16)
                norm(4, cT, hT[:, :, :])
                split_h(4)

            def norm_tokens():
                norm(5, xT[:, :, :], hT[:, :, :])
                split_h(5)

            ffn(0, norm_ctx)
            ffn(1, norm_tokens)
            def projected(name, *parts):
                high_parts(ahead_of(name))
                for half, (dst, scale) in enumerate(parts):
                    u = U[name] + half
                    await_unit(act, u)
                    act.activation(dst, unit(u).rearrange("p (c t) -> p c t", c=4), ACT.Copy, scale=scale).then_inc(
                        psum_free[u % 4], 1)

            projected("even_qk", (z2q, HD ** -0.5), (z2k[:, :, 0:T], 1.0))
            projected("even_vu", (z2v[:, :, 0:T], 1.0), (z2u, 1.0))
            act.wait_ge(sem("x_ready"), 4)
            act.dma_start(pool_band, ins["pool_band"]).then_inc(sem("band_landed"), 16)
            norm(6, cT, hT[:, :, :])
            split_h(6)
            projected("even_ctx", (z2k[:, :, T:2 * T], 1.0), (z2v[:, :, T:2 * T], 1.0))
            for n in range(2):
                u = U["na_vturn"] + n
                await_unit(act, u)
                act.activation(vnat2[:, 2 * n:2 * n + 2, :], unit(u).rearrange("p (b c) -> p b c", b=2),
                               ACT.Copy).then_inc(psum_free[u % 4], 1)
            u = U["pool_map"]
            await_unit(act, u)
            act.activation(pool_mapped, unit(u).rearrange("p (b c) -> p b c", b=2), ACT.Copy).then_inc(
                psum_free[u % 4], 1)

            def na_exps(s):
                u = U[f"na_scores{s}"]
                act.wait_ge(sem("na_max_ready"), s + 1)
                if s >= 1:
                    await_unit(act, U[f"na_turn{s - 1}"])
                for j in range(2):
                    last = act.activation(na_probs[:, j, :], unit(u)[:, 512 * j:512 * j + 512], ACT.Exp,
                                          bias=stats[:, 1, s, j:j + 1], accum_out=stats[:, 2, s, j:j + 1])
                last.then_inc(psum_free[u % 4], 1)

            def na_turned(s):
                u = U[f"na_turn{s}"]
                await_unit(act, u)
                act.activation(na_probsT, unit(u), ACT.Copy).then_inc(psum_free[u % 4], 1)

            na_exps(0)
            for s in range(len(NA_STEPS)):
                na_turned(s)
                if s + 1 < len(NA_STEPS):
                    na_exps(s + 1)
            u = U["na_oturn"]
            await_unit(act, u)
            act.activation(cat[:, 0:4, :], unit(u).rearrange("p (c t) -> p c t", c=4), ACT.Copy).then_inc(
                psum_free[u % 4], 1)
            for n, e in ((7, 2), (8, 3)):
                norm(n, xT[:, :, :], hT[:, :, :])
                split_h(n)
                ffn(e)
            norm(9, xT[:, :, :], hT[:, :, :])
            split_h(9)
            for n, dst in enumerate((conv_b, conv_c)):
                projected(f"conv{n}", (dst[:, 0:4, :], 1.0), (dst[:, 4:8, :], 1.0))
            high_parts(ahead_of("conv2"))
            norm(10, xT[:, :, :], hT[:, :, :])
            split_h(10)
            ffn(4)
            norm(11, xT[:, :, :], hT[:, :, :])

        @block.tensor
        def _(pe):
            def gemm(name, k_chunks, n_chunks, operands, parts_ready=None):
                slots, u0 = PLAN.slots[name], U[name]
                n_units = sum(-(-n // 4) for _, _, n in operands)
                for u in range(n_units):
                    open_unit(pe, u0 + u)
                for k in range(k_chunks):
                    s = slots[k // 2]
                    if parts_ready and k % 2 == 0:
                        parts_ready(k)
                    if k % 2 == 0:
                        await_slot(pe, s)
                    w = slot_ap(s, 2, n_chunks * P)
                    u = u0
                    for rhs, c0, n in operands:
                        for j in range(n):
                            mm = pe.matmul(unit(u + j // 4)[:, (j % 4) * T:(j % 4 + 1) * T],
                                           w[:, k % 2, (c0 + j) * P:(c0 + j + 1) * P], rhs(k),
                                           start=(k == 0 and j % 2 == 0), stop=(k == k_chunks - 1),
                                           skip_group_check=True)
                            if k == k_chunks - 1 and (j % 4 == 3 or j == n - 1):
                                mm.then_inc(psum_full, 1)
                        u += -(-n // 4)
                    if k % 2 == 1 and k != k_chunks - 1:
                        mm.then_inc(slots_used, 1)

            def split_gemm(name, k_chunks, n_chunks, high, low, parts_ready=None, halves_last=False):
                slots, u0 = PLAN.slots[name], U[name]

                def products(k, half):
                    s = slots[k // 2]
                    wh, wl = high_ap(PLAN.split_no[s], n_chunks * P), low_ap(s, n_chunks * P)
                    for j in range(4 * half, min(4 * half + 4, n_chunks)):
                        dst = unit(u0 + half)[:, (j % 4) * T:(j % 4 + 1) * T]
                        cols = slice(j * P, (j + 1) * P)
                        first, last = k == 0 and j % 2 == 0, k == k_chunks - 1
                        pe.matmul(dst, wh[:, k % 2, cols], high[:, k, :], start=first, stop=False,
                                  skip_group_check=True)
                        pe.matmul(dst, wh[:, k % 2, cols], low[:, k, :], start=False, stop=False,
                                  skip_group_check=True)
                        mm = pe.matmul(dst, wl[:, k % 2, cols], high[:, k, :], start=False, stop=last,
                                       skip_group_check=True)
                    if last:
                        mm.then_inc(psum_full, 1)
                    if half == 1 and k % 2 == 1 and not last:
                        mm.then_inc(slots_used, 1)

                def await_parts(k):
                    if k % 2 == 0:
                        pe.wait_ge(sem("w_split"), PLAN.split_no[slots[k // 2]] + 1)
                        if parts_ready:
                            parts_ready(k)

                for half in range(2):
                    open_unit(pe, u0 + half)
                together = k_chunks - 4 if halves_last else k_chunks
                for k in range(together):
                    await_parts(k)
                    for half in range(2):
                        products(k, half)
                for half in range(2):
                    for k in range(together, k_chunks):
                        if half == 0:
                            await_parts(k)
                        products(k, half)

            def after_norm(n):
                return lambda k: pe.wait_ge(sem("h_parts"), H_PARTS * (n - 3) + k // 2 + 1)

            def mod_sum(n):
                conds = MODS[n][3]
                u = U[mod_unit(n)]
                pe.wait_ge(sem("mod_partials"), n + 1)
                open_unit(pe, u)
                for c in range(conds):
                    for j in range(DC):
                        at = j * conds + c
                        mm = pe.matmul(unit(u)[:, at:at + 1], mod_sums[:, MOD_BUFFERS[n][c], j * P:(j + 1) * P],
                                       ones[:, 0:1], start=True, stop=True)
                mm.then_inc(psum_full, 1)

            def mod_sums_of(name):
                for n in PLAN.mods_after[name]:
                    mod_sum(n)

            def norm(n, squares):
                u = U[f"norm{n}"]
                open_unit(pe, u)
                for k in range(DC):
                    if k == 0 or (k == 4 and n in NORM_AFTER):
                        pe.wait_ge(sem("squares_ready"), squares_before(n) + k // 4 + 1)
                    mm = pe.matmul(unit(u)[:, 0:T], ones, squares[:, k, :], start=(k == 0), stop=(k == DC - 1))
                mm.then_inc(psum_full, 1)

            def h_rhs(k):
                return hT[:, k, :]

            pe.wait_ge(sem("consts_landed"), 16)
            mod_sum(0)
            mod_sum(1)
            norm(0, hT)
            pe.wait_ge(sem("h_ready"), 1)
            for n, (c0, nc_) in enumerate(Z_PASSES):
                gemm(f"z{n}", DC, nc_, [(h_rhs, 0, nc_)])
                mod_sum(2 + n)
            pe.wait_ge(sem("z_ready"), len(Z_PASSES))
            for b in range(TB):
                u = U["vnat"] + b
                open_unit(pe, u)
                for n, z in enumerate(Z_V + [Z_GATE]):
                    mm = pe.transpose(unit(u)[:, n * P:(n + 1) * P], zT[:, z, b * P:(b + 1) * P], ident)
                mm.then_inc(psum_full, 1)
            pe.wait_ge(sem("blocks_ready"), 1)
            u = U["cmp_hidden"]
            open_unit(pe, u)
            for m in range(2):
                for half in range(2):
                    await_slot(pe, PLAN.slots["cmp_w1"] + 2 * m + half)
                for f in range(2):
                    for j in range(16):
                        w = slot_ap(PLAN.slots["cmp_w1"] + 2 * m + j // 8, 8, 256)
                        mm = pe.matmul(unit(u)[:, (2 * m + f) * 32:(2 * m + f) * 32 + 31],
                                       w[:, j % 8, f * P:(f + 1) * P],
                                       blocks[:, m, j * 32:j * 32 + 31], start=(j == 0), stop=(j == 15))
            mm.then_inc(psum_full, 1)
            hidden = small[:, 64:192].rearrange("p (m f c) -> p m f c", m=2, f=2)
            w2 = vec("cmp_w2").rearrange("p (m f c) -> p m f c", m=2, f=2)
            await_freed(pe, U["cmp_hidden"])
            u = U["cmp_kv"]
            open_unit(pe, u)
            for f in range(2):
                pe.matmul(unit(u)[:, 0:2 * NCMP], w2[:, 0, f, :], hidden[:, 0, f, 0:2 * NCMP],
                          start=(f == 0), stop=(f == 1))
            for g in range(2):
                for f in range(2):
                    mm = pe.matmul(unit(u)[0:NCMP, 512 + g * HD:512 + (g + 1) * HD],
                                   hidden[:, 1, f, g * NCMP:(g + 1) * NCMP], w2[:, 1, f, 0:HD],
                                   start=(f == 0), stop=(f == 1))
            mm.then_inc(psum_full, 1)
            kcT, vc = small[:, 200:230], small[:, 232:360]
            await_freed(pe, U["cmp_kv"])
            u = U["cmp_scores"]
            open_unit(pe, u)
            for b in range(TB):
                for g in range(2):
                    rows = slice(64 * g, 64 * g + 64)
                    for j in range(4):
                        at = 512 * g + (b * 4 + j) * 16
                        mm = pe.matmul(unit(u)[:, at:at + NCMP], zT[rows, Z_QC + j, b * P:(b + 1) * P],
                                       kcT[rows, g * NCMP:(g + 1) * NCMP], start=True, stop=True)
            mm.then_inc(psum_full, 1)
            pe.wait_ge(sem("cmp_probs"), 1)
            for b in range(TB):
                u = U["cmp_turn"] + b
                open_unit(pe, u)
                for h in range(8):
                    mm = pe.transpose(unit(u)[0:NCMP, h * P:(h + 1) * P], cmpP[:, b * 8 + h, 0:NCMP], ident)
                mm.then_inc(psum_full, 1)
            u = U["cmp_out"]
            open_unit(pe, u)
            for b in range(TB):
                await_freed(pe, U["cmp_turn"] + b)
                for h in range(8):
                    g = h // 4
                    mm = pe.matmul(unit(u)[:, b * 512 + h * HD:b * 512 + (h + 1) * HD],
                                   cmpPT[0:NCMP, (b * 8 + h) * P:(b * 8 + h + 1) * P],
                                   vc[0:NCMP, g * HD:(g + 1) * HD], start=True, stop=True)
            mm.then_inc(psum_full, 1)

            def scores(s):
                kind, blk, g = ATT[s]
                u = U[f"scores{s}"]
                rows = slice(64 * g, 64 * g + 64)
                open_unit(pe, u)
                for j in range(4):
                    qz, kz = {"swa": (Z_QA + j, Z_KA), "slc": (Z_QC + j, Z_KSL), "win": (Z_QC + j, Z_KWN),
                              "diff": (Z_QB + j, Z_KB + j)}[kind]
                    mm = pe.matmul(unit(u)[:, j * T:j * T + P * (blk + 1)], zT[rows, qz, blk * P:(blk + 1) * P],
                                   zT[rows, kz, 0:P * (blk + 1)], start=True, stop=True)
                mm.then_inc(psum_full, 1)

            def turn_and_apply(s):
                kind, blk, g = ATT[s]
                nb = blk + 1
                u = U[f"turn{s}"]
                await_freed(pe, U[f"scores{s}"])
                open_unit(pe, u)
                for j in range(4):
                    for kb in range(nb):
                        mm = pe.transpose(unit(u)[:, (j * nb + kb) * P:(j * nb + kb + 1) * P],
                                          probs[:, s % 2, j * T + kb * P:j * T + (kb + 1) * P], ident)
                mm.then_inc(psum_full, 1)
                await_freed(pe, u)
                u = U[f"out{s}"]
                open_unit(pe, u)
                dv = P if kind == "diff" else HD
                for j in range(4):
                    col = {"swa": HD * g, "slc": 5 * P + HD * g, "win": 6 * P + HD * g, "diff": P * (1 + j)}[kind]
                    for kb in range(nb):
                        mm = pe.matmul(unit(u)[:, j * dv:(j + 1) * dv], probsT[:, (j * nb + kb) * P:(j * nb + kb + 1) * P],
                                       vnat[:, kb, col:col + dv], start=(kb == 0), stop=(kb == nb - 1))
                mm.then_inc(psum_full, 1)

            scores(0)
            for s in range(len(ATT)):
                if s + 1 < len(ATT):
                    scores(s + 1)
                turn_and_apply(s)
                for n in mods_ending(*ATT_MOD_SLOTS[s:s + 2]):
                    mod_sum(n)
            pe.wait_ge(sem("branches_ready"), 1)
            for br in range(3):
                u = U["branch_turn"] + br
                open_unit(pe, u)
                for c in range(4):
                    for b in range(TB):
                        mm = pe.transpose(unit(u)[:, c * T + b * P:c * T + (b + 1) * P],
                                          o_nat[:, b, br, c * P:(c + 1) * P], ident)
                mm.then_inc(psum_full, 1)
            for br in range(3):
                gemm(f"merge{br}", DC, DC, [(h_rhs, 0, DC)])
                mod_sums_of(f"merge{br}")
                await_freed(pe, U["branch_turn"] + br)
                gemm(f"branch{br}", 4, DC, [(lambda k, br=br: oT[:, 4 * br + k, :], 0, DC)])
                mod_sums_of(f"branch{br}")
            pe.wait_ge(sem("merged_ready"), 1)
            gemm("w_out", DC, DC, [(lambda k: merged[:, k, :], 0, DC)])
            mod_sums_of("w_out")

            norm(1, hT)
            pe.wait_ge(sem("h_ready"), 2)
            for b in range(TB):
                u = U["h_turn"] + b
                open_unit(pe, u)
                for k in range(DC):
                    mm = pe.transpose(unit(u)[:, k * P:(k + 1) * P], hT[:, k, b * P:(b + 1) * P], ident)
                mm.then_inc(psum_full, 1)
            rw = vec("router_w").rearrange("p (k e) -> p k e", k=DC)
            u = U["logits"]
            open_unit(pe, u)
            for b in range(TB):
                for k in range(DC):
                    mm = pe.matmul(unit(u)[:, b * N_EXPERTS:(b + 1) * N_EXPERTS], hT[:, k, b * P:(b + 1) * P],
                                   rw[:, k, :], start=(k == 0), stop=(k == DC - 1))
            mm.then_inc(psum_full, 1)
            mask = small[:, 264:328]
            pe.wait_ge(sem("mask_ready"), 1)
            u = U["positions"]
            open_unit(pe, u)
            E = N_EXPERTS
            pe.matmul(unit(u)[:, 0:E], before, mask[:, 0:E], start=True, stop=True)
            pe.matmul(unit(u)[:, E:2 * E], ones, mask[:, 0:E], start=True, stop=False)
            pe.matmul(unit(u)[:, E:2 * E], before, mask[:, E:2 * E], start=False, stop=True)
            pe.matmul(unit(u)[:, 2 * E:3 * E], ones, mask[:, 0:E], start=True, stop=False)
            pe.matmul(unit(u)[:, 2 * E:3 * E], ones, mask[:, E:2 * E], start=False, stop=True).then_inc(psum_full, 1)
            gate = small[:, 328:392]
            pe.wait_ge(sem("gates_ready"), 1)
            u = U["gate_turn"]
            open_unit(pe, u)
            for b in range(TB):
                mm = pe.matmul(unit(u)[0:E, b * P:(b + 1) * P], gate[:, E * b:E * b + E], ident, start=True, stop=True)
            mm.then_inc(psum_full, 1)
            await_freed(pe, u)
            pe.wait_ge(sem("b2_landed"), 16)
            for k in range(DC):
                u = U["bias_sum"] + k // 4
                if k % 4 == 0:
                    open_unit(pe, u)
                mm = pe.matmul(unit(u)[:, (k % 4) * T:(k % 4 + 1) * T], b2_rows[0:E, k * P:(k + 1) * P], gateT[0:E, :],
                               start=True, stop=True)
                if k % 4 == 3:
                    mm.then_inc(psum_full, 1)

            def unused(u, *turn):
                open_unit(pe, u, *turn)
                pe.matmul(unit(u)[:, 0:E], before, mask[:, 0:E], start=True, stop=True).then_inc(
                    full_x if turn else psum_full, 1)

            for name in PLAN.pads:
                unused(U[name])

            def gather(u, half):
                sel = moe_buf("sel", TB)
                for n in range(4):
                    k = 4 * half + n
                    for b in range(TB):
                        at = 512 * (n // 2) + (n % 2) * 2 * CAP
                        mm = pe.matmul(u[:, at:at + 2 * CAP], h_nat[:, b, k * P:(k + 1) * P], sel[:, b, :],
                                       start=(b == 0), stop=(b == TB - 1), skip_group_check=True)
                return mm

            pe.wait_ge(sem("sel_ready"), 1)
            for half in range(2):
                open_unit(pe, U["gather"] + half)
                gather(unit(U["gather"] + half), half).then_inc(psum_full, 1)

            def experts(c, last=False):
                def rows_gemm(name, j0, high, low):
                    c.open_unit(pe, name)
                    u = c.unit(name)
                    for k in range(DC):
                        j = j0 + k // 2
                        if k % 2 == 0:
                            pe.wait_ge(sem("expert_split" + c.x), c.turn * TURN_SLOTS + (j + 1))
                        wh, wl = high_ap(j, D), low_ap(PLAN.moe_slot + j, D)
                        for half in range(2):
                            for w in (wh, wl):
                                cols = slice(512 * half, 512 * half + 512)
                                pe.matmul(u[0:CAP, cols], high(k), w[:, k % 2, cols], start=(k == 0 and w is wh),
                                          stop=False, skip_group_check=True)
                        for half in range(2):
                            cols = slice(512 * half, 512 * half + 512)
                            mm = pe.matmul(u[0:CAP, cols], low(k), wh[:, k % 2, cols], start=False, stop=(k == DC - 1),
                                           skip_group_check=True)
                        if k % 2 == 1:
                            mm.then_inc(c.used if k != DC - 1 else c.full, 1)

                def project(name, e, j0):
                    mine = slice(e * CAP, e * CAP + CAP)
                    rows_gemm(name, j0, lambda k: xg_high[:, k, mine], lambda k: xg_low[:, k, mine])

                def turn_rows(name, of, rows, e=None):
                    c.await_freed(pe, of)
                    c.open_unit(pe, name)
                    u = c.unit(name)
                    for k in range(DC):
                        at = 512 * (k // 4) + (k % 4) * CAP
                        mm = pe.transpose(u[:, at:at + CAP], moe_buf(rows)[0:CAP, k * P:(k + 1) * P],
                                          ident[0:CAP, 0:CAP])
                    if e is not None:
                        for b in range(TB):
                            at = 512 * b + 4 * CAP
                            mm = pe.transpose(u[0:CAP, at:at + P], moe_buf("selG", TB)[:, b, e * CAP:e * CAP + CAP],
                                              ident)
                    mm.then_inc(c.full, 1)

                def down(e):
                    pe.wait_ge(sem("expert_hidden" + c.x), c.turn * 2 + (e + 1))
                    rows_gemm(f"down{e}", 16 + 4 * e, lambda k: hid_high[:, k, :], lambda k: hid_low[:, k, :])

                def result(e):
                    c.await_freed(pe, f"gate{e}_turn")
                    c.await_freed(pe, f"down{e}")
                    for k in range(DC):
                        name = f"result{e}" + "b" * (k // 4)
                        if k % 4 == 0:
                            c.open_unit(pe, name)
                        mm = pe.matmul(c.unit(name)[:, (k % 4) * T:(k % 4 + 1) * T],
                                       moe_buf(f"y_rows{e}")[0:CAP, k * P:(k + 1) * P],
                                       moe_buf(f"selT{e}")[0:CAP, :], start=True, stop=True)
                        if k % 4 == 3:
                            mm.then_inc(c.full, 1)

                def gather_next(half):
                    pe.wait_ge(sem("sel_ready" + c.x), c.gathers + 2)
                    c.open_unit(pe, f"gather{half}")
                    gather(c.unit(f"gather{half}"), half).then_inc(c.full, 1)

                pe.wait_ge(sem("xg_ready" + c.x), c.gathers * 2 + 2)
                project("gate0", 0, 0)
                project("up0", 0, 4)
                turn_rows("gate0_turn", "gate0", "gate_rows", 0)
                project("gate1", 1, 8)
                turn_rows("up0_turn", "up0", "up_rows")
                project("up1", 1, 12)
                turn_rows("gate1_turn", "gate1", "gate_rows", 1)
                down(0)
                turn_rows("up1_turn", "up1", "up_rows")
                gather_next(0)
                result(0)
                down(1)
                gather_next(1)
                result(1)

            with pe.Fori(0, PAIRS - 1) as i:
                experts(first_turn(i))
            experts(first_turn(PAIRS - 1))
            with pe.If(many(pe) > CAP):
                for q in range(4):
                    pe.wait_ge(psum_free[q], (PLAN.moe_unit + TURN_UNITS * PAIRS) // 4)
                pe.sem_inc(full_x, X_UNITS)
                pe.sem_inc(used_x, TURN_SIGNALS)

                def before_pairs(r):
                    pe.wait_ge(sem("sel_ready_x"), r * (PAIRS + 1) + 1)
                    for half in range(2):
                        open_unit(pe, X_UNITS + half, r * (4 * PAIRS + 1), 4, free_x)
                        gather(unit(X_UNITS + half), half).then_inc(full_x, 1)
                    for n in range(2, 4):
                        unused(X_UNITS + n, r * (4 * PAIRS + 1), 4, free_x)
                rounds_loop(pe, before_pairs, experts)
                for q in range(4):
                    pe.wait_ge(free_x[q], 4 + (1 + 4 * PAIRS) * (ROUNDS - 1))

            norm(2, hT)

            def ffn(e, normed, norm_between=None):
                for ab in range(2):
                    for n, (c0, nc_) in enumerate(FFN_PASSES):
                        split_gemm(f"ffn{e}_{'ab'[ab]}{n}", DC, nc_, h_high, h_low,
                                   after_norm(normed) if (ab, n) == (0, 0) else None)
                        mod_sums_of(f"ffn{e}_{'ab'[ab]}{n}")
                if norm_between is not None:
                    norm(norm_between, hT)
                split_gemm(f"ffn{e}_out", FC, DC, m_high, m_low,
                           lambda k: pe.wait_ge(sem("ffn_hidden"), 6 * e + k // 4 + 1), halves_last=True)
                mod_sums_of(f"ffn{e}_out")

            norm(3, hT)
            ffn(0, 3, 4)
            ffn(1, 4, 5)
            split_gemm("even_qk", DC, DC, h_high, h_low, after_norm(5))
            split_gemm("even_vu", DC, DC, h_high, h_low)
            norm(6, hT)
            split_gemm("even_ctx", DC, DC, h_high, h_low, after_norm(6))
            await_freed(pe, U["even_vu"])
            await_freed(pe, U["even_ctx"] + 1)
            for n in range(2):
                u = U["na_vturn"] + n
                open_unit(pe, u)
                for b in range(2):
                    for c in range(4):
                        at = (2 * n + b) * P
                        mm = pe.transpose(unit(u)[:, b * 512 + c * P:b * 512 + (c + 1) * P], z2v[:, c, at:at + P],
                                          ident)
                mm.then_inc(psum_full, 1)
            await_freed(pe, U["even_vu"] + 1)
            pw = vec("pool_w").rearrange("p (g n) -> p g n", g=4)
            u = U["pool_map"]
            open_unit(pe, u)
            for b in range(TB):
                for g in range(4):
                    mm = pe.matmul(unit(u)[:, b * 512 + g * P:b * 512 + (g + 1) * P], z2u[:, g, b * P:(b + 1) * P],
                                   pw[:, g, :], start=True, stop=True)
            mm.then_inc(psum_full, 1)
            await_freed(pe, u)
            pe.wait_ge(sem("band_landed"), 16)
            u = U["pool_out"]
            open_unit(pe, u)
            for g in range(4):
                for b in range(TB):
                    mm = pe.matmul(unit(u)[:, g * T:(g + 1) * T], pool_mapped[:, b, g * P:(g + 1) * P],
                                   pool_band[:, b, g, :], start=(b == 0), stop=(b == TB - 1))
            mm.then_inc(psum_full, 1)

            def na_scores(s):
                blk, pair = NA_STEPS[s]
                u = U[f"na_scores{s}"]
                open_unit(pe, u)
                for j in range(2):
                    rows = slice(64 * j, 64 * j + 64)
                    mm = pe.matmul(unit(u)[:, 512 * j:512 * j + 512], z2q[rows, pair, blk * P:(blk + 1) * P],
                                   z2k[rows, pair, :], start=True, stop=True)
                mm.then_inc(psum_full, 1)

            await_freed(pe, U["even_qk"])
            await_freed(pe, U["even_qk"] + 1)
            await_freed(pe, U["even_ctx"])
            na_scores(0)
            for s in range(len(NA_STEPS)):
                if s + 1 < len(NA_STEPS):
                    na_scores(s + 1)
                blk, pair = NA_STEPS[s]
                u = U[f"na_turn{s}"]
                await_freed(pe, U[f"na_scores{s}"])
                open_unit(pe, u)
                for j in range(2):
                    for kb in range(4):
                        mm = pe.transpose(unit(u)[:, (4 * j + kb) * P:(4 * j + kb + 1) * P],
                                          na_probs[:, j, kb * P:(kb + 1) * P], ident)
                mm.then_inc(psum_full, 1)
                await_freed(pe, u)
                u = U[f"na_out{s}"]
                open_unit(pe, u)
                for j in range(2):
                    h = 2 * pair + j
                    for kb in range(4):
                        mm = pe.matmul(unit(u)[:, j * HD:(j + 1) * HD], na_probsT[:, (4 * j + kb) * P:(4 * j + kb + 1) * P],
                                       vnat2[:, kb, h * HD:(h + 1) * HD], start=(kb == 0), stop=(kb == 3))
                mm.then_inc(psum_full, 1)
            await_freed(pe, U[f"na_out{len(NA_STEPS) - 1}"])
            u = U["na_oturn"]
            open_unit(pe, u)
            for c in range(4):
                for b in range(TB):
                    mm = pe.transpose(unit(u)[:, c * T + b * P:c * T + (b + 1) * P], na_o[:, b, c * P:(c + 1) * P],
                                      ident)
            mm.then_inc(psum_full, 1)
            await_freed(pe, u)
            await_freed(pe, U["pool_out"])
            gemm("even_out", DC, DC, [(lambda k: cat[:, k, :], 0, DC)])
            for e in (2, 3):
                norm(5 + e, hT)
                ffn(e, 5 + e)
            norm(9, hT)
            for n in range(3):
                split_gemm(f"conv{n}", DC, DC, h_high, h_low, after_norm(9) if n == 0 else None)
            gemm("conv_out", DC, DC, [(lambda k: conv_y[:, k, :], 0, DC)],
                 lambda k: pe.wait_ge(sem("conv_ready"), k // 2 + 1))
            norm(10, hT)
            ffn(4, 10)
            norm(11, hT)

        @block.vector
        def _(dve):
            steps = Steps(dve, dve_steps)
            link = steps.link

            def wide(v, n):
                return v[:, :, None].broadcast_to([v.shape[0], v.shape[1], n])

            def chunks(u, n=4, width=T):
                return unit(u)[:, 0:n * width].rearrange("p (c t) -> p c t", c=n)

            def free(ins_, u):
                ins_.then_inc(psum_free[u % 4], 1)

            def finish(ins_, u, done):
                free(ins_, u)
                await_freed(dve, u)
                dve.sem_inc(sem(done), 1)

            dve.wait_ge(sem("vecs_landed"), 16)
            lp = vec("lambda").rearrange("p (n d) -> p n d", n=4)
            lam = small[:, 414:415]
            link(dve.tensor_tensor(lp[:, 0::2, :], lp[:, 0::2, :], lp[:, 1::2, :], ALU.mult))
            dve.tensor_reduce(small[:, 410:412], lp[:, 0::2, :], AX_X, ALU.add).then_inc(sem("lambda_dots"), 1)
            dve.wait_ge(sem("lambda_exp"), 1)
            link(dve.tensor_tensor(lam, small[:, 413:414], small[:, 412:413], ALU.subtract))
            link(dve.tensor_scalar(lam, lam, -LAM_INIT, None, ALU.add))
            link(dve.tensor_scalar(vec("subln"), vec("subln"), 1.0 - LAM_INIT, None, ALU.mult))

            dve.wait_ge(sem("cond_ready"), 2)

            def mod_slot(i):
                n, pair = divmod(i, 4)
                block_, layer, g, conds = MODS[n]
                s = PLAN.mod_at[i]
                await_slot(dve, s)
                w = slot_ap(s)
                for c in range(conds):
                    last_group = MOD_BUFFER_BEFORE[n][c]
                    if pair == 0 and last_group is not None:
                        await_unit(dve, U[mod_unit(last_group)])
                for k in (2 * pair, 2 * pair + 1):
                    for c in range(conds):
                        part = mod_sums[:, MOD_BUFFERS[n][c], :]
                        cond = cs[:, k:k + 1] if block_ == 1 else cs2[:, k, c:c + 1]
                        if k == 0:
                            last = dve.tensor_scalar(part, w[:, k % 2, :], cond, None, ALU.mult)
                        else:
                            last = dve.scalar_tensor_tensor(part, w[:, k % 2, :], cond, part, ALU.mult, ALU.add)
                        if (k % 2, c) != (1, conds - 1):
                            steps.done(last)
                    if k % 2 == 0:
                        steps.settle()
                last.then_inc(sem("mod_slots_used"), 1)
                dve.wait_ge(sem("mod_slots_used"), i + 1)
                if pair == 3:
                    dve.sem_inc(sem("mod_partials"), 1)

            def modulation(n):
                block_, layer, g, conds = MODS[n]
                u = U[mod_unit(n)]
                await_unit(dve, u)
                if block_ == 1:
                    free(dve.tensor_tensor(mod1[:, g, :], unit(u)[:, 0:DC], vec("mod_b")[:, g * DC:(g + 1) * DC],
                                           ALU.add), u)
                    if g in (1, 4):
                        await_freed(dve, u)
                        link(dve.scalar_tensor_tensor(mod1[:, g, :], mod1[:, g, :], 1.0,
                                                      vec("norm1" if g == 1 else "norm2"), ALU.add, ALU.mult))
                    return
                m = mod2[:, layer, g, :, 0:conds]
                at = (layer * N_MOD + g) * DC
                free(dve.tensor_tensor(m, unit(u)[:, 0:conds * DC].rearrange("p (k s) -> p k s", s=conds),
                                       wide(vec("mod_b2")[:, at:at + DC], conds), ALU.add), u)
                if g % 3 == 1:
                    await_freed(dve, u)
                    at = (layer * 3 + g // 3) * DC
                    link(dve.scalar_tensor_tensor(m, m, 1.0, wide(vec("norm_g2")[:, at:at + DC], conds), ALU.add,
                                                  ALU.mult))
                if g in (2, 8):
                    await_freed(dve, u)
                    link(dve.tensor_scalar(m, m, 0.5, None, ALU.mult))

            for i in range(8):
                mod_slot(i)
            modulation(0)
            modulation(1)

            def norm(n, src, dst, scale, shift, eps):
                u = U[f"norm{n}"]
                await_unit(dve, u)
                free(dve.tensor_scalar(rstd[:, 0, :], unit(u)[:, 0:T], 1.0 / D, eps, ALU.mult, ALU.add), u)
                dve.wait_ge(sem("root_ready"), n + 1)
                link(dve.reciprocal(rstd[:, 0, :], rstd[:, 1, :]))

                def scaled(first, n_chunks):
                    some = slice(first, first + n_chunks)
                    link(dve.tensor_tensor(dst[:, some, :], src[:, some, :],
                                           rstd[:, 0:1, :].broadcast_to([P, n_chunks, T]), ALU.mult))
                    for k in range(first, first + n_chunks):
                        if shift is None:
                            last = dve.tensor_scalar(dst[:, k, :], dst[:, k, :], scale[:, k:k + 1], None, ALU.mult)
                        else:
                            last = dve.tensor_scalar(dst[:, k, :], dst[:, k, :], scale[:, k:k + 1], shift[:, k:k + 1],
                                                     ALU.mult, ALU.add)
                    return last

                def low_part(part):
                    two = slice(2 * part, 2 * part + 2)
                    dve.wait_ge(sem("h_high_ready"), H_PARTS * (n - 3) + part + 1)
                    dve.tensor_tensor(h_low[:, two, :], dst[:, two, :], h_high[:, two, :].bitcast(F32),
                                      ALU.subtract).then_inc(sem("h_parts"), 1)

                if n in PLAIN_NORMS:
                    scaled(0, DC).then_inc(sem("h_ready"), 1)
                    return
                for part in range(H_PARTS):
                    scaled(2 * part, 2).then_inc(sem("h_whole"), 1)
                    if part:
                        low_part(part - 1)
                low_part(H_PARTS - 1)

            norm(0, xT[:, :, :], hT[:, :, :], mod1[:, 1, :], mod1[:, 0, :], EPS1)
            for n, (c0, nc_) in enumerate(Z_PASSES):
                for i in range(8 + 4 * n, 12 + 4 * n):
                    mod_slot(i)
                for half in range(-(-nc_ // 4)):
                    u, k = U[f"z{n}"] + half, min(4, nc_ - 4 * half)
                    z = c0 + 4 * half
                    await_unit(dve, u)
                    last = dve.tensor_tensor(zT[:, z:z + k, :], chunks(u, k), wide(vec("b_in")[:, z:z + k], T), ALU.add)
                    if half == 0:
                        free(last, u)
                finish(last, u, "z_ready")
                modulation(2 + n)
            for m, z in enumerate((Z_KCM, Z_VCM)):
                dst = blocks[:, m, :].rearrange("p (j c) -> p j c", j=16)
                for g in range(2):
                    for odd in range(2):
                        for late in range(2):
                            src = zT[64 * g:64 * g + 64, z, 16 * late:16 * late + 16 * NCMP]
                            src = src.rearrange("p (c x) -> p x c", x=16)[:, odd::2, :]
                            dve.tensor_copy(dst[64 * odd:64 * odd + 64, 8 * late:8 * late + 8,
                                                g * NCMP:(g + 1) * NCMP], src)
                last = dve.tensor_copy(dst[:, :, 30:31], vec("cmp_pos")[:, 16 * m:16 * m + 16, None])
            last.then_inc(sem("blocks_ready"), 1)
            u = U["cmp_hidden"]
            await_unit(dve, u)
            dve.tensor_tensor(small[:, 192:196], unit(u)[:, 30:128:32], vec("cmp_b1"), ALU.add).then_inc(
                sem("cmp_bias_ready"), 1)
            u = U["cmp_kv"]
            await_unit(dve, u)
            dve.tensor_scalar(small[:, 200:230], unit(u)[:, 0:2 * NCMP], vec("cmp_b2k"), None, ALU.add)
            b2v = vec("cmp_b2v")[0:NCMP, None, :].broadcast_to([NCMP, 2, HD])
            free(dve.tensor_tensor(small[0:NCMP, 232:360].rearrange("p (g d) -> p g d", g=2),
                                   unit(u)[0:NCMP, 512:640].rearrange("p (g d) -> p g d", g=2), b2v, ALU.add), u)
            u = U["cmp_scores"]
            await_unit(dve, u)
            for b in range(TB):
                cb = const("cmp_bias")[:, None, 16 * b:16 * b + NCMP].broadcast_to([P, 4, NCMP])
                for g in range(2):
                    src = unit(u)[:, 512 * g + 64 * b:512 * g + 64 * b + 64]
                    src = src.rearrange("p (h c) -> p h c", h=4)[:, :, 0:NCMP]
                    last = dve.scalar_tensor_tensor(cmpP[:, 8 * b + 4 * g:8 * b + 4 * g + 4, 0:NCMP], src, HD ** -0.5,
                                                    cb, ALU.mult, ALU.add)
            free(last, u)
            await_freed(dve, u)
            cp = cmpP[:, :, 0:NCMP]
            link(dve.tensor_reduce(small[:, 360:376], cp, AX_X, ALU.max))
            dve.tensor_tensor(cp, cp, wide(small[:, 360:376], NCMP), ALU.subtract).then_inc(sem("cmp_shifted"), 1)
            dve.wait_ge(sem("cmp_exp"), 1)
            link(dve.tensor_reduce(small[:, 376:392], cp, AX_X, ALU.add))
            link(dve.reciprocal(small[:, 376:392], small[:, 376:392]))
            link(dve.tensor_tensor(cp, cp, wide(small[:, 376:392], NCMP), ALU.mult))
            for b in range(TB):
                cv = const("cmp_valid")[:, None, 16 * b:16 * b + NCMP].broadcast_to([P, 8, NCMP])
                last = dve.tensor_tensor(cmpP[:, 8 * b:8 * b + 8, 0:NCMP], cmpP[:, 8 * b:8 * b + 8, 0:NCMP], cv,
                                         ALU.mult)
            last.then_inc(sem("cmp_probs"), 1)
            u = U["cmp_out"]
            await_unit(dve, u)
            for b in range(TB):
                await_freed(dve, U["vnat"] + b)
                gates = small[:, 24 * b:24 * b + 24].rearrange("p (h r) -> p h r", h=8)
                last = dve.tensor_tensor(o_nat[:, b, 2, :].rearrange("p (h d) -> p h d", h=8),
                                         unit(u)[:, 512 * b:512 * b + 512].rearrange("p (h d) -> p h d", h=8),
                                         gates[:, :, 0:1].broadcast_to([P, 8, HD]), ALU.mult)
            free(last, u)

            dve.wait_ge(sem("alibi_landed"), 32)

            def soft(s):
                kind, blk, g = ATT[s]
                kw = P * (blk + 1)
                u = U[f"scores{s}"]
                table = alibi_near if kind == "swa" else alibi_full
                table = table[:, 1::2, T - kw:T] if kind == "diff" else table[:, 4 * g:4 * g + 4, T - kw:T]
                sc = chunks(u)[:, :, 0:kw]
                await_unit(dve, u)
                link(dve.scalar_tensor_tensor(sc, sc, HD ** -0.5, table, ALU.mult, ALU.add))
                link(dve.tensor_reduce(stats[:, 0, s, :], sc, AX_X, ALU.max))
                if kind == "swa":
                    sinks = vec("sinks")[:, 4 * g:4 * g + 4]
                    link(dve.tensor_tensor(stats[:, 0, s, :], stats[:, 0, s, :], sinks, ALU.max))
                    dve.tensor_tensor(stats[:, 3, s, :], sinks, stats[:, 0, s, :], ALU.subtract)
                dve.tensor_scalar(stats[:, 1, s, :], stats[:, 0, s, :], -1.0, None, ALU.mult).then_inc(
                    sem("row_max_ready"), 1)

            tmp = rstd[:, :, :].rearrange("p a t -> p (a t)")

            def attended(s):
                kind, blk, g = ATT[s]
                u = U[f"out{s}"]
                await_freed(dve, U[f"scores{s}"])
                if kind == "swa":
                    dve.wait_ge(sem("sink_exp"), [a[0] for a in ATT[:s + 1]].count("swa"))
                    link(dve.tensor_tensor(stats[:, 2, s, :], stats[:, 2, s, :], stats[:, 3, s, :], ALU.add))
                link(dve.reciprocal(stats[:, 2, s, :], stats[:, 2, s, :]))
                if kind in ("slc", "win"):
                    gates = small[:, 24 * blk:24 * blk + 24].rearrange("p (h r) -> p h r", h=8)
                    br = 1 if kind == "slc" else 2
                    link(dve.tensor_tensor(stats[:, 2, s, :, None], stats[:, 2, s, :, None],
                                           gates[:, 4 * g:4 * g + 4, br:br + 1], ALU.mult))
                if kind == "diff" and g == 1:
                    link(dve.tensor_scalar(stats[:, 2, s, :], stats[:, 2, s, :], lam, None, ALU.mult))
                dv = P if kind == "diff" else HD
                branch = {"swa": 0, "diff": 1, "slc": 2, "win": 2}[kind]
                at = 0 if kind == "diff" else 256 * g
                dst = o_nat[:, blk, branch, at:at + 4 * dv]
                adds = kind in ("slc", "win") or (kind == "diff" and g == 1)
                await_unit(dve, u)
                to = tmp[:, 0:4 * dv] if adds else dst
                free(dve.tensor_tensor(to.rearrange("p (h d) -> p h d", h=4), chunks(u, 4, dv),
                                       wide(stats[:, 2, s, :], dv), ALU.mult), u)
                if adds:
                    await_freed(dve, u)
                    link(dve.tensor_tensor(dst, dst, to, ALU.add))

            soft(0)
            for s in range(len(ATT)):
                if s + 1 < len(ATT):
                    soft(s + 1)
                if s:
                    for n in mods_ending(*ATT_MOD_SLOTS[s - 1:s + 1]):
                        modulation(n)
                for i in range(*ATT_MOD_SLOTS[s:s + 2]):
                    mod_slot(24 + i)
                attended(s)
            for n in mods_ending(*ATT_MOD_SLOTS[-2:]):
                modulation(n)
            for b in range(TB):
                link(dve.tensor_tensor(tmp, o_nat[:, b, 1, :], o_nat[:, b, 1, :], ALU.mult))
                link(dve.tensor_reduce(small[:, 400 + 4 * b:404 + 4 * b], tmp.rearrange("p (h d) -> p h d", h=4),
                                       AX_X, ALU.add))
            dve.tensor_scalar(small[:, 400:408], small[:, 400:408], 1.0 / P, EPS1, ALU.mult, ALU.add).then_inc(
                sem("subln_mean"), 1)
            dve.wait_ge(sem("subln_root"), 1)
            link(dve.reciprocal(small[:, 400:408], small[:, 400:408]))
            for b in range(TB):
                ob = o_nat[:, b, 1, :].rearrange("p (h d) -> p h d", h=4)
                link(dve.tensor_tensor(ob, ob, wide(small[:, 400 + 4 * b:404 + 4 * b], P), ALU.mult))
                last = dve.tensor_tensor(ob, ob, vec("subln")[:, None, :].broadcast_to([P, 4, P]), ALU.mult)
            last.then_inc(sem("branches_ready"), 1)

            def mods_of(name):
                for i, s in enumerate(PLAN.mod_at):
                    if PLAN.slots[name][0] < s <= PLAN.slots[name][-1] + 1:
                        mod_slot(i)
                for n in PLAN.mods_after[name]:
                    modulation(n)

            for br in range(3):
                mods_of(f"merge{br}")
                mods_of(f"branch{br}")
                for half in range(2):
                    u = U[f"branch{br}"] + half
                    gate = gm[:, br * DC + 4 * half:br * DC + 4 * half + 4, :]
                    dst = merged[:, 4 * half:4 * half + 4, :]
                    await_freed(dve, U[f"merge{br}"] + half)
                    await_unit(dve, u)
                    if br == 0:
                        free(dve.tensor_tensor(dst, chunks(u), gate, ALU.mult), u)
                        await_freed(dve, u)
                    else:
                        free(dve.tensor_tensor(merge_tmp, chunks(u), gate, ALU.mult), u)
                        await_freed(dve, u)
                        last = dve.tensor_tensor(dst, dst, merge_tmp, ALU.add)
                        if (br, half) == (2, 1):
                            last.then_inc(sem("merged_ready"), 1)
                        else:
                            link(last)

            def add_to(dst, u0, gate):
                for k in range(DC):
                    u = u0 + k // 4
                    if k % 4 == 0:
                        await_unit(dve, u)
                    last = dve.scalar_tensor_tensor(dst[:, k, :], unit(u)[:, (k % 4) * T:(k % 4 + 1) * T],
                                                    gate[:, k:k + 1], dst[:, k, :], ALU.mult, ALU.add)
                    if k == 3:
                        free(last, u)
                return last, u

            mods_of("w_out")
            finish(*add_to(xT, U["w_out"], mod1[:, 2, :]), "x_ready")
            norm(1, xT[:, :, :], hT[:, :, :], mod1[:, 4, :], mod1[:, 3, :], EPS1)

            E = N_EXPERTS
            vals, top, negmax = small[:, 0:72], small[:, 72:88], small[:, 88:90]
            total, expd, replaced = small[:, 92:94], small[:, 128:192], small[:, 192:264]
            mask, gate, place = small[:, 264:328], small[:, 328:392], small[:, 392:456]
            u = U["logits"]
            await_unit(dve, u)
            for b in range(TB):
                last = dve.tensor_tensor(vals[:, 36 * b:36 * b + E], unit(u)[:, E * b:E * b + E], vec("router_b"),
                                         ALU.add)
            free(last, u)
            await_freed(dve, u)
            for b in range(TB):
                link(dve.max(top[:, 8 * b:8 * b + 8], vals[:, 36 * b:36 * b + E]))
            for b in range(TB):
                dve.tensor_scalar(negmax[:, b:b + 1], top[:, 8 * b:8 * b + 1], -1.0, None, ALU.mult).then_inc(
                    sem("top_ready"), 1)
            for n in range(4):
                for b in range(TB):
                    link(dve.memset(vals[:, 36 * b + E + n:36 * b + E + n + 1], -(n + 1.0) * 1e37))
                    link(dve.memset(top[:, 8 * b + 4 + n:8 * b + 5 + n], -(n + 1.0) * 1e37))
            for b in range(TB):
                v, r = vals[:, 36 * b:36 * b + 36], replaced[:, 36 * b:36 * b + 36]
                link(dve.match_replace(r, top[:, 8 * b:8 * b + 8], v, 3e38))
                last = dve.tensor_tensor(mask[:, E * b:E * b + E], r[:, 0:E], v[:, 0:E], ALU.not_equal)
                link(last) if b == 0 else last.then_inc(sem("mask_ready"), 1)
            dve.wait_ge(sem("mask_ready"), 1)
            dve.wait_ge(sem("route_exp"), 2)
            link(dve.tensor_tensor(gate, expd, mask, ALU.mult))
            link(dve.tensor_reduce(total, gate.rearrange("p (b e) -> p b e", b=TB), AX_X, ALU.add))
            link(dve.reciprocal(total, total))
            link(dve.tensor_tensor(gate.rearrange("p (b e) -> p b e", b=TB), gate.rearrange("p (b e) -> p b e", b=TB),
                                   wide(total, E), ALU.mult))
            dve.sem_inc(sem("gates_ready"), 1)
            u = U["positions"]
            await_unit(dve, u)
            dve.scalar_tensor_tensor(place, unit(u)[:, 0:2 * E], 1.0, mask, ALU.add, ALU.mult)
            free(dve.tensor_reduce(small[:, 460:461], unit(u)[:, 2 * E:3 * E], AX_X, ALU.max), u)
            await_freed(dve, u)
            link(dve.tensor_scalar(place, place, -1.0, None, ALU.add))
            dve.tensor_copy(count_max[:, :], small[:, 460:461]).then_inc(sem("count_ready"), 1)
            link(dve.memset(small[:, 456:458], -1.0))

            slot_no = const("iota")[:, 0:CAP]

            def select(col, x):
                sel, sg = moe_buf("sel", TB), moe_buf("selG", TB)
                for e in range(2):
                    for b in range(TB):
                        p_, g_ = col(392 + E * b + e), col(328 + E * b + e)
                        mine = slice(e * CAP, e * CAP + CAP)
                        dve.tensor_scalar(sel[:, b, mine], slot_no, p_, None, ALU.is_equal)
                        last = dve.tensor_scalar(sg[:, b, mine], slot_no, p_, g_, ALU.is_equal, ALU.mult)
                last.then_inc(sem("sel_ready" + x), 1)

            def first_col(at):
                return small[:, at:at + 1]

            def gathered_low(half, src, freed, x, n):
                dve.wait_ge(sem("xg_high_ready" + x), n)
                mine = slice(4 * half, 4 * half + 4)
                dve.tensor_tensor(banked(xg_low[:, mine, :], 2), four_chunks(src, 2, 2 * CAP),
                                  banked(xg_high[:, mine, :].bitcast(F32), 2), ALU.subtract).then_inc(
                    sem("xg_ready" + x), 1)
                dve.wait_ge(sem("xg_ready" + x), n)
                dve.sem_inc(freed, 1)

            select(first_col, "")
            for half in range(2):
                u = U["bias_sum"] + half
                await_unit(dve, u)
                free(dve.tensor_copy(acc[:, 4 * half:4 * half + 4, :], chunks(u)), u)
                await_freed(dve, u)
            for name in PLAN.pads:
                u = U[name]
                await_unit(dve, u)
                free(dve.tensor_copy(small[:, 461:462], unit(u)[:, 0:1]), u)
                await_freed(dve, u)
            for half in range(2):
                u = U["gather"] + half
                await_unit(dve, u)
                gathered_low(half, unit(u), psum_free[u % 4], "", half + 1)

            def low(c, *slots):
                for j in slots:
                    dve.wait_ge(sem("expert_high_ready" + c.x), c.turn * TURN_SLOTS + (j + 1))
                    dve.tensor_tensor(low_ap(PLAN.moe_slot + j, D), slot_ap(PLAN.moe_slot + j),
                                      high_ap(j, D).bitcast(F32), ALU.subtract).then_inc(
                        sem("expert_split" + c.x), 1)

            def experts(c, steps, last=False):
                gb, ub, sig = moe_buf("gate", DC), moe_buf("up", DC), moe_buf("sig", DC)
                b1 = VEC_AT["exp_b1"][0]

                def biased(dst, name, e, chunk):
                    bias = vecs[:, bass.ds(c.pair * (4 * DC) + (b1 + 2 * DC * e + chunk), DC)]
                    c.await_unit(dve, name)
                    c.free_unit(dve.tensor_tensor(banked(dst, 4), four_chunks(c.unit(name), 4, CAP),
                                                  banked(wide(bias, CAP), 4), ALU.add), name)
                    c.await_freed(dve, name)

                def gate_half(e):
                    dve.wait_ge(sem("selT_ready" + c.x), c.turn * 2 + (e + 1))
                    biased(gb, f"gate{e}_turn", e, 0)
                    dve.tensor_scalar(gb, gb, LIMIT, None, ALU.min).then_inc(sem("gate_clamped" + c.x), 1)

                def up_half(e):
                    biased(ub, f"up{e}_turn", e, DC)
                    steps.link(dve.tensor_scalar(ub, ub, LIMIT, -LIMIT, ALU.min, ALU.max))
                    dve.wait_ge(sem("gate_sigmoid" + c.x), c.turn * 2 + (e + 1))
                    steps.link(dve.tensor_tensor(gb, gb, sig, ALU.mult))
                    steps.link(dve.scalar_tensor_tensor(gb, ub, 1.0, gb, ALU.add, ALU.mult))
                    steps.link(dve.tensor_scalar(hid_high[:, :, :], gb, 1.0, None, ALU.mult))
                    dve.tensor_tensor(hid_low[:, :, :], gb, hid_high[:, :, :].bitcast(F32), ALU.subtract).then_inc(
                        sem("expert_hidden" + c.x), 1)
                    dve.wait_ge(sem("expert_hidden" + c.x), c.turn * 2 + (e + 1))

                def add_result(e):
                    for half in range(2):
                        name = f"result{e}" + "b" * half
                        c.await_unit(dve, name)
                        dst = acc[:, 4 * half:4 * half + 4, :]
                        c.free_unit(dve.tensor_tensor(dst, chunks(c.u0 + MU[name]), dst, ALU.add), name)
                        c.await_freed(dve, name)

                def gathered(half):
                    name = f"gather{half}"
                    c.await_unit(dve, name)
                    gathered_low(half, c.unit(name), c.free[(c.u0 + MU[name]) % 4], c.x, c.gathers * 2 + (3 + half))

                low(c, 3, 4, 5, 6, 7, 8, 9, 10)
                gate_half(0)
                low(c, 11, 12, 13, 14, 15)
                up_half(0)
                low(c, 16, 17, 18, 19)
                gate_half(1)
                select(lambda at: small[:, bass.ds(c.pair * 2 + (at + 2), 1)], c.x)
                low(c, 20, 21)
                up_half(1)
                low(c, 22, 23)
                gathered(0)
                add_result(0)
                if not last:
                    low(c, *NEXT_SLOTS)
                gathered(1)
                add_result(1)

            low(first_turn(0), 0, 1, 2)
            with dve.Fori(0, PAIRS - 1) as i:
                steps.enter(i, 8)
                experts(first_turn(i), steps)
                steps.leave(PAIRS - 1)
            experts(first_turn(PAIRS - 1), steps, last=True)
            with dve.If(many(dve) > CAP):
                for q in range(4):
                    dve.sem_inc(free_x[q], X_UNITS // 4)
                steps_x = Steps(dve, sem("dve_steps_x"))

                def before_pairs(r):
                    dve.tensor_scalar(place, place, -float(CAP), None, ALU.add).then_inc(sem("round_shifted"), 1)
                    dve.wait_ge(sem("round_shifted"), r + 1)
                    select(first_col, "_x")
                    for n in range(4):
                        await_unit(dve, X_UNITS + n, r * (4 * PAIRS + 1), 4, full_x)
                        if n < 2:
                            gathered_low(n, unit(X_UNITS + n), free_x[n], "_x", r * (2 * PAIRS + 2) + (n + 1))
                        else:
                            dve.tensor_copy(small[:, 461:462], unit(n)[:, 0:1]).then_inc(free_x[n], 1)
                            await_freed(dve, X_UNITS + n, r * (4 * PAIRS + 1), 4, free_x)
                    low(x_turn(r, 0), 0, 1, 2)
                    dve.memset(small[:, 463:464], 0.0)

                def later(c, last=False):
                    steps_x.n = 0
                    steps_x.enter(c.turn, 8)
                    experts(c, steps_x, last)
                rounds_loop(dve, before_pairs, later)
            for k in range(DC):
                last = dve.scalar_tensor_tensor(xT[:, k, :], acc[:, k, :], mod1[:, 5, k:k + 1], xT[:, k, :],
                                                ALU.mult, ALU.add)
            last.then_inc(sem("x_ready"), 1)
            dve.wait_ge(sem("x_ready"), 2)
            norm(2, xT[:, :, :], xT[:, :, :], vec("final1"), None, EPS1)

            def norm2(n, layer, which, t=0):
                norm(n, (xT[:, :, :], cT)[t], hT[:, :, :], mod2[:, layer, 3 * which + 1, :, t],
                     mod2[:, layer, 3 * which, :, t], EPS2)

            lows, mods_done, at = [0], [4 * L1_MODS], [moe_end]

            def low_parts(until):
                for s in range(at[0], until):
                    if s in PLAN.split_no:
                        m, cols = PLAN.split_no[s], PLAN.stream[s][5]
                        dve.wait_ge(sem("w_high_ready"), m + 1)
                        dve.tensor_tensor(low_ap(s, cols), slot_ap(s, 2, cols), high_ap(m, cols).bitcast(F32),
                                          ALU.subtract).then_inc(sem("w_split"), 1)
                    elif mods_done[0] < len(PLAN.mod_at) and PLAN.mod_at[mods_done[0]] == s:
                        mod_slot(mods_done[0])
                        mods_done[0] += 1
                at[0] = max(at[0], until)

            def modulations_of(name):
                for n in PLAN.mods_after[name]:
                    modulation(n)

            def ffn(e, layer, which, between=None):
                t = FFNS[e][1]
                for n in range(len(FFN_PASSES)):
                    low_parts(ahead_of(f"ffn{e}_a{n}"))
                    modulations_of(f"ffn{e}_a{n}")
                for n, (c0, nc_) in enumerate(FFN_PASSES):
                    low_parts(ahead_of(f"ffn{e}_b{n}"))
                    for half in range(2):
                        k = min(4, nc_ - 4 * half)
                        u = U[f"ffn{e}_b{n}"] + half
                        dst = hm[:, c0 + 4 * half:c0 + 4 * half + k, :]
                        await_freed(dve, U[f"ffn{e}_a{n}"] + half)
                        await_unit(dve, u)
                        free(dve.tensor_tensor(dst, chunks(u, k), dst, ALU.mult), u)
                    for half in range(2):
                        k = min(4, nc_ - 4 * half)
                        c = c0 + 4 * half
                        dve.wait_ge(sem("m_high_ready"), 6 * e + 2 * n + half + 1)
                        dve.tensor_tensor(m_low[:, c:c + k, :], hm[:, c:c + k, :],
                                          m_high[:, c:c + k, :].bitcast(F32), ALU.subtract).then_inc(
                            sem("ffn_hidden"), 1)
                    modulations_of(f"ffn{e}_b{n}")
                if between:
                    between()
                low_parts(ahead_of(f"ffn{e}_out"))
                finish(*add_to((xT, cT)[t], U[f"ffn{e}_out"], mod2[:, layer, 3 * which + 2, :, t]), "x_ready")
                modulations_of(f"ffn{e}_out")

            dve.wait_ge(sem("h_ready"), 3)
            low_parts(PLAN.split_at[HIGHS - 1] + 1)
            norm2(3, 0, 0)
            ffn(0, 0, 0, lambda: norm2(4, 0, 0, 1))
            ffn(1, 0, 0, lambda: norm2(5, 0, 1))
            low_parts(ahead_of("even_qk"))
            low_parts(ahead_of("even_vu"))
            norm2(6, 0, 1, 1)
            low_parts(ahead_of("even_ctx"))
            u = U["pool_out"]
            await_unit(dve, u)
            for g in range(4):
                last = dve.tensor_scalar(cat[:, 4 + g, :], unit(u)[:, g * T:(g + 1) * T],
                                         vec("pool_scale")[:, g:g + 1], None, ALU.mult)
            free(last, u)
            dve.wait_ge(sem("rpb_masked"), 1)

            def na_soft(s):
                blk, pair = NA_STEPS[s]
                u = U[f"na_scores{s}"]
                sc = unit(u).rearrange("p (j k) -> p j k", j=2)
                await_unit(dve, u)
                link(dve.tensor_tensor(sc[:, :, 0:T], sc[:, :, 0:T],
                                       rpb[:, 8 * blk + 2 * pair:8 * blk + 2 * pair + 2, :], ALU.add))
                link(dve.tensor_reduce(stats[:, 0, s, 0:2], sc, AX_X, ALU.max))
                dve.tensor_scalar(stats[:, 1, s, 0:2], stats[:, 0, s, 0:2], -1.0, None, ALU.mult).then_inc(
                    sem("na_max_ready"), 1)

            na_soft(0)
            for s in range(len(NA_STEPS)):
                if s + 1 < len(NA_STEPS):
                    na_soft(s + 1)
                blk, pair = NA_STEPS[s]
                u = U[f"na_out{s}"]
                await_freed(dve, U[f"na_scores{s}"])
                link(dve.reciprocal(stats[:, 2, s, 0:2], stats[:, 2, s, 0:2]))
                await_unit(dve, u)
                free(dve.tensor_tensor(na_o[:, blk, P * pair:P * pair + P].rearrange("p (h d) -> p h d", h=2),
                                       chunks(u, 2, HD), wide(stats[:, 2, s, 0:2], HD), ALU.mult), u)
            finish(*add_to(xT, U["even_out"], mod2[:, 0, 5, :, 0]), "x_ready")
            norm2(7, 0, 2)
            ffn(2, 0, 2)
            norm2(8, 1, 0)
            ffn(3, 1, 0)
            norm2(9, 1, 1)
            low_parts(ahead_of("conv0"))
            low_parts(ahead_of("conv1"))
            low_parts(ahead_of("conv2"))
            dve.wait_ge(sem("conv_edges"), 2)
            for half in range(2):
                u = U["conv2"] + half
                await_freed(dve, U["conv1"] + half)
                await_unit(dve, u)
                free(dve.tensor_tensor(conv_z[:, 4 * half:4 * half + 4, 1:T + 1], chunks(u),
                                       conv_c[:, 4 * half:4 * half + 4, :], ALU.mult), u)
            taps = vec("conv_w").rearrange("p (n k) -> p n k", n=3)
            for part in range(DC // 2):
                two = range(2 * part, 2 * part + 2)
                if part % 2 == 0:
                    await_freed(dve, U["conv2"] + part // 2)
                    await_freed(dve, U["conv0"] + part // 2)
                for k in two:
                    last = dve.tensor_scalar(conv_y[:, k, :], conv_z[:, k, 0:T], taps[:, 0, k:k + 1], None, ALU.mult)
                link(last)
                for n in (1, 2):
                    for k in two:
                        last = dve.scalar_tensor_tensor(conv_y[:, k, :], conv_z[:, k, n:n + T], taps[:, n, k:k + 1],
                                                        conv_y[:, k, :], ALU.mult, ALU.add)
                    link(last)
                y = conv_y[:, 2 * part:2 * part + 2, :]
                dve.tensor_tensor(y, y, conv_b[:, 2 * part:2 * part + 2, :], ALU.mult).then_inc(sem("conv_ready"), 1)
            finish(*add_to(xT, U["conv_out"], mod2[:, 1, 5, :, 0]), "x_ready")
            norm2(10, 1, 2)
            ffn(4, 1, 2)
            norm(11, xT[:, :, :], hT[:, :, :], vec("final2"), None, EPS2)


def shape_constants():
    q = np.arange(P)
    c = {}
    c["ident"] = np.eye(P, dtype=np.float32)
    c["ones"] = np.ones((P, P), np.float32)
    c["before"] = (q[:, None] < q[None, :]).astype(np.float32)
    c["iota"] = np.tile(np.arange(P, dtype=np.float32), (P, 1))
    col = np.arange(GRID_W)
    start = np.clip(col - KW // 2, 0, GRID_W - KW)
    ok = (col[None, :] >= start[:, None]) & (col[None, :] < start[:, None] + KW)
    c["col_mask"] = np.tile(np.where(ok, 0.0, NEG).astype(np.float32), (2, 1))
    valid = np.zeros((P, 2, 16), np.float32)
    for b in range(TB):
        t = b * P + q
        valid[:, b, :NCMP] = (np.arange(NCMP)[None, :] * 16 + 31) <= t[:, None]
    c["cmp_valid"] = valid.reshape(P, 32)
    c["cmp_bias"] = np.where(valid > 0, 0.0, NEG).astype(np.float32).reshape(P, 32)
    packed = np.concatenate([c[name] for name, _ in CONSTS], axis=1)
    dist = (q[:, None] + P - np.arange(T)[None, :]).astype(np.float32)
    slopes = 2.0 ** -np.arange(1, 9, dtype=np.float32)
    full = np.where(dist[:, None, :] >= 0, -slopes[None, :, None] * dist[:, None, :], NEG)
    near = np.where(dist[:, None, :] < 128, full, NEG)
    band = np.zeros((P, TB, 4, T), np.float32)
    t = np.arange(T)
    for g, w in enumerate((2, 4, 8, 16)):
        lo, hi = np.clip(t - w // 2, 0, T), np.clip(t - w // 2 + w, 0, T)
        m = ((t[:, None] >= lo[None, :]) & (t[:, None] < hi[None, :])) / (hi - lo)[None, :]
        m = (m - np.eye(T)).astype(np.float32)
        band[:, :, g, :] = m.reshape(TB, P, T).transpose(1, 0, 2)
    return packed, full, near, band


def kernel(**inputs):
    import ml_dtypes
    import concourse.bacc as bacc
    from concourse.bass_utils import run_bass_kernel_spmd

    a = {k: np.asarray(v) for k, v in inputs.items()}

    def cols(v):
        v = v.reshape(-1, P)
        return np.ascontiguousarray(v.T)

    def rows(v):
        return np.broadcast_to(v.reshape(1, -1), (P, v.size))

    def pairs_of_heads(w):
        h = w.reshape(w.shape[0], 2, 4, HD)
        return h.transpose(0, 2, 1, 3).reshape(w.shape[0], 512)

    def mixer_columns(w):
        at = np.cumsum([512, 128, 128, 512, 512, 512, 512, 128, 128, 128, 128, 128, 128, 24])
        qa, ka, va, qb, kb, vb, qc, kcm, vcm, ksl, vsl, kwn, vwn, gates, merge = np.split(w, at, axis=1)
        pad = np.zeros((w.shape[0], P - 24), w.dtype)
        return np.concatenate([pairs_of_heads(qa), pairs_of_heads(qc), qb, kb, ka, va, vb, kcm, vcm, ksl, vsl,
                               kwn, vwn, gates, pad, merge], axis=1)

    w2 = a["cmp_w2"][0].reshape(2, 2, P, HD)
    w2 = np.concatenate([w2, w2], axis=3).transpose(2, 0, 1, 3).reshape(P, 4 * P)
    vec = {
        "c": cols(a["c"]), "mod_b": cols(a["mod_b"]), "norm1": cols(a["norm1_g"]), "norm2": cols(a["norm2_g"]),
        "b_in": cols(mixer_columns(a["b_in"])), "final1": cols(a["final_g"]),
        "exp_b1": cols(a["exp_b1"]),
        "cmp_pos": cols(a["cmp_pos"]), "cmp_b1": cols(a["cmp_b1"]),
        "cmp_b2k": np.concatenate([a["cmp_b2"][0, 0]] * 2)[:, None], "cmp_b2v": rows(a["cmp_b2"][0, 1]),
        "cmp_w2": w2, "sinks": rows(a["sinks"]), "lambda": rows(a["diff_lambda"]), "subln": rows(a["diff_subln_g"]),
        "router_w": a["router_w"][0].reshape(DC, P, N_EXPERTS).transpose(1, 0, 2).reshape(P, -1),
        "router_b": rows(a["router_b"]),
        "cond2": np.stack([cols(a["c_2"]), cols(a["c_ctx_2"])], axis=2).reshape(P, -1),
        "mod_b2": cols(a["mod_b_2"]), "norm_g2": cols(a["norm_g_2"]),
        "pool_w": a["pool_w_2"][0].transpose(1, 0, 2).reshape(P, -1), "pool_scale": cols(a["pool_scale_2"]),
        "conv_w": cols(a["conv_w_2"]), "final2": cols(a["final_g_2"]),
    }
    packed, full, near, band = shape_constants()
    padded = np.zeros((8, 15, 2 * GRID_W), np.float32)
    padded[:, :, 48:79] = a["na_rpb_2"][0]
    first = GRID_W - 1 - np.arange(GRID_W)
    rpb = np.stack([padded[:, :, f:f + GRID_W] for f in first]).reshape(GRID_W, 8, 15 * GRID_W)
    arrays = {
        "vecs": np.concatenate([vec[name] for name, _ in VECS], axis=1), "consts": packed,
        "xT": np.ascontiguousarray(a["x"][0].T), "ctxT": np.ascontiguousarray(a["ctx_2"][0].T),
        "alibi_full": full.astype(ml_dtypes.bfloat16), "alibi_near": near.astype(ml_dtypes.bfloat16),
        "pool_band": band, "rpb": rpb,
        "mod_w": a["mod_w"], "w_in": mixer_columns(a["w_in"][0])[None], "cmp_w1": a["cmp_w1"][0],
        "w_branch": a["w_branch"][0], "exp_b2": a["exp_b2"].reshape(N_EXPERTS, D), "w_out": a["w_out"], "exp_w1": a["exp_w1"][0], "exp_w2": a["exp_w2"][0],
        "mod_w_2": a["mod_w_2"], "ffn_w13": a["ffn_w13_2"].reshape(4, D, 2 * FF),
        "ffn_w2": a["ffn_w2_2"].reshape(4, FF, D), "even_w_in": a["even_w_in_2"], "even_w_out": a["even_w_out_2"],
        "conv_w_in": a["conv_w_in_2"], "conv_w_out": a["conv_w_out_2"],
    }
    nc = bacc.Bacc("TRN2", target_bir_lowering=False, num_devices=1, dynamic_dma_scratch_size=1024)
    ins = {}
    for name, v in arrays.items():
        arrays[name] = v = np.ascontiguousarray(v)
        ins[name] = nc.dram_tensor(f"in_{name}", v.shape, mybir.dt.from_np(v.dtype), kind="ExternalInput").ap()
    out = nc.dram_tensor("out_y", (D, T), F32, kind="ExternalOutput").ap()
    build(nc, ins, out)
    r = run_bass_kernel_spmd(nc, [{f"in_{n}": v for n, v in arrays.items()}], core_ids=[0])
    return np.ascontiguousarray(r.results[0]["out_y"].T)[None]
```
